# Optimizing a Trainium2 kernel written in Bass

```python
import math
import jax, jax.numpy as jnp
from jax import lax
import numpy as np

D_MODEL = 1024
BATCH = 1
SEQ = 512
DEPTH = 1
DEC_BATCH = 8
DEC_SEQ = 1
PAST_LEN = 2048
PAGE_SIZE = 128

N_HEADS = 16
HEAD_DIM = 64
N_KV_HEADS = 4
GROUP = N_HEADS // N_KV_HEADS
WINDOW = 128
BLOCK = 128
ROPE_THETA = 500000.0
ROPE_DIM = HEAD_DIM // 4
Q_WIDTH = N_HEADS * HEAD_DIM
KV_WIDTH = N_KV_HEADS * HEAD_DIM
POOL_WINDOWS = (2, 4, 8, 16)
POOL_GROUPS = 4
POOL_WIDTH = D_MODEL // 2
POOL_GROUP_DIM = POOL_WIDTH // POOL_GROUPS
POOL_STATE = max(POOL_WINDOWS) - 1
N_MEM = 256
MEM_HEADS = 4
MEM_HEAD_DIM = 64
MEM_WIDTH = MEM_HEADS * MEM_HEAD_DIM
N_BRANCHES = 3
IN_SIZES = (Q_WIDTH, KV_WIDTH, KV_WIDTH, POOL_WIDTH, MEM_WIDTH, N_BRANCHES * D_MODEL)
IN_WIDTH = sum(IN_SIZES)
N_EXPERT_GROUPS = 4
EXPERTS_PER_GROUP = 4
N_EXPERTS = N_EXPERT_GROUPS * EXPERTS_PER_GROUP
TOP_K_INNER = 2
D_EXPERT = 512
ALPHA = (2.0 * DEPTH) ** 0.25
BETA = (8.0 * DEPTH) ** -0.25
LN_EPS = 1e-5

kernel_name = 'hybrid_swa_pool_memxattn_hmoe_step'

def _layer_norm(x, g, b):
    xf = x.astype(jnp.float32)
    mu = jnp.mean(xf, -1, keepdims=True)
    var = jnp.mean(jnp.square(xf - mu), -1, keepdims=True)
    return ((xf - mu) * lax.rsqrt(var + LN_EPS) * g + b).astype(x.dtype)

def _split_in(z):
    idx = [int(i) for i in np.cumsum(IN_SIZES)[:-1]]
    q, k, v, u, cq, gz = jnp.split(z, idx, axis=-1)
    lead = z.shape[:-1]
    return (q.reshape(*lead, N_HEADS, HEAD_DIM),
            k.reshape(*lead, N_KV_HEADS, HEAD_DIM),
            v.reshape(*lead, N_KV_HEADS, HEAD_DIM),
            u,
            cq.reshape(*lead, MEM_HEADS, MEM_HEAD_DIM),
            jax.nn.sigmoid(gz.astype(jnp.float32)).reshape(*lead, N_BRANCHES, D_MODEL))

def _partial_rope(x, pos):
    half = ROPE_DIM // 2
    inv = jnp.power(ROPE_THETA, -jnp.arange(half, dtype=jnp.float32) * (2.0 / ROPE_DIM))
    ang = pos.astype(jnp.float32)[:, None] * inv[None, :]
    cos = jnp.cos(ang)[:, None, :]
    sin = jnp.sin(ang)[:, None, :]
    xr = x[..., :ROPE_DIM].astype(jnp.float32)
    x1, x2 = xr[..., :half], xr[..., half:]
    rot = jnp.concatenate([x1 * cos - x2 * sin, x2 * cos + x1 * sin], axis=-1).astype(x.dtype)
    return jnp.concatenate([rot, x[..., ROPE_DIM:]], axis=-1)

def _gqa_sink_attend(q, k, v, mask, sinks):
    s = jnp.einsum('...qkgd,...skd->...kgqs', q, k, preferred_element_type=jnp.float32) * (HEAD_DIM ** -0.5)
    s = jnp.where(mask, s, -jnp.inf)
    sink = sinks.astype(jnp.float32).reshape(N_KV_HEADS, GROUP)[:, :, None, None]
    m = jnp.maximum(jnp.max(s, axis=-1, keepdims=True), sink)
    p = jnp.exp(s - m)
    p = p / (jnp.sum(p, axis=-1, keepdims=True) + jnp.exp(sink - m))
    return jnp.einsum('...kgqs,...skd->...qkgd', p.astype(v.dtype), v)

def _swa_prompt(q, k, v, sinks):
    B, L = q.shape[0], q.shape[1]
    nb = L // BLOCK
    qb = q.reshape(B, nb, BLOCK, N_KV_HEADS, GROUP, HEAD_DIM)
    kb = k.reshape(B, nb, BLOCK, N_KV_HEADS, HEAD_DIM)
    vb = v.reshape(B, nb, BLOCK, N_KV_HEADS, HEAD_DIM)
    padb = ((0, 0), (1, 0), (0, 0), (0, 0), (0, 0))
    kk = jnp.concatenate([jnp.pad(kb, padb)[:, :-1], kb], axis=2)
    vv = jnp.concatenate([jnp.pad(vb, padb)[:, :-1], vb], axis=2)
    blk = jnp.arange(nb)[:, None, None]
    qpos = blk * BLOCK + jnp.arange(BLOCK)[None, :, None]
    kpos = (blk - 1) * BLOCK + jnp.arange(2 * BLOCK)[None, None, :]
    mask = (kpos <= qpos) & (kpos >= qpos - WINDOW) & (kpos >= 0)
    o = _gqa_sink_attend(qb, kk, vv, mask[None, :, None, None], sinks)
    return o.reshape(B, L, Q_WIDTH)

def _swa_sample(q, k_new, v_new, ck, cv, sinks):
    DB, S = q.shape[0], q.shape[1]
    W = ck.shape[1]
    kk = jnp.concatenate([ck, k_new], axis=1)
    vv = jnp.concatenate([cv, v_new], axis=1)
    kpos = jnp.concatenate([PAST_LEN - W + jnp.arange(W), PAST_LEN + jnp.arange(S)])
    qpos = PAST_LEN + jnp.arange(S)
    mask = (kpos[None, :] <= qpos[:, None]) & (kpos[None, :] >= qpos[:, None] - WINDOW)
    o = _gqa_sink_attend(q.reshape(DB, S, N_KV_HEADS, GROUP, HEAD_DIM), kk, vv, mask, sinks)
    return o.reshape(DB, S, Q_WIDTH), kk, vv

def _multiscale_pool(u_ext, pos, w_mix, scale):
    P = POOL_STATE
    B, L = u_ext.shape[0], u_ext.shape[1] - P
    uf = u_ext.astype(jnp.float32)
    c = jnp.pad(jnp.cumsum(uf, axis=1), ((0, 0), (1, 0), (0, 0)))
    cur = uf[:, P:]
    top = c[:, P + 1:]
    outs = []
    for g, w in enumerate(POOL_WINDOWS):
        sl = slice(g * POOL_GROUP_DIM, (g + 1) * POOL_GROUP_DIM)
        wsum = top[..., sl] - c[:, P + 1 - w:P + 1 - w + L, sl]
        cnt = jnp.minimum(pos + 1, w).astype(jnp.float32)[None, :, None]
        outs.append(wsum / cnt - cur[..., sl])
    pooled = jnp.stack(outs, axis=2)
    mixed = jnp.einsum('blgc,gcd->blgd', pooled, w_mix.astype(jnp.float32))
    return (mixed.reshape(B, L, POOL_WIDTH) * scale).astype(u_ext.dtype)

def _cross_attend(cq, mk, mv):
    B, L = cq.shape[0], cq.shape[1]
    s = jnp.einsum('blhd,bmhd->bhlm', cq, mk, preferred_element_type=jnp.float32) * (MEM_HEAD_DIM ** -0.5)
    p = jax.nn.softmax(s, axis=-1)
    o = jnp.einsum('bhlm,bmhd->blhd', p.astype(mv.dtype), mv)
    return o.reshape(B, L, MEM_WIDTH)

def _hier_moe(h, w_group, b_group, w_router, b_router, w_gate, w_up, w_down):
    hf = h.astype(jnp.float32)
    g_prob = jax.nn.softmax(hf @ w_group.astype(jnp.float32) + b_group, axis=-1)
    g_top_p, g_top = lax.top_k(g_prob, 1)
    e_logits = jnp.einsum('td,dge->tge', hf, w_router.astype(jnp.float32)) + b_router
    e_logits = jnp.take_along_axis(e_logits, g_top[:, :, None], axis=1)[:, 0]
    e_top_v, e_top = lax.top_k(e_logits, TOP_K_INNER)
    wts = jax.nn.softmax(e_top_v, axis=-1) * g_top_p
    eid = g_top * EXPERTS_PER_GROUP + e_top
    combine = jnp.einsum('tk,tke->te', wts, jax.nn.one_hot(eid, N_EXPERTS, dtype=jnp.float32))
    y = jnp.zeros(h.shape, jnp.float32)
    for e in range(N_EXPERTS):
        hid = jax.nn.silu(h @ w_gate[e]) * (h @ w_up[e])
        y = y + combine[:, e:e + 1] * (hid @ w_down[e]).astype(jnp.float32)
    return y.astype(h.dtype)

def _merge_and_ffn(x, o_a, o_b, o_c, gates, wa, wb, wc, wo, g1, b1, g2, b2,
                   w_group, b_group, w_router, b_router, w_gate, w_up, w_down):
    m = (gates[..., 0, :] * (o_a @ wa).astype(jnp.float32)
         + gates[..., 1, :] * (o_b @ wb).astype(jnp.float32)
         + gates[..., 2, :] * (o_c @ wc).astype(jnp.float32)).astype(x.dtype)
    h = _layer_norm(ALPHA * x + m @ wo, g1, b1)
    f = _hier_moe(h.reshape(-1, D_MODEL), w_group, b_group, w_router, b_router,
                  w_gate, w_up, w_down).reshape(h.shape)
    return _layer_norm(ALPHA * h + f, g2, b2)

def setup_inputs(seed: int = 0) -> dict:
    key = jax.random.key(seed)
    ks = jax.random.split(key, 32)

    def nrm(k, shape, s):
        return jax.random.normal(k, shape, jnp.float32) * s

    w_c = min(WINDOW, PAST_LEN)
    return {
        'x_prompt': nrm(ks[0], (BATCH, SEQ, D_MODEL), 1.0),
        'x_sample': nrm(ks[1], (DEC_BATCH, DEC_SEQ, D_MODEL), 1.0),
        'cache_win_k': nrm(ks[2], (DEPTH, DEC_BATCH, w_c, N_KV_HEADS, HEAD_DIM), 1.0),
        'cache_win_v': nrm(ks[3], (DEPTH, DEC_BATCH, w_c, N_KV_HEADS, HEAD_DIM), 1.0),
        'state_pool': nrm(ks[4], (DEPTH, DEC_BATCH, POOL_STATE, POOL_WIDTH), 1.0),
        'cache_mem_k': nrm(ks[5], (DEPTH, DEC_BATCH, N_MEM, MEM_HEADS, MEM_HEAD_DIM), 1.0),
        'cache_mem_v': nrm(ks[6], (DEPTH, DEC_BATCH, N_MEM, MEM_HEADS, MEM_HEAD_DIM), 1.0),
        'mem_prompt': nrm(ks[7], (BATCH, N_MEM, D_MODEL), 1.0),
        'w_in': nrm(ks[8], (DEPTH, D_MODEL, IN_WIDTH), D_MODEL ** -0.5),
        'sinks': nrm(ks[9], (DEPTH, N_HEADS), 0.5),
        'w_pool_mix': nrm(ks[10], (DEPTH, POOL_GROUPS, POOL_GROUP_DIM, POOL_GROUP_DIM), POOL_GROUP_DIM ** -0.5),
        'pool_scale': 1.0 + nrm(ks[11], (DEPTH, POOL_WIDTH), 0.02),
        'w_mem_k': nrm(ks[12], (DEPTH, D_MODEL, MEM_WIDTH), D_MODEL ** -0.5),
        'w_mem_v': nrm(ks[13], (DEPTH, D_MODEL, MEM_WIDTH), D_MODEL ** -0.5),
        'w_branch_a': nrm(ks[14], (DEPTH, Q_WIDTH, D_MODEL), Q_WIDTH ** -0.5),
        'w_branch_b': nrm(ks[15], (DEPTH, POOL_WIDTH, D_MODEL), POOL_WIDTH ** -0.5),
        'w_branch_c': nrm(ks[16], (DEPTH, MEM_WIDTH, D_MODEL), MEM_WIDTH ** -0.5),
        'w_out': nrm(ks[17], (DEPTH, D_MODEL, D_MODEL), BETA * D_MODEL ** -0.5),
        'ln1_g': 1.0 + nrm(ks[18], (DEPTH, D_MODEL), 0.02),
        'ln1_b': nrm(ks[19], (DEPTH, D_MODEL), 0.02),
        'w_group': nrm(ks[20], (DEPTH, D_MODEL, N_EXPERT_GROUPS), D_MODEL ** -0.5),
        'b_group': nrm(ks[21], (DEPTH, N_EXPERT_GROUPS), 0.01),
        'w_router': nrm(ks[22], (DEPTH, D_MODEL, N_EXPERT_GROUPS, EXPERTS_PER_GROUP), D_MODEL ** -0.5),
        'b_router': nrm(ks[23], (DEPTH, N_EXPERT_GROUPS, EXPERTS_PER_GROUP), 0.01),
        'w_gate': nrm(ks[24], (DEPTH, N_EXPERTS, D_MODEL, D_EXPERT), D_MODEL ** -0.5),
        'w_up': nrm(ks[25], (DEPTH, N_EXPERTS, D_MODEL, D_EXPERT), D_MODEL ** -0.5),
        'w_down': nrm(ks[26], (DEPTH, N_EXPERTS, D_EXPERT, D_MODEL), BETA * D_EXPERT ** -0.5),
        'ln2_g': 1.0 + nrm(ks[27], (DEPTH, D_MODEL), 0.02),
        'ln2_b': nrm(ks[28], (DEPTH, D_MODEL), 0.02),
    }

def reference(x_prompt, x_sample, cache_win_k, cache_win_v, state_pool, cache_mem_k, cache_mem_v, mem_prompt,
              w_in, sinks, w_pool_mix, pool_scale, w_mem_k, w_mem_v, w_branch_a, w_branch_b, w_branch_c,
              w_out, ln1_g, ln1_b, w_group, b_group, w_router, b_router, w_gate, w_up, w_down, ln2_g, ln2_b):
    pos_p = jnp.arange(x_prompt.shape[1], dtype=jnp.int32)
    pos_s = PAST_LEN + jnp.arange(x_sample.shape[1], dtype=jnp.int32)
    keep_p = min(WINDOW, x_prompt.shape[1])
    keep_s = cache_win_k.shape[2]
    bp = x_prompt.shape[0]
    xp, xs = x_prompt, x_sample
    nk_p, nv_p, npool_p, nmk_p, nmv_p, nk_s, nv_s, npool_s = ([] for _ in range(8))
    for l in range(DEPTH):
        merge_w = (w_branch_a[l], w_branch_b[l], w_branch_c[l], w_out[l], ln1_g[l], ln1_b[l], ln2_g[l], ln2_b[l],
                   w_group[l], b_group[l], w_router[l], b_router[l], w_gate[l], w_up[l], w_down[l])
        q, k, v, u, cq, gates = _split_in(xp @ w_in[l])
        q = _partial_rope(q, pos_p)
        k = _partial_rope(k, pos_p)
        o_a = _swa_prompt(q, k, v, sinks[l])
        u_ext = jnp.pad(u, ((0, 0), (POOL_STATE, 0), (0, 0)))
        o_b = _multiscale_pool(u_ext, pos_p, w_pool_mix[l], pool_scale[l])
        mk = (mem_prompt @ w_mem_k[l]).reshape(bp, N_MEM, MEM_HEADS, MEM_HEAD_DIM)
        mv = (mem_prompt @ w_mem_v[l]).reshape(bp, N_MEM, MEM_HEADS, MEM_HEAD_DIM)
        o_c = _cross_attend(cq, mk, mv)
        nk_p.append(k[:, k.shape[1] - keep_p:])
        nv_p.append(v[:, v.shape[1] - keep_p:])
        npool_p.append(u_ext[:, u_ext.shape[1] - POOL_STATE:])
        nmk_p.append(mk)
        nmv_p.append(mv)
        xp = _merge_and_ffn(xp, o_a, o_b, o_c, gates, *merge_w)
        q, k, v, u, cq, gates = _split_in(xs @ w_in[l])
        q = _partial_rope(q, pos_s)
        k = _partial_rope(k, pos_s)
        o_a, kk, vv = _swa_sample(q, k, v, cache_win_k[l], cache_win_v[l], sinks[l])
        u_ext = jnp.concatenate([state_pool[l].astype(u.dtype), u], axis=1)
        o_b = _multiscale_pool(u_ext, pos_s, w_pool_mix[l], pool_scale[l])
        o_c = _cross_attend(cq, cache_mem_k[l], cache_mem_v[l])
        nk_s.append(kk[:, kk.shape[1] - keep_s:])
        nv_s.append(vv[:, vv.shape[1] - keep_s:])
        npool_s.append(u_ext[:, u_ext.shape[1] - POOL_STATE:])
        xs = _merge_and_ffn(xs, o_a, o_b, o_c, gates, *merge_w)
    return (xp, xs, jnp.stack(nk_p), jnp.stack(nv_p), jnp.stack(npool_p), jnp.stack(nmk_p), jnp.stack(nmv_p),
            jnp.stack(nk_s), jnp.stack(nv_s), jnp.stack(npool_s))


_drawn_inputs = setup_inputs


def setup_inputs(seed=0):
    import zlib

    import numpy as np

    out = dict(_drawn_inputs(seed))
    spreads = {}
    factors = {'sinks': 33.448,
     'pool_scale': 6.751,
     'b_group': 39.662,
     'b_router': 35.278,
     'ln2_g': 9.709,
     'ln2_b': 8.534,
     'cache_mem_k': 4.601,
     'cache_mem_v': 3.657,
     'w_branch_c': 2.779}
    for name, (base, spread) in spreads.items():
        noise = np.random.default_rng([zlib.crc32(name.encode()), seed]).standard_normal(out[name].shape)
        drawn = base * np.exp(spread * noise) if base else spread * noise
        out[name] = __import__('jax').numpy.asarray(drawn.astype(out[name].dtype))
    for name, factor in factors.items():
        out[name] = (out[name] * factor).astype(out[name].dtype)
    return out
```

```python
from contextlib import ExitStack

import concourse.bass as bass
from concourse import mybir

F32 = mybir.dt.float32
F32R = mybir.dt.float32r
I32 = mybir.dt.int32
ALU = mybir.AluOpType
ACT = mybir.ActivationFunctionType
AX = mybir.AxisListType

P = 128
D = 1024
KD = D // P
SEQ, NS = 512, 8
T = SEQ + NS
TH = T // 2
TT = 5
TR = T // TT
NB = SEQ // P
HD, NH, NKV, GRP = 64, 16, 4, 4
WIN = 128
NMEM, MH = 256, 4
POOL_W = (2, 4, 8, 16)
PST = 15
NG, EG = 4, 4
NE = NG * EG
DE = 512
CAP = P
NOVER = 8
NSLOT = (NE + NOVER) * CAP
ALPHA = 2.0 ** 0.25
EPS = 1e-5
SCALE = HD ** -0.5
NEG = -1.0e30
R_DD = 25

ZQ, ZU, ZK, ZC = 0, 8, 12, 14
ZT = 16
ZP = ZT * KD * P // 2048
MT = 3 * KD + 8 + 4 + 2
MPW = MT // 2 * P
PW = 2048

C_ID, C_ROT, C_COS, C_SIN, C_MASK = 0, 128, 256, 776, 1296
C_POOL, C_UP, C_ONE, C_I4, C_I16, C_B1, C_TOK, C_BM, C_I8, C_END = (
    1552, 1616, 1720, 1848, 1852, 1868, 1884, 1889, 1897, 1905)
Q_SINK, Q_SINKR, Q_PSC, Q_BIAS, Q_END = 0, 16, 17, 21, 41


def decoder_step(nc, a, o):
    ctx = ExitStack()
    with ctx:
        def sem(name):
            return ctx.enter_context(nc.semaphore(name))

        def at(name, offset, shape, dt=F32):
            return nc.alloc_sbuf_tensor_at(name, shape, dt, offset=offset)

        RING, X, Z, OAL = 16512, 74880, 109120, 142400
        OB, OC, ML, CON, PRM, VV, TAIL = 159040, 175680, 184000, 200640, 208320, 211200, 222464
        SL = MPW * 4
        raw = [at(f"raw{s}", RING + s * SL, [P, MPW]) for s in range(2)]
        whi = [at(f"whi{s}", RING + (2 + s) * SL, [P, MPW], F32R) for s in range(2)]
        wlo = [at(f"wlo{s}", RING + (4 + s) * SL, [P, MPW], F32R) for s in range(2)]
        XPAD = KD * T + P - NS
        xhi = at("xhi", X, [P, XPAD], F32R)
        xlo = at("xlo", X + 17120, [P, XPAD], F32R)
        z = at("z", Z, [P, ZT, T])
        oahi = at("oahi", Z, [P, 8, T], F32R)
        mhi = at("mhi", Z + 16640, [P, 8, T], F32R)
        oalo = at("oalo", OAL, [P, 8, T], F32R)
        obhi = at("obhi", OB, [P, 4, T], F32R)
        oblo = at("oblo", OB + 8320, [P, 4, T], F32R)
        ochi = at("ochi", OC, [P, 2, T], F32R)
        oclo = at("oclo", OC + 4160, [P, 2, T], F32R)
        mlo = at("mlo", ML, [P, 8, T], F32R)
        con = at("con", CON, [P, C_END])
        prm = at("prm", PRM, [P, Q_END])
        wmix = at("wmix", PRM + 192, [P, 4, P])
        wrt = at("wrt", PRM + 192 + 2048, [P, KD, 20])
        xtok = at("xtok", OAL, [P, NB, D])
        xsam = at("xsam", OAL + 16384, [NS, D])
        mtok = at("mtok", OAL + 20480, [P, 2, D])
        mthi = at("mthi", ML, [P, KD, NMEM], F32R)
        mtlo = at("mtlo", ML + 8192, [P, KD, NMEM], F32R)
        pooled = at("pooled", OAL, [P, 4, T])
        pbuf = [at(f"pbuf{s}", OAL + 8320 + s * 2080, [P, T]) for s in range(2)]
        pstate = at("pstate", OAL + 12480, [NS * PST, 512])
        pext = at("pext", OAL + 14528, [P, 4, NS, PST + 1])
        rtmp = [at(f"rtmp{s}", ML + s * 2080, [P, T]) for s in range(2)]
        v = at("v", VV, [P, NB + 1, NKV * HD])
        mkv = at("mkv", VV + 5120, [P, 2, 512])
        mkt = at("mkt", VV + 9216, [P, 2, NMEM])
        probs = [at(f"probs{s}", ML + s * 4096, [P, GRP, 2 * P]) for s in range(2)]
        pt = [at(f"pt{s}", ML + 8192 + s * 4096, [P, 2, GRP * P]) for s in range(2)]
        stat = at("stat", TAIL + 512, [P, 2, 8, 4])
        nsink = at("nsink", TAIL + 768, [P, 17])
        kvrow = at("kvrow", TAIL + 1024, [P, 512])
        cach_k = at("cach_k", ML, [P, NS, 256])
        cach_v = at("cach_v", ML + 8192, [P, NS, 256])
        kt = [at(f"kt{s}", VV + 5120 + s * 2048, [P, 512]) for s in range(2)]
        srow = at("srow", TAIL + 3072, [P, 264])
        scol = at("scol", TAIL + 4160, [P, P])
        pcol = at("pcol", TAIL + 4672, [P, P])
        pnew = at("pnew", TAIL + 5184, [P, P])
        sstat = at("sstat", TAIL + 5696, [P, 16])
        qsam = at("qsam", TAIL + 5760, [P, 64])
        urow = at("urow", TAIL + 3072, [P, 512])
        gate = [at(f"gate{s}", VV + s * 2080, [P, T]) for s in range(3)]
        zrow = at("zrow", VV, [P, D])
        mval = at("mval", VV + 6240, [P, T])
        wohi = at("wohi", X, [P, KD, D], F32R)
        wolo = at("wolo", OAL, [P, KD, D], F32R)
        hall = at("hall", RING + 2 * SL, [TR, TT, D])
        xrow = [at(f"xrow{s}", RING + 2 * SL + 20480 + s * 4096, [TR, D]) for s in range(2)]
        ht = at("ht", RING + 2 * SL + 28672, [P, KD, TR])
        lng = at("lng", VV, [P, D])
        lnb = at("lnb", VV + 4096, [P, D])
        lstat = at("lstat", VV + 8192, [P, 32])
        R0 = ML
        K0 = VV + 8448

        def rt(name, k, shape, dt=F32):
            return at(name, R0 + k * 320, shape, dt)
        lg = at("lg", R0, [TR, TT, 20])
        gm, gd, gs = rt("gm", 2, [TR, TT]), rt("gd", 3, [TR, TT, 4]), rt("gs", 4, [TR, TT])
        gi, gk = rt("gi", 5, [TR, TT]), rt("gk", 6, [TR, TT, 4])
        em, cd = rt("em", 7, [TR, TT, NE]), rt("cd", 8, [TR, TT, NE])
        one1, one2 = rt("one1", 9, [TR, TT, NE]), rt("one2", 10, [TR, TT, NE])
        both = rt("both", 11, [TR, TT, NE])
        m1, m2, i1, i2 = (rt(n, 12 + k, [TR, TT]) for k, n in enumerate(("m1", "m2", "i1", "i2")))
        w1, w2 = at("w1", K0, [TR, TT]), at("w2", K0 + 32, [TR, TT])
        slotf, sltmp = rt("slotf", 18, [TR, TT, NE]), rt("sltmp", 19, [TR, TT, NE])
        s1f, s2f = rt("s1f", 20, [TR, TT]), rt("s2f", 21, [TR, TT])
        s1, s2 = at("s1", K0 + 64, [TR, TT], I32), at("s2", K0 + 96, [TR, TT], I32)
        cnt, oc = rt("cnt", 24, [P, NE]), rt("oc", 25, [P, NE])
        inc = [rt(f"inc{k}", 26 + k, [P, NE]) for k in range(2)]
        base2, ovf = rt("base2", 28, [P, NE]), rt("ovf", 29, [P, 8, NE])
        ovi = at("ovi", R0 + 32 * 320, [P, 8])
        ove = at("ove", K0 + 128, [P, 16], I32)
        slots = at("slots", K0 + 192, [P, NE + NOVER], I32)
        slrow = at("slrow", R0 + 33 * 320, [NE + NOVER, P])
        zslot = at("zslot", TAIL, [NE + NOVER, P])
        MR = 8192
        eraw = [at(f"eraw{s}", X + s * MR, [P, PW]) for s in range(6)]
        ehi = [at(f"ehi{s}", X + (6 + s) * MR, [P, PW], F32R) for s in range(3)]
        elo = [at(f"elo{s}", X + (9 + s) * MR, [P, PW], F32R) for s in range(3)]
        E0 = X + 12 * MR
        xe = at("xe", E0, [P, D])
        xethi = at("xethi", E0 + 4096, [P, KD, P], F32R)
        xetlo = at("xetlo", E0 + 8192, [P, KD, P], F32R)
        sig = at("sig", E0 + 12288, [P, DE])
        act = at("act", E0 + 14336, [P, DE])
        hid = at("hid", E0 + 16384, [P, DE])
        hthi = at("hthi", E0 + 18432, [P, 4, P], F32R)
        htlo = at("htlo", E0 + 20480, [P, 4, P], F32R)
        yout = at("yout", E0 + 22528, [P, D])
        slotc = at("slotc", E0 + 26624, [P, 1], I32)
        ya = [at(f"ya{s}", X + s * 8192, [TR, D]) for s in range(2)]
        yb = [at(f"yb{s}", X + s * 8192 + 4096, [TR, D]) for s in range(2)]
        res = [at(f"res{s}", X + 16384 + s * 4096, [TR, D]) for s in range(2)]

        ps = ctx.enter_context(nc.psum_tensor("ps", [P, 8, 512], F32))
        h_dram = nc.dram_tensor("h_dram", (T, D), F32, kind="Internal").ap()
        slot_dram = nc.dram_tensor("slot_dram", (NSLOT, 1), F32, kind="Internal").ap()
        y_dram = nc.dram_tensor("y_dram", (NSLOT, D), F32, kind="Internal").ap()

        ident = con[:, C_ID:C_ID + P]
        upper = con[0:TR, C_UP:C_UP + TR]
        ones = con[0:TR, C_ONE:C_ONE + P]

        id_in, con_in, x_in, m_in = sem("id_in"), sem("con_in"), sem("x_in"), sem("m_in")
        st_in, win_in, winv_in, cm_in, cmv_in = (sem(n) for n in ("st_in", "win_in", "winv_in", "cm_in", "cmv_in"))
        raw_in = [sem(f"raw_in{s}") for s in range(2)]
        hi_split, lo_split, piece_used = sem("hi_split"), sem("lo_split"), sem("piece_used")
        pad_zero = sem("pad_zero")
        xt_ps, xt_hi, xt_lo = sem("xt_ps"), sem("xt_hi"), sem("xt_lo")
        z_even, z_out = sem("z_even"), sem("z_out")
        v_out, mkv_out, mkt_ps, mkt_out = sem("v_out"), sem("mkv_out"), sem("mkt_ps"), sem("mkt_out")
        rot_ps, rot_mul, rot_cos, roped = sem("rot_ps"), sem("rot_mul"), sem("rot_cos"), sem("roped")
        row_ps, row_out, rows_sent = sem("row_ps"), sem("row_out"), sem("rows_sent")
        st_ps, st_out, pool_step, pooled_in = sem("st_ps"), sem("st_out"), sem("pool_step"), sem("pooled_in")
        mix_ps, mix_hi, mix_lo = sem("mix_ps"), sem("mix_hi"), sem("mix_lo")
        prep = sem("prep")
        sc_ps, sc_row, sc_max, sc_neg, sc_snk, sc_exp, sc_den, sc_rec, sc_nrm = (sem(n) for n in (
            "sc_ps", "sc_row", "sc_max", "sc_neg", "sc_snk", "sc_exp", "sc_den", "sc_rec", "sc_nrm"))
        pt_ps, pt_act, pt_dve, o_ps, o_hi, o_lo = (sem(n) for n in (
            "pt_ps", "pt_act", "pt_dve", "o_ps", "o_hi", "o_lo"))
        qsam_ok = sem("qsam_ok")
        sa_ps, sa_act, sa_dve = sem("sa_ps"), sem("sa_act"), sem("sa_dve")
        prod_ps, gate_out, m_step, m_val, m_hi, m_lo = (sem(n) for n in (
            "prod_ps", "gate_out", "m_step", "m_val", "m_hi", "m_lo"))
        ln_in, xrow_in = sem("ln_in"), [sem(f"xrow_in{s}") for s in range(2)]
        h_ps, h_sum, h_stat, h_nrm, h_done, h_sent = (sem(n) for n in (
            "h_ps", "h_sum", "h_stat", "h_nrm", "h_done", "h_sent"))
        sq_in, sq_out = sem("sq_in"), sem("sq_out")
        ht_ps, ht_out, lg_ps, lg_out = sem("ht_ps"), sem("ht_out"), sem("lg_ps"), sem("lg_out")
        rd, r_exp, both_ok, rank_ps, slots_ok, z_slot, z_sent = (sem(n) for n in (
            "rd", "r_exp", "both_ok", "rank_ps", "slots_ok", "z_slot", "z_sent"))
        slot_sent, slot_in, slot_ps, slot_ok = sem("slot_sent"), sem("slot_in"), sem("slot_ps"), sem("slot_ok")
        eraw_in = [sem(f"eraw_in{s}") for s in range(6)]
        ehi_ok, elo_ok, e_used = sem("ehi_ok"), sem("elo_ok"), sem("e_used")
        slc_seen = sem("slc_seen")
        slc_ok, xe_in, xet_ps, xet_hi, xet_lo = (sem(n) for n in ("slc_ok", "xe_in", "xet_ps", "xet_hi", "xet_lo"))
        g_ps, sig_ok, act_ok, hid_ok, hidt_ps, hidt_hi, hidt_lo = (sem(n) for n in (
            "g_ps", "sig_ok", "act_ok", "hid_ok", "hidt_ps", "hidt_hi", "hidt_lo"))
        y_out, y_sent, moe_done = sem("y_out"), sem("y_sent"), sem("moe_done")
        ln2_in, ya_in = sem("ln2_in"), [sem(f"ya_in{s}") for s in range(2)]
        f_step, f_sum, f_stat, f_nrm, f_done = (sem(n) for n in ("f_step", "f_sum", "f_stat", "f_nrm", "f_done"))
        f_sent = [sem(f"f_sent{s}") for s in range(2)]
        copied = sem("copied")

        groups = [("swa", b, h) for b in range(NB) for h in range(NKV)] + [("mem", b, 0) for b in range(NB)]
        NGR = len(groups)
        MEM_ORDER = (0, 2, 1, 3)
        N_V, N_M, N_G = ZP, ZP + 1, ZP + 3
        N_O = N_G + 2 * KD

        def both_dims(src, n):
            return src.rearrange("p (a n) -> p a n", a=1).broadcast_to([TR, TT, n])

        def halves(ap):
            return ap.rearrange("p (h c) -> p h c", h=2)

        def pair(s, rows=slice(0, P)):
            return ps[rows, 2 * s:2 * s + 2, 0:TH]

        block = ctx.enter_context(nc.Block())

        @block.sync
        def _(sp):
            sp.dma_start(con[:, 0:P], a["consts"][:, 0:P]).then_inc(id_in, 16)
            xp = a["x_prompt"].rearrange("(t p) d -> p t d", p=P)
            for t in range(NB):
                sp.dma_start(xtok[:, t, :], xp[:, t, :]).then_inc(x_in, 16)
            sp.dma_start(xsam[:, :], a["x_sample"]).then_inc(x_in, 16)

            def piece(n, src, width, first=False):
                if not first:
                    sp.wait_ge(hi_split, n - 1)
                    sp.wait_ge(lo_split, n - 1)
                sp.dma_start(raw[n % 2][:, 0:width], src).then_inc(raw_in[n % 2], 16)

            for n in range(2):
                piece(n, a["wz"][n], PW, True)
            sp.dma_start(mtok[:, :, :], a["mem_prompt"].rearrange("(t p) d -> p t d", p=P)).then_inc(m_in, 16)
            sp.dma_start(con[:, P:C_END], a["consts"][:, P:C_END]).then_inc(con_in, 16)
            sp.dma_start(prm[:, :], a["params"]).then_inc(con_in, 16)
            sp.dma_start(wmix[:, :, :], a["w_pool_mix"].rearrange("g c d -> c g d")).then_inc(con_in, 16)
            sp.dma_start(wrt[:, :, :], a["w_route"]).then_inc(con_in, 16)
            with sp.Fori(1, ZP // 2) as i:
                for j in range(2):
                    sp.wait_ge(hi_split, 2 * i + j - 1)
                    sp.wait_ge(lo_split, 2 * i + j - 1)
                    sp.dma_start(raw[j][:, 0:PW], a["wz"][bass.ds(2 * i + j, 1)].rearrange("a p n -> (a p) n"))\
                      .then_inc(raw_in[j], 16)
            sp.wait_ge(xt_lo, KD + 1)
            sp.wait_ge(xt_hi, KD + 1)
            sp.dma_start(pstate[:, :], a["state_pool"].rearrange("b r c -> (b r) c")).then_inc(st_in, 16)
            piece(N_V, a["wv"], PW)
            for j in range(2):
                piece(N_M + j, a["wmem"][j], PW)
            for j in range(2):
                piece(N_G + j, a["wm"][j], MPW)
            sp.wait_ge(v_out, 3)
            sp.dma_start(o["new_v_prompt"], v[:, NB - 1, :]).then_inc(copied, 16)
            sp.dma_start(o["new_v_sample"][:, WIN - 1, :], v[0:NS, NB, :]).then_inc(copied, 16)
            sp.wait_ge(mkv_out, 2)
            sp.dma_start(o["new_mem_k"].rearrange("(t p) d -> p t d", p=P), mkv[:, :, 0:256]).then_inc(copied, 16)
            sp.dma_start(o["new_mem_v"].rearrange("(t p) d -> p t d", p=P), mkv[:, :, 256:512]).then_inc(copied, 16)
            sp.dma_start(o["new_k_sample"][:, 0:WIN - 1, :], a["cache_win_k"][:, 1:WIN, :]).then_inc(copied, 16)
            sp.dma_start(o["new_v_sample"][:, 0:WIN - 1, :], a["cache_win_v"][:, 1:WIN, :]).then_inc(copied, 16)
            sp.dma_start(o["new_pool_sample"][:, 0:PST - 1, :], a["state_pool"][:, 1:PST, :]).then_inc(copied, 16)
            sp.wait_ge(row_out, 1)
            sp.dma_start(o["new_k_prompt"], kvrow[:, 0:256]).then_inc(rows_sent, 16)
            sp.wait_ge(row_out, 2)
            sp.dma_start(o["new_k_sample"][:, WIN - 1, :], kvrow[0:NS, 256:512]).then_inc(rows_sent, 16)
            sp.wait_ge(row_out, 3)
            sp.dma_start(o["new_pool_prompt"], urow[0:PST, :]).then_inc(rows_sent, 16)
            sp.dma_start(o["new_pool_sample"][:, PST - 1, :], urow[PST:PST + NS, :]).then_inc(rows_sent, 16)
            sp.wait_ge(o_lo, NGR)
            sp.wait_ge(o_hi, NGR)
            sp.dma_start(cach_k[:, :, :], a["cache_win_k"].rearrange("b k d -> k b d")).then_inc(win_in, 16)
            sp.dma_start(cach_v[:, :, :], a["cache_win_v"].rearrange("b k d -> k b d")).then_inc(winv_in, 16)
            ck = a["cache_mem_k"].rearrange("b (t p) d -> p b t d", p=P)
            cv = a["cache_mem_v"].rearrange("b (t p) d -> p b t d", p=P)

            def half_cache(dst, src, q, arrived):
                for t in range(2):
                    sp.dma_start(dst[:, :, :].rearrange("p (b t) d -> p b t d", t=2)[:, :, t, :],
                                 src[:, 4 * q:4 * q + 4, t, :]).then_inc(arrived, 16)

            sp.wait_ge(sa_ps, 7)
            half_cache(cach_k, ck, 0, cm_in)
            sp.wait_ge(sa_ps, 12)
            half_cache(cach_v, cv, 0, cmv_in)
            sp.wait_ge(sa_ps, 19)
            half_cache(cach_k, ck, 1, cm_in)
            sp.wait_ge(sa_ps, 31)
            half_cache(cach_v, cv, 1, cmv_in)
            with sp.Fori(1, KD) as i:
                for j in range(2):
                    s = (N_G + j) % 2
                    sp.wait_ge(hi_split, 2 * i + N_G + j - 1)
                    sp.wait_ge(lo_split, 2 * i + N_G + j - 1)
                    sp.dma_start(raw[s][:, :], a["wm"][bass.ds(2 * i + j, 1)].rearrange("a p n -> (a p) n"))\
                      .then_inc(raw_in[s], 16)
            for j in range(4):
                piece(N_O + j, a["wo"][j], PW)
            sp.wait_ge(m_hi, KD)
            sp.wait_ge(m_lo, KD)
            sp.dma_start(lng[:, :], a["ln1_g"].broadcast_to([P, D])).then_inc(ln_in, 16)
            sp.dma_start(lnb[:, :], a["ln1_b"].broadcast_to([P, D])).then_inc(ln_in, 16)
            for t in range(TT):
                if t >= 2:
                    sp.wait_ge(h_sum, t - 1)
                n = min(TR, SEQ - t * TR)
                sp.dma_start(xrow[t % 2][0:n, :], a["x_prompt"][t * TR:t * TR + n, :]).then_inc(xrow_in[t % 2], 16)
                if n < TR:
                    sp.dma_start(xrow[t % 2][n:TR, :], a["x_sample"]).then_inc(xrow_in[t % 2], 16)

            def expert_piece(n, s, src, first=False):
                if not first:
                    sp.wait_ge(ehi_ok, n - 5)
                    sp.wait_ge(elo_ok, n - 5)
                sp.dma_start(eraw[s][:, :], src).then_inc(eraw_in[s], 16)

            wg = a["w_gate"].rearrange("e (p h k) n -> e h p (k n)", h=2, k=4)
            wu = a["w_up"].rearrange("e (p h k) n -> e h p (k n)", h=2, k=4)
            wd = a["w_down"].rearrange("e (p h k) n -> e h p (k n)", h=2, k=2)

            def of(w, e, h):
                return w[bass.ds(e, 1), h].rearrange("a p n -> (a p) n")

            sp.wait_ge(h_ps, TT)
            for n in range(4):
                expert_piece(n, n, (wg if n < 2 else wu)[0, n % 2], True)
            for n in range(2):
                expert_piece(4 + n, 4 + n, wg[1, n], True)
            for n in range(2):
                expert_piece(6 + n, n, wu[1, n])
            for n in range(2):
                expert_piece(8 + n, 2 + n, wd[0, n])
            with sp.Fori(2, NE) as e:
                for k, w in enumerate((wg, wg, wu, wu)):
                    expert_piece(6 * e - 2 + k, (4 + k) % 6, of(w, e, k % 2))
                for k in range(2):
                    expert_piece(6 * e + 2 + k, 2 + k, of(wd, e - 1, k))
            for k in range(2):
                expert_piece(6 * NE - 2 + k, 4 + k, wd[NE - 1, k])
            sp.wait_ge(h_done, TT)
            sp.dma_start(lng[:, :], a["ln2_g"].broadcast_to([P, D])).then_inc(ln2_in, 16)
            sp.dma_start(lnb[:, :], a["ln2_b"].broadcast_to([P, D])).then_inc(ln2_in, 16)
            sp.wait_ge(slots_ok, 1)
            n_over = sp.value_load(ove[0:1, 8:9], min_val=0, max_val=NOVER)
            with sp.Fori(0, NOVER) as j:
                e = sp.value_load(ove[0:1, bass.ts(j, 1)], min_val=0, max_val=NE - 1)
                with sp.If(j < n_over):
                    for k, w in enumerate((wg, wg, wu, wu, wd, wd)):
                        expert_piece(6 * NE + 6 * j + k, k, of(w, e, k % 2))
            for t in range(TT):
                sp.wait_ge(f_done, t + 1)
                n = min(TR, SEQ - t * TR)
                sp.dma_start(o["y_prompt"][t * TR:t * TR + n, :], res[t % 2][0:n, :]).then_inc(f_sent[t % 2], 16)
                if n < TR:
                    sp.dma_start(o["y_sample"], res[t % 2][n:TR, :]).then_inc(f_sent[t % 2], 16)
            sp.wait_ge(f_sent[0], 16 * 4)
            sp.wait_ge(f_sent[1], 16 * 2)
            sp.wait_ge(copied, 16 * 7)
            sp.wait_ge(rows_sent, 16 * 4)

        @block.scalar
        def _(ac):
            for k in range(KD):
                ac.wait_ge(xt_ps, k + 1)
                ac.activation(xhi[:, k * T:k * T + SEQ], ps[:, 4 + k % 2, :], ACT.Copy).then_inc(xt_hi, 1)
            ac.wait_ge(xt_ps, KD + 1)
            ac.activation(xhi[:, 0:KD * T].rearrange("p (k t) -> p k t", k=KD)[:, :, SEQ:T],
                          ps[:, 6, 0:KD * NS].rearrange("p (k t) -> p k t", k=KD), ACT.Copy).then_inc(xt_hi, 1)

            def split(n, s, width, arrived, first=False, out=None):
                ac.wait_ge(raw_in[s], arrived)
                if not first:
                    ac.wait_ge(piece_used, n - 1)
                ac.activation(whi[s][:, 0:width] if out is None else out, raw[s][:, 0:width], ACT.Copy)\
                  .then_inc(hi_split, 1)

            def z_tile(t, s):
                ac.activation(z[:, bass.ds(t, 1), :].rearrange("p a (h c) -> p (a h) c", h=2), pair(s),
                              ACT.Copy).then_inc(z_out, 1)

            split(0, 0, PW, 16, True)
            split(1, 1, PW, 16, True)
            with ac.Fori(0, ZP // 2) as i:
                for j in range(2):
                    ac.wait_ge(z_even, 2 * i + j + 1)
                    z_tile(4 * i + 2 * j, 0)
                    ac.wait_ge(piece_used, 2 * i + j + 1)
                    z_tile(4 * i + 2 * j + 1, 1)
                    split(2 * i + j + 2, j, PW, 16 * i + 32)
            for k in range(4):
                ac.wait_ge(xt_ps, KD + 2 + k)
                ac.activation(mthi[:, 2 * k:2 * k + 2, :], ps[:, 4 + k % 2, :].rearrange("p (k m) -> p k m", k=2),
                              ACT.Copy).then_inc(xt_hi, 1)
            ac.wait_ge(st_ps, 1)
            ac.activation(pext[:, :, :, :].rearrange("p g b r -> p (g b) r")[:, :, 0:PST],
                          ps[:, 7, 0:4 * NS * PST].rearrange("p (g r) -> p g r", r=PST), ACT.Copy).then_inc(st_out, 1)
            ac.wait_ge(piece_used, N_V + 1)
            ac.wait_ge(z_sent, 16 * (NOVER + 1))
            for k in range(2):
                ac.activation(v[:, 2 * k:2 * k + 2, :], ps[:, 4 + k, :].rearrange("p (b d) -> p b d", b=2),
                              ACT.Copy).then_inc(v_out, 1)
            ac.activation(v[0:NS, NB, :], ps[0:NS, 6, 0:256], ACT.Copy).then_inc(v_out, 1)
            split(N_M + 1, 0, PW, 16 * ((N_M + 1) // 2 + 1))
            ac.wait_ge(piece_used, N_M + 2)
            for m in range(2):
                ac.activation(mkv[:, m, :], ps[:, (7, 0)[m], :], ACT.Copy).then_inc(mkv_out, 1)
            for j in range(2):
                split(N_G + j, (N_G + j) % 2, MPW, 16 * ((N_G + j) // 2 + 1))
            ac.wait_ge(mkt_ps, 1)
            ac.activation(mkt[:, :, :], ps[:, 1, :].rearrange("p (t m) -> p t m", t=2), ACT.Copy).then_inc(mkt_out, 1)
            ac.wait_ge(row_ps, 2)
            ac.activation(kvrow[:, 0:256], ps[:, 6, 0:256], ACT.Copy).then_inc(row_out, 1)
            ac.activation(kvrow[0:NS, 256:512], ps[0:NS, 6, 256:512], ACT.Copy).then_inc(row_out, 1)
            ac.wait_ge(row_ps, 3)
            ac.activation(urow[0:PST + NS, :], ps[0:PST + NS, 7, :], ACT.Copy).then_inc(row_out, 1)
            ac.wait_ge(con_in, 64)
            for g in range(4):
                ac.wait_ge(mix_ps, g + 1)
                ac.activation(halves(obhi[:, g, :]), pair(1 + g % 2), ACT.Copy if g > 9 else ACT.Identity,
                              scale=prm[:, Q_PSC + g:Q_PSC + g + 1]).then_inc(mix_hi, 1)

            def exps(g):
                kind, b, h = groups[g]
                s, w = g % 2, P if kind == "swa" and b == 0 else 2 * P
                ac.wait_ge(sc_neg, g + 1)
                if kind == "mem":
                    ac.wait_ge(pt_ps, g - 1)
                for j in range(GRP):
                    src = probs[s][:, j, 0:w] if kind == "swa" else ps[:, 2 * s + j // 2, (j % 2) * 256:(j % 2) * 256 + w]
                    last = ac.activation(probs[s][:, j, 0:w], src, ACT.Exp, bias=stat[:, s, 1, j:j + 1],
                                         scale=1.0 if kind == "swa" else SCALE, accum_out=stat[:, s, 3, j:j + 1])
                if kind == "swa":
                    ac.wait_ge(sc_snk, g + 1)
                    last = ac.activation(stat[:, s, 4, :], stat[:, s, 2, :], ACT.Exp)
                last.then_inc(sc_exp, 1)

            exps(0)
            for g, (kind, b, h) in enumerate(groups):
                s = g % 2
                if g + 1 < NGR:
                    exps(g + 1)
                ac.wait_ge(pt_ps, g + 1)
                if g >= 2:
                    ac.wait_ge(o_ps, g - 1)
                n = 256 if kind == "swa" and b == 0 else 512
                ac.activation(pt[s][:, 0, 0:n], ps[:, 4, 0:n], ACT.Copy).then_inc(pt_act, 1)
                ac.wait_ge(o_ps, g + 1)
                if kind == "swa":
                    r, p = 64 * (h % 2), h // 2
                    ac.activation(oahi[r:r + 64, 4 * p:4 * p + 4, b * P:b * P + P],
                                  ps[r:r + 64, 6 + s, :].rearrange("p (j q) -> p j q", j=4), ACT.Copy).then_inc(o_hi, 1)
                else:
                    ac.activation(ochi[:, :, b * P:b * P + P],
                                  ps[:, 6 + s, 0:256].rearrange("p (t q) -> p t q", t=2), ACT.Copy).then_inc(o_hi, 1)

            for q in range(4):
                ac.wait_ge(sa_ps, 2 * q + 1)
                ac.activation(kt[q % 2][:, :], ps[:, 4 + q % 2, :], ACT.Copy).then_inc(sa_act, 1)
            ac.wait_ge(rows_sent, 64)
            ac.wait_ge(sa_ps, 8)
            for r in range(2):
                last = ac.activation(scol[:, :].rearrange("p (a r c) -> p a r c", a=2, r=2)[:, :, r, :],
                                     ps[:, r, 0:P].rearrange("p (a r c) -> p a r c", a=2, r=2)[:, :, r, :], ACT.Copy)
            last.then_inc(sa_act, 1)
            ac.wait_ge(sa_dve, 7)
            ac.activation(srow[:, 0:WIN + 1], srow[:, 0:WIN + 1], ACT.Exp, bias=sstat[:, 1:2],
                          accum_out=sstat[:, 3:4])
            ac.activation(sstat[:, 4:5], sstat[:, 2:3], ACT.Exp).then_inc(sa_act, 1)
            ac.wait_ge(sa_ps, 11)
            ac.activation(pcol[:, :], ps[:, 3, 0:P], ACT.Copy)
            ac.activation(pnew[0:NS, :], ps[0:NS, 3, P:2 * P], ACT.Copy).then_inc(sa_act, 1)
            ac.wait_ge(sa_ps, 12)
            for p in range(2):
                last = ac.activation(oahi[:, 4 * p:4 * p + 4, SEQ:T],
                                     ps[:, 6, 32 * p:32 * p + 32].rearrange("p (b j) -> p j b", j=4), ACT.Copy)
            last.then_inc(sa_act, 1)
            for b in range(NS):
                ac.wait_ge(sa_ps, 13 + 2 * b)
                ac.activation(kt[b % 2][:, :], ps[:, 4 + b % 2, :], ACT.Copy).then_inc(sa_act, 1)
            ac.wait_ge(sa_ps, 28)
            for r in range(2):
                last = ac.activation(scol[:, 0:64].rearrange("p (a r c) -> p a r c", a=4, r=2)[:, :, r, :],
                                     ps[:, (7, 0)[r], 0:64].rearrange("p (a r c) -> p a r c", a=4, r=2)[:, :, r, :],
                                     ACT.Copy)
            last.then_inc(sa_act, 1)
            ac.wait_ge(sa_dve, 14)
            ac.activation(srow[0:32, 0:NMEM], ps[0:32, 2, 0:NMEM], ACT.Exp, bias=sstat[0:32, 1:2], scale=SCALE,
                          accum_out=sstat[0:32, 3:4]).then_inc(sa_act, 1)
            ac.wait_ge(sa_ps, 30)
            ac.activation(pcol[:, 0:64], ps[:, 3, 0:64], ACT.Copy).then_inc(sa_act, 1)
            ac.wait_ge(sa_ps, 32)
            ac.activation(ochi[:, :, SEQ:T], ps[:, 6, 64:80].rearrange("p (t b) -> p t b", t=2), ACT.Copy)\
              .then_inc(sa_act, 1)

            def merge(i, more):
                for s in range(3):
                    ac.wait_ge(prod_ps, 5 * i + s + 1)
                    ac.activation(halves(gate[s][:, :]), pair(s), ACT.Sigmoid).then_inc(gate_out, 1)
                    if s == 1 and more:
                        split(2 * i + N_G + 2, N_G % 2, MPW, 16 * i + 16 * ((N_G + 2) // 2 + 1))
                if more:
                    split(2 * i + N_G + 3, (N_G + 1) % 2, MPW, 16 * i + 16 * ((N_G + 3) // 2 + 1))
                ac.wait_ge(m_val, i + 1)
                ac.activation(mhi[:, bass.ds(i, 1), :].rearrange("p a c -> p (a c)"), mval[:, :], ACT.Copy)\
                  .then_inc(m_hi, 1)

            with ac.Fori(0, KD - 1) as i:
                merge(i, True)
            merge(KD - 1, False)
            ac.wait_ge(piece_used, N_O)
            for j in range(4):
                n = N_O + j
                split(n, n % 2, PW, 16 * (n // 2 + 1), True,
                      out=wohi[:, 2 * j:2 * j + 2, :].rearrange("p k n -> p (k n)"))
            for t in range(TT):
                ac.wait_ge(h_stat, 10 * t + 4)
                ac.activation(lstat[0:TR, 15:16], lstat[0:TR, 14:15], ACT.Sqrt).then_inc(sq_out, 1)
                ac.wait_ge(h_stat, 10 * t + 9)
                ac.activation(hall[:, t, :], hall[:, t, :], ACT.Identity, bias=lstat[0:TR, 20:21],
                              scale=lstat[0:TR, 18:19]).then_inc(h_nrm, 1)
                ac.wait_ge(ht_ps, t + 1)
                if t:
                    ac.wait_ge(lg_ps, t)
                ac.activation(ht[:, :, :].rearrange("p (a k) c -> p a (k c)", a=2), ps[:, 4:6, 0:4 * TR], ACT.Copy)\
                  .then_inc(ht_out, 1)

            def esplit(n, s, arrived, first=False):
                ac.wait_ge(eraw_in[s], arrived)
                if not first:
                    ac.wait_ge(e_used, n - 2)
                ac.activation(ehi[s % 3][:, :], eraw[s][:, :], ACT.Copy).then_inc(ehi_ok, 1)

            def xet(c):
                ac.wait_ge(xet_ps, c + 1)
                ac.activation(xethi[:, :, :].rearrange("p (a k) c -> p a (k c)", a=2), ps[:, 4:6, :], ACT.Copy)\
                  .then_inc(xet_hi, 1)

            def gated(c, ready):
                ac.wait_ge(e_used, ready)
                ac.activation(sig[:, :], ps[:, 0, :], ACT.Sigmoid).then_inc(sig_ok, 1)

            def hidt(c):
                ac.wait_ge(hidt_ps, c + 1)
                ac.activation(hthi[:, :, :].rearrange("p j c -> p (j c)"), ps[:, 6, :], ACT.Copy).then_inc(hidt_hi, 1)

            def y_copy(c, ready, first=False):
                ac.wait_ge(e_used, ready)
                if not first:
                    ac.wait_ge(y_sent, 16 * c)
                ac.activation(yout[:, :].rearrange("p (h n) -> p h n", h=2), ps[:, 2:4, :], ACT.Copy).then_inc(y_out, 1)

            def y_send(c):
                ac.wait_ge(y_out, c + 1)
                ac.dma_start(y_dram[bass.ds(c * CAP, CAP), :], yout[:, :]).then_inc(y_sent, 16)

            def expert(e, y=True, more=True):
                esplit(6 * e, 0, 16 * e + 16)
                if y:
                    y_copy(e - 2, 6 * e - 2, y == "first")
                esplit(6 * e + 1, 1, 16 * e + 16)
                if y:
                    y_send(e - 2)
                gated(e, 6 * e)
                hidt(e - 1)
                esplit(6 * e + 2, 2, 16 * e + 16)
                esplit(6 * e + 3, 3, 16 * e + 16)
                if more:
                    xet(e + 1)
                esplit(6 * e + 4, 4, 16 * e + 16)
                esplit(6 * e + 5, 5, 16 * e + 16)

            ac.wait_ge(h_ps, TT)
            for n in range(3):
                esplit(n, n, 16, True)
            ac.wait_ge(rd, 3)
            ac.activation(gd[:, :, :], gd[:, :, :], ACT.Exp).then_inc(r_exp, 1)
            ac.wait_ge(rd, R_DD)
            ac.activation(m2[:, :], m2[:, :], ACT.Exp).then_inc(r_exp, 1)
            xet(0)
            esplit(3, 3, 16)
            gated(0, 2)
            esplit(4, 4, 16)
            esplit(5, 5, 16)
            xet(1)
            expert(1, False)
            expert(2, "first")
            with ac.Fori(3, NE - 1) as e:
                expert(e)
            expert(NE - 1, True, False)
            y_copy(NE - 2, 6 * NE - 2)
            y_send(NE - 2)
            hidt(NE - 1)
            y_copy(NE - 1, 6 * NE)
            y_send(NE - 1)
            ac.wait_ge(y_sent, 16 * NE)
            n_over = ac.value_load(ove[0:1, 8:9], min_val=0, max_val=NOVER)
            with ac.Fori(0, NOVER) as j:
                with ac.If(j < n_over):
                    n, c = 6 * j + 6 * NE, j + NE
                    xet(c)
                    for k in range(4):
                        esplit(n + k, k, 16 * c + 16)
                    gated(c, n + 2)
                    esplit(n + 4, 4, 16 * c + 16)
                    esplit(n + 5, 5, 16 * c + 16)
                    hidt(c)
                    y_copy(c, n + 6)
                    y_send(c)
            ac.wait_ge(y_sent, 16 * n_over + 16 * NE)
            ac.sem_inc(moe_done, 1)
            for t in range(TT):
                ac.wait_ge(f_stat, 10 * t + 4)
                ac.activation(lstat[0:TR, 15:16], lstat[0:TR, 14:15], ACT.Sqrt).then_inc(sq_out, 1)
                ac.wait_ge(f_stat, 10 * t + 9)
                ac.activation(res[t % 2][:, :], res[t % 2][:, :], ACT.Identity, bias=lstat[0:TR, 20:21],
                              scale=lstat[0:TR, 18:19]).then_inc(f_nrm, 1)

        @block.tensor
        def _(pe):
            pe.wait_ge(id_in, 16)
            pe.wait_ge(x_in, 16 * (NB + 1))
            for k in range(KD):
                if k >= 2:
                    pe.wait_ge(xt_hi, k - 1)
                    pe.wait_ge(xt_lo, k - 1)
                for t in range(NB):
                    last = pe.transpose(ps[:, 4 + k % 2, t * P:t * P + P], xtok[:, t, k * P:k * P + P], ident)
                last.then_inc(xt_ps, 1)
            for k in range(KD):
                last = pe.transpose(ps[:, 6, k * NS:k * NS + NS], xsam[:, k * P:k * P + P], ident[0:NS, 0:NS])
            last.then_inc(xt_ps, 1)

            def product(outs, parts, start=True, stop=True):
                for n, out in enumerate(outs):
                    for k, (sh, sl, mh, ml) in enumerate(parts):
                        pe.matmul(out, sh, mh[n], start=start and k == 0, stop=False)
                        pe.matmul(out, sl, mh[n], start=False, stop=False)
                        last = pe.matmul(out, sh, ml[n], start=False, stop=stop and k == len(parts) - 1)
                return last

            def cols(w, n):
                return w[:, n * P:n * P + P]

            def by_half(ap):
                return [ap[:, 0:TH], ap[:, TH:T]]

            def tokens(s):
                return [ps[:, 2 * s + h, 0:TH] for h in range(2)]

            def xk(t, k):
                return by_half(t[:, k * T:k * T + T])

            pe.wait_ge(xt_hi, KD + 1)
            pe.wait_ge(xt_lo, KD + 1)

            def z_piece(n, s, first=False):
                pe.wait_ge(lo_split, n + 1)
                for u in range(2):
                    if not first:
                        pe.wait_ge(z_out, 2 * n + u - 1)
                    last = product(tokens(u), [(cols(whi[s], 8 * u + k), cols(wlo[s], 8 * u + k), xk(xhi, k), xk(xlo, k))
                                               for k in range(KD)])
                    last.then_inc(piece_used if u else z_even, 1)

            z_piece(0, 0, True)
            z_piece(1, 1)
            with pe.Fori(1, ZP // 2) as i:
                for j in range(2):
                    z_piece(2 * i + j, j)
            pe.wait_ge(m_in, 16)
            for k in range(4):
                if k >= 2:
                    pe.wait_ge(xt_hi, KD + k)
                    pe.wait_ge(xt_lo, KD + k)
                for u in range(4):
                    last = pe.transpose(ps[:, 4 + k % 2, u * P:u * P + P],
                                        mtok[:, u % 2, (2 * k + u // 2) * P:(2 * k + u // 2) * P + P], ident)
                last.then_inc(xt_ps, 1)
            pe.wait_ge(st_in, 16)
            n = NS * PST
            for g in range(4):
                last = pe.transpose(ps[:, 7, g * n:g * n + n], pstate[:, g * P:g * P + P], ident[0:n, 0:n])
            last.then_inc(st_ps, 1)
            pe.wait_ge(xt_hi, KD + 5)
            pe.wait_ge(xt_lo, KD + 5)
            pe.wait_ge(pad_zero, 2)
            pe.wait_ge(lo_split, N_V + 1)
            for b in range(NB + 1):
                out = ps[:, 4 + b // 2, (b % 2) * 256:(b % 2) * 256 + 256]
                last = product([out], [(xhi[:, k * T + b * P:k * T + b * P + P], xlo[:, k * T + b * P:k * T + b * P + P],
                                        [whi[0][:, k * 256:k * 256 + 256]], [wlo[0][:, k * 256:k * 256 + 256]])
                                       for k in range(KD)])
            last.then_inc(piece_used, 1)
            pe.wait_ge(z_out, ZT)
            pe.wait_ge(st_out, 1)
            for j in range(2):
                n = N_M + j
                pe.wait_ge(lo_split, n + 1)
                for m in range(2):
                    last = product([ps[:, (7, 0)[m], :]],
                                   [(mthi[:, 4 * j + k, m * P:m * P + P], mtlo[:, 4 * j + k, m * P:m * P + P],
                                     [whi[n % 2][:, k * 512:k * 512 + 512]], [wlo[n % 2][:, k * 512:k * 512 + 512]])
                                    for k in range(4)], start=j == 0, stop=j == 1)
                last.then_inc(piece_used, 1)
            pe.wait_ge(mkv_out, 2)
            for t in range(2):
                for m in range(2):
                    last = pe.transpose(ps[:, 1, t * 256 + m * P:t * 256 + m * P + P], mkv[:, m, t * P:t * P + P], ident)
            last.then_inc(mkt_ps, 1)
            pe.wait_ge(con_in, 64)
            pe.wait_ge(v_out, 3)
            for r, t in enumerate((0, 1, 2, 3, 4, 5, 6, 7, ZK, ZK + 1)):
                if r >= 2:
                    pe.wait_ge(rot_mul, r - 1)
                for h in range(2):
                    last = pe.matmul(ps[:, 2 + 2 * (r % 2) + h, 0:TH], con[:, C_ROT:C_ROT + P],
                                     z[:, t, h * TH:h * TH + TH], start=True, stop=True)
                last.then_inc(rot_ps, 1)
            pe.wait_ge(roped, 10)
            for p in range(2):
                last = pe.transpose(ps[:, 6, p * P:p * P + P], z[:, ZK + p, SEQ - P:SEQ], ident)
            last.then_inc(row_ps, 1)
            for p in range(2):
                last = pe.transpose(ps[0:NS, 6, 256 + p * P:256 + p * P + P], z[:, ZK + p, SEQ:T], ident)
            last.then_inc(row_ps, 1)
            pe.wait_ge(mkv_out, 2)
            for g in range(4):
                last = pe.transpose(ps[0:PST + NS, 7, g * P:g * P + P], z[:, ZU + g, SEQ - PST:T], ident)
            last.then_inc(row_ps, 1)
            for g in range(4):
                pe.wait_ge(pooled_in, g + 1)
                if g >= 2:
                    pe.wait_ge(mix_hi, g - 1)
                    pe.wait_ge(mix_lo, g - 1)
                for h in range(2):
                    last = pe.matmul(ps[:, 2 + 2 * (g % 2) + h, 0:TH], wmix[:, g, :],
                                     pooled[:, g, h * TH:h * TH + TH], start=True, stop=True)
                last.then_inc(mix_ps, 1)

            def scores(g):
                kind, b, h = groups[g]
                s = g % 2
                if g >= 2:
                    pe.wait_ge(sc_exp, g - 1)
                for j in range(GRP):
                    if kind == "swa":
                        r, p = 64 * (h % 2), h // 2
                        k0, w = (0, P) if b == 0 else ((b - 1) * P, 2 * P)
                        q, k = z[r:r + 64, 4 * p + j, b * P:b * P + P], z[r:r + 64, ZK + p, k0:k0 + w]
                    else:
                        m = MEM_ORDER[j]
                        r, w = 64 * (m % 2), NMEM
                        q, k = z[r:r + 64, ZC + m // 2, b * P:b * P + P], mkt[r:r + 64, m // 2, :]
                    last = pe.matmul(ps[:, 2 * s + j // 2, (j % 2) * 256:(j % 2) * 256 + w], q, k, start=True, stop=True)
                last.then_inc(sc_ps, 1)

            pe.wait_ge(mkt_out, 1)
            pe.wait_ge(mix_hi, 4)
            pe.wait_ge(mix_lo, 4)
            pe.wait_ge(row_out, 3)
            scores(0)
            for g, (kind, b, h) in enumerate(groups):
                s = g % 2
                if g + 1 < NGR:
                    scores(g + 1)
                nk = 1 if kind == "swa" and b == 0 else 2
                pe.wait_ge(sc_nrm, g + 1)
                if g:
                    pe.wait_ge(pt_act, g)
                    pe.wait_ge(pt_dve, g)
                for k in range(nk):
                    for j in range(GRP):
                        last = pe.transpose(ps[:, 4 + k, j * P:j * P + P], probs[s][:, j, k * P:k * P + P], ident)
                last.then_inc(pt_ps, 1)
                pe.wait_ge(pt_act, g + 1)
                pe.wait_ge(pt_dve, g + 1)
                if g >= 2:
                    pe.wait_ge(o_hi, g - 1)
                    pe.wait_ge(o_lo, g - 1)
                if kind == "swa":
                    r = 64 * (h % 2)
                    for k in range(nk):
                        last = pe.matmul(ps[r:r + 64, 6 + s, :], v[:, b - nk + 1 + k, h * HD:h * HD + HD],
                                         pt[s][:, k, :], start=k == 0, stop=k == nk - 1)
                else:
                    for j, m in enumerate(MEM_ORDER):
                        r = 64 * (m % 2)
                        for k in range(2):
                            last = pe.matmul(ps[r:r + 64, 6 + s, (m // 2) * P:(m // 2) * P + P],
                                             mkv[:, k, 256 + m * HD:256 + m * HD + HD], pt[s][:, k, j * P:j * P + P],
                                             start=k == 0, stop=k == 1)
                last.then_inc(o_ps, 1)

            pe.wait_ge(o_hi, NGR)
            pe.wait_ge(o_lo, NGR)
            pe.wait_ge(win_in, 16)
            for q in range(4):
                for u in range(4):
                    last = pe.transpose(ps[:, 4 + q % 2, u * P:u * P + P],
                                        cach_k[:, 2 * q + u // 2, (u % 2) * P:(u % 2) * P + P], ident)
                last.then_inc(sa_ps, 1)
                pe.wait_ge(sa_act, q + 1)
                for u in range(2):
                    for h in range(NKV):
                        r, p, b = 64 * (h % 2), h // 2, 2 * q + u
                        last = pe.matmul(ps[:, h % 2, h * 32 + b * 4:h * 32 + b * 4 + 4],
                                         kt[q % 2][r:r + 64, (2 * u + p) * P:(2 * u + p) * P + P],
                                         z[r:r + 64, 4 * p:4 * p + 4, SEQ + b], start=True, stop=True)
                last.then_inc(sa_ps, 1)
            pe.wait_ge(qsam_ok, 1)
            for h in range(NKV):
                r, p = 64 * (h % 2), h // 2
                last = pe.matmul(ps[32 * h:32 * h + 32, 3, 0:NS],
                                 qsam[r:r + 64, 32 * p:32 * p + 32],
                                 z[r:r + 64, ZK + p, SEQ:T], start=True, stop=True)
            last.then_inc(sa_ps, 1)
            pe.wait_ge(sa_act, 5)
            pe.transpose(ps[:, 2, 0:P], scol[:, :], ident).then_inc(sa_ps, 1)
            pe.wait_ge(sa_dve, 11)
            pe.transpose(ps[:, 3, 0:P], srow[:, 0:P], ident)
            pe.transpose(ps[0:NS, 3, P:2 * P], sstat[:, 8:16], ident).then_inc(sa_ps, 1)
            pe.wait_ge(sa_act, 7)
            pe.wait_ge(winv_in, 16)
            for h in range(NKV):
                r, p = 64 * (h % 2), h // 2
                last = pe.matmul(ps[r:r + 64, 6, 32 * p:32 * p + 32], v[0:NS, NB, h * HD:h * HD + HD],
                                 pnew[0:NS, 32 * h:32 * h + 32], start=p == 0, stop=False, skip_group_check=True)
            for b in range(NS):
                for h in range(NKV):
                    r, p = 64 * (h % 2), h // 2
                    last = pe.matmul(ps[r:r + 64, 6, 32 * p + 4 * b:32 * p + 4 * b + 4],
                                     cach_v[:, b, h * HD:h * HD + HD],
                                     pcol[:, 32 * h + 4 * b:32 * h + 4 * b + 4],
                                     start=False, stop=b == NS - 1, skip_group_check=True)
            last.then_inc(sa_ps, 1)
            for b in range(NS):
                pe.wait_ge(cm_in, 32 + 32 * (b // 4))
                for u in range(4):
                    last = pe.transpose(ps[:, 4 + b % 2, u * P:u * P + P],
                                        cach_k[:, 2 * (b % 4) + u // 2, (u % 2) * P:(u % 2) * P + P], ident)
                last.then_inc(sa_ps, 1)
                pe.wait_ge(sa_act, 9 + b)
                for h in range(MH):
                    r = 64 * (h % 2)
                    for k in range(2):
                        c = 32 * k + 8 * h + b
                        last = pe.matmul(ps[:, (7, 0)[h % 2], c:c + 1], kt[b % 2][r:r + 64, (2 * k + h // 2) * P:(2 * k + h // 2) * P + P],
                                         z[r:r + 64, ZC + h // 2, SEQ + b:SEQ + b + 1], start=True, stop=True)
                last.then_inc(sa_ps, 1)
            pe.wait_ge(sa_act, 17)
            for k in range(2):
                last = pe.transpose(ps[0:32, 2, k * P:k * P + P], scol[:, 32 * k:32 * k + 32], ident)
            last.then_inc(sa_ps, 1)
            pe.wait_ge(sa_dve, 16)
            for k in range(2):
                last = pe.transpose(ps[:, 3, 32 * k:32 * k + 32], srow[0:32, k * P:k * P + P], ident[0:32, 0:32])
            last.then_inc(sa_ps, 1)
            pe.wait_ge(sa_act, 19)
            for q in range(2):
                pe.wait_ge(cmv_in, 32 + 32 * q)
                for b in range(4 * q, 4 * q + 4):
                    for h in range(MH):
                        r, c = 64 * (h % 2), 64 + (h // 2) * NS + b
                        for k in range(2):
                            last = pe.matmul(ps[r:r + 64, 6, c:c + 1], cach_v[:, 2 * (b % 4) + k, h * HD:h * HD + HD],
                                             pcol[:, 32 * k + 8 * h + b:32 * k + 8 * h + b + 1],
                                             start=k == 0, stop=k == 1)
                last.then_inc(sa_ps, 1)

            pe.wait_ge(sa_act, 20)
            pe.wait_ge(sa_dve, 17)
            A, B = N_G % 2, (N_G + 1) % 2

            def block_of(n):
                return (A, n) if n < MT // 2 else (B, n - MT // 2)

            def merge(i, first=False):
                n = 0
                for u, (hi, lo, nk) in enumerate(((None, None, KD),) * 3 + ((oahi, oalo, 8), (obhi, oblo, 4), (ochi, oclo, 2))):
                    if u == 0:
                        pe.wait_ge(lo_split, 2 * i + N_G + 1)
                        if not first:
                            pe.wait_ge(m_step, 4 * i - 3)
                    if u == 1 and not first:
                        pe.wait_ge(m_step, 4 * i - 1)
                    if u == 2 and not first:
                        pe.wait_ge(m_val, i)
                    if u >= 3:
                        pe.wait_ge(gate_out, 3 * i + u - 2)
                    for half in range(2):
                        for k in range(nk):
                            s, q = block_of(n + k)
                            if s == B and half == 0 and q == 0:
                                pe.wait_ge(lo_split, 2 * i + N_G + 2)
                            if u < 3:
                                mh, ml = xk(xhi, k)[half], xk(xlo, k)[half]
                            else:
                                mh, ml = by_half(hi[:, k, :])[half], by_half(lo[:, k, :])[half]
                            out = ps[:, 2 * (u % 3) + half, 0:TH]
                            pe.matmul(out, cols(whi[s], q), mh, start=k == 0, stop=False)
                            pe.matmul(out, cols(wlo[s], q), mh, start=False, stop=False)
                            last = pe.matmul(out, cols(whi[s], q), ml, start=False, stop=k == nk - 1)
                            if half == 1 and n + k == MT // 2 - 1:
                                last.then_inc(piece_used, 1)
                    last.then_inc(prod_ps if u < 5 else piece_used, 1)
                    n += nk

            merge(0, True)
            with pe.Fori(1, KD) as i:
                merge(i)

            def project(t):
                if t >= 2:
                    pe.wait_ge(h_sum, t - 1)
                for k in range(KD):
                    if t == 0:
                        pe.wait_ge(lo_split, N_O + k // 2 + 1)
                    for h in range(2):
                        out = ps[0:TR, 2 * (t % 2) + h, :]
                        mt = slice(t * TR, t * TR + TR)
                        pe.matmul(out, mhi[:, k, mt], wohi[:, k, h * 512:h * 512 + 512], start=k == 0, stop=False)
                        pe.matmul(out, mlo[:, k, mt], wohi[:, k, h * 512:h * 512 + 512], start=False, stop=False)
                        last = pe.matmul(out, mhi[:, k, mt], wolo[:, k, h * 512:h * 512 + 512], start=False,
                                         stop=k == KD - 1)
                last.then_inc(h_ps, 1)

            def route(t):
                pe.wait_ge(h_done, t + 1)
                if t:
                    pe.wait_ge(ht_out, t)
                for k in range(KD):
                    last = pe.transpose(ps[:, 4 + k // 4, (k % 4) * TR:(k % 4) * TR + TR],
                                        hall[:, t, k * P:k * P + P], ident[0:TR, 0:TR])
                last.then_inc(ht_ps, 1)
                pe.wait_ge(ht_out, t + 1)
                for k in range(KD):
                    last = pe.matmul(ps[0:TR, 6, t * 20:t * 20 + 20], ht[:, k, :], wrt[:, k, :],
                                     start=k == 0, stop=k == KD - 1)
                last.then_inc(lg_ps, 1)

            pe.wait_ge(m_hi, KD)
            pe.wait_ge(m_lo, KD)
            project(0)
            for t in range(TT):
                if t + 1 < TT:
                    project(t + 1)
                route(t)
            pe.wait_ge(both_ok, 1)
            for t in range(TT):
                for u in range(t + 1):
                    pe.matmul(ps[0:TR, 7, t * NE:t * NE + NE], ones[:, 0:TR] if u < t else upper, both[:, u, :],
                              start=u == 0, stop=u == t)
            for u in range(TT):
                last = pe.matmul(ps[:, 7, TT * NE:TT * NE + NE], ones, both[:, u, :], start=u == 0, stop=u == TT - 1)
            last.then_inc(rank_ps, 1)
            pe.wait_ge(slot_in, 16)
            pe.wait_ge(slots_ok, 1)
            n = NE + NOVER
            pe.transpose(ps[:, 6, P:P + n], slrow[:, :], ident[0:n, 0:n]).then_inc(slot_ps, 1)

            def xet(c, first=False):
                pe.wait_ge(xe_in, 16 * c + 16)
                if not first:
                    pe.wait_ge(xet_hi, c)
                    pe.wait_ge(xet_lo, c)
                for k in range(KD):
                    last = pe.transpose(ps[:, 4 + k // 4, (k % 4) * P:(k % 4) * P + P],
                                        xe[:, :].rearrange("p (c k) -> p k c", k=KD)[:, k, :], ident)
                last.then_inc(xet_ps, 1)

            def wide(n, s, bank, first=False, free=None):
                if free is not None:
                    pe.wait_ge(*free)
                for j in range(2):
                    pe.wait_ge(elo_ok, n + j + 1)
                    for q in range(4):
                        k, w = 4 * j + q, slice(q * 512, q * 512 + 512)
                        pe.matmul(ps[:, bank, :], xethi[:, k, :], ehi[s[j]][:, w], start=k == 0, stop=False)
                        pe.matmul(ps[:, bank, :], xetlo[:, k, :], ehi[s[j]][:, w], start=False, stop=False)
                        last = pe.matmul(ps[:, bank, :], xethi[:, k, :], elo[s[j]][:, w], start=False, stop=k == KD - 1)
                    last.then_inc(e_used, 1)

            def hidt(c, first=False):
                pe.wait_ge(hid_ok, c + 1)
                if not first:
                    pe.wait_ge(hidt_hi, c)
                    pe.wait_ge(hidt_lo, c)
                for j in range(4):
                    last = pe.transpose(ps[:, 6, j * P:j * P + P], hid[:, :].rearrange("p (c j) -> p j c", j=4)[:, j, :],
                                        ident)
                last.then_inc(hidt_ps, 1)

            def down(c, n, s, first=False):
                pe.wait_ge(hidt_hi, c + 1)
                pe.wait_ge(hidt_lo, c + 1)
                if not first:
                    pe.wait_ge(y_out, c)
                for j in range(2):
                    pe.wait_ge(elo_ok, n + j + 1)
                    for q in range(2):
                        f = 2 * j + q
                        for h in range(2):
                            w = slice(q * D + h * 512, q * D + h * 512 + 512)
                            pe.matmul(ps[:, 2 + h, :], hthi[:, f, :], ehi[s[j]][:, w], start=f == 0, stop=False)
                            pe.matmul(ps[:, 2 + h, :], htlo[:, f, :], ehi[s[j]][:, w], start=False, stop=False)
                            last = pe.matmul(ps[:, 2 + h, :], hthi[:, f, :], elo[s[j]][:, w], start=False, stop=f == 3)
                    last.then_inc(e_used, 1)

            def expert(e, first=False, more=True):
                pe.wait_ge(xet_hi, e + 1)
                pe.wait_ge(xet_lo, e + 1)
                wide(6 * e - 2, (1, 2), 0, free=(act_ok, e))
                hidt(e - 1, first)
                wide(6 * e, (0, 1), 1, free=(hid_ok, e))
                if more:
                    xet(e + 1)
                down(e - 1, 6 * e + 2, (2, 0), first)

            xet(0, True)
            pe.wait_ge(xet_hi, 1)
            pe.wait_ge(xet_lo, 1)
            wide(0, (0, 1), 0)
            wide(2, (2, 0), 1)
            xet(1)
            expert(1, True)
            with pe.Fori(2, NE - 1) as e:
                expert(e)
            expert(NE - 1, more=False)
            hidt(NE - 1)
            down(NE - 1, 6 * NE - 2, (1, 2))
            n_over = pe.value_load(ove[0:1, 8:9], min_val=0, max_val=NOVER)
            with pe.Fori(0, NOVER) as j:
                with pe.If(j < n_over):
                    n, c = 6 * j + 6 * NE, j + NE
                    xet(c)
                    pe.wait_ge(xet_hi, c + 1)
                    pe.wait_ge(xet_lo, c + 1)
                    wide(n, (0, 1), 0, free=(act_ok, c))
                    wide(n + 2, (2, 0), 1, free=(hid_ok, c))
                    hidt(c)
                    down(c, n + 4, (1, 2))

        @block.vector
        def _(ve):
            for k in range(KD):
                ve.wait_ge(xt_hi, k + 1)
                ve.tensor_tensor(xlo[:, k * T:k * T + SEQ], ps[:, 4 + k % 2, :], xhi[:, k * T:k * T + SEQ].bitcast(F32),
                                 ALU.subtract).then_inc(xt_lo, 1)
            ve.wait_ge(xt_hi, KD + 1)
            ve.tensor_tensor(xlo[:, 0:KD * T].rearrange("p (k t) -> p k t", k=KD)[:, :, SEQ:T],
                             ps[:, 6, 0:KD * NS].rearrange("p (k t) -> p k t", k=KD),
                             xhi[:, 0:KD * T].rearrange("p (k t) -> p k t", k=KD)[:, :, SEQ:T].bitcast(F32),
                             ALU.subtract).then_inc(xt_lo, 1)

            def split(n, s, width, first=False, out=None, hi=None):
                ve.wait_ge(hi_split, n + 1)
                if not first:
                    ve.wait_ge(piece_used, n - 1)
                ve.tensor_tensor(wlo[s][:, 0:width] if out is None else out, raw[s][:, 0:width],
                                 (whi[s][:, 0:width] if hi is None else hi).bitcast(F32), ALU.subtract)\
                  .then_inc(lo_split, 1)

            split(0, 0, PW, True)
            split(1, 1, PW, True)
            with ve.Fori(0, ZP // 2) as i:
                for j in range(2):
                    split(2 * i + j + 2, j, PW)
            for k in range(4):
                ve.wait_ge(xt_hi, KD + 2 + k)
                ve.tensor_tensor(mtlo[:, 2 * k:2 * k + 2, :], ps[:, 4 + k % 2, :].rearrange("p (k m) -> p k m", k=2),
                                 mthi[:, 2 * k:2 * k + 2, :].bitcast(F32), ALU.subtract).then_inc(xt_lo, 1)
            split(N_M + 1, 0, PW)
            for j in range(2):
                split(N_G + j, (N_G + j) % 2, MPW)
            ve.wait_ge(con_in, 64)
            ve.tensor_scalar(nsink[:, :], prm[:, 0:17], -1.0, None, ALU.mult).then_inc(prep, 1)
            for r, t in enumerate((0, 1, 2, 3, 4, 5, 6, 7, ZK, ZK + 1)):
                s = r % 2
                ve.wait_ge(rot_ps, r + 1)
                ve.tensor_tensor(halves(rtmp[s][:, :]), pair(1 + s), halves(con[:, C_SIN:C_SIN + T]), ALU.mult)\
                  .then_inc(rot_mul, 1)
                ve.wait_ge(rot_mul, r + 1)
                ve.wait_ge(rot_cos, r + 1)
                ve.tensor_tensor(z[:, t, :], z[:, t, :], rtmp[s][:, :], ALU.add).then_inc(roped, 1)
            for g in range(4):
                ve.wait_ge(mix_hi, g + 1)
                ve.scalar_tensor_tensor(halves(oblo[:, g, :]), pair(1 + g % 2), prm[:, Q_PSC + g:Q_PSC + g + 1],
                                        halves(obhi[:, g, :].bitcast(F32)), ALU.mult, ALU.subtract).then_inc(mix_lo, 1)
            ve.wait_ge(prep, 1)
            ve.wait_ge(roped, 10)

            def row_max(g):
                kind, b, h = groups[g]
                s = g % 2
                st = stat[:, s]
                src = ps[:, 2 * s:2 * s + 2, :].rearrange("p a (j w) -> p (a j) w", j=2)
                ve.wait_ge(sc_ps, g + 1)
                if kind == "swa":
                    w = P if b == 0 else 2 * P
                    mask = con[:, C_MASK + 2 * P - w:C_MASK + 2 * P].rearrange("p (a w) -> p a w", a=1)
                    if g >= 2:
                        ve.wait_ge(pt_ps, g - 1)
                    ve.scalar_tensor_tensor(probs[s][:, :, 0:w], src[:, :, 0:w], SCALE, mask.broadcast_to([P, GRP, w]),
                                            ALU.mult, ALU.add).then_inc(sc_row, 1)
                    ve.wait_ge(sc_row, g + 1)
                    ve.tensor_reduce(st[:, 0, :], probs[s][:, :, 0:w], AX.X, ALU.max).then_inc(sc_max, 1)
                    ve.wait_ge(sc_max, g + 1)
                    ve.scalar_tensor_tensor(st[:, 1, :], st[:, 0, :], -1.0, nsink[:, 4 * h:4 * h + 4], ALU.mult,
                                            ALU.min).then_inc(sc_neg, 1)
                    ve.wait_ge(sc_neg, g + 1)
                    ve.tensor_tensor(st[:, 2, :], st[:, 1, :], prm[:, 4 * h:4 * h + 4], ALU.add).then_inc(sc_snk, 1)
                else:
                    ve.tensor_reduce(st[:, 0, :], src, AX.X, ALU.max).then_inc(sc_max, 1)
                    ve.wait_ge(sc_max, g + 1)
                    ve.tensor_scalar(st[:, 1, :], st[:, 0, :], -SCALE, None, ALU.mult).then_inc(sc_neg, 1)

            row_max(0)
            for g, (kind, b, h) in enumerate(groups):
                s = g % 2
                st = stat[:, s]
                if g + 1 < NGR:
                    row_max(g + 1)
                w = P if kind == "swa" and b == 0 else 2 * P
                ve.wait_ge(sc_exp, g + 1)
                den = 3
                if kind == "swa":
                    ve.tensor_tensor(st[:, 5, :], st[:, 3, :], st[:, 4, :], ALU.add).then_inc(sc_den, 1)
                    ve.wait_ge(sc_den, g + 1)
                    den = 5
                ve.reciprocal(st[:, 6, :], st[:, den, :]).then_inc(sc_rec, 1)
                ve.wait_ge(sc_rec, g + 1)
                ve.tensor_tensor(probs[s][:, :, 0:w], probs[s][:, :, 0:w],
                                 st[:, 6, :].rearrange("p (j w) -> p j w", w=1).broadcast_to([P, GRP, w]), ALU.mult)\
                  .then_inc(sc_nrm, 1)
                ve.wait_ge(pt_ps, g + 1)
                if g >= 2:
                    ve.wait_ge(o_ps, g - 1)
                if w == P:
                    ve.wait_ge(pt_act, g + 1)
                    ve.tensor_copy(pt[s][:, 0, 256:512], ps[:, 4, 256:512]).then_inc(pt_dve, 1)
                else:
                    ve.tensor_copy(pt[s][:, 1, :], ps[:, 5, :]).then_inc(pt_dve, 1)
                ve.wait_ge(o_hi, g + 1)
                if kind == "swa":
                    r, p = 64 * (h % 2), h // 2
                    dst = (slice(r, r + 64), slice(4 * p, 4 * p + 4), slice(b * P, b * P + P))
                    ve.tensor_tensor(oalo[dst], ps[r:r + 64, 6 + s, :].rearrange("p (j q) -> p j q", j=4),
                                     oahi[dst].bitcast(F32), ALU.subtract).then_inc(o_lo, 1)
                else:
                    dst = (slice(0, P), slice(0, 2), slice(b * P, b * P + P))
                    ve.tensor_tensor(oclo[dst], ps[:, 6 + s, 0:256].rearrange("p (t q) -> p t q", t=2),
                                     ochi[dst].bitcast(F32), ALU.subtract).then_inc(o_lo, 1)

            ve.wait_ge(rows_sent, 64)
            for p in range(2):
                last = ve.tensor_copy(qsam[:, 32 * p:32 * p + 32].rearrange("p (b j) -> p b j", j=4),
                                      z[:, 4 * p:4 * p + 4, SEQ:T].rearrange("p j b -> p b j"))
            last.then_inc(qsam_ok, 1)
            ve.wait_ge(sa_ps, 9)
            ve.tensor_tensor(sstat[:, 8:16], ps[:, 3, 0:NS], con[:, C_BM:C_BM + NS], ALU.mult).then_inc(sa_dve, 1)
            ve.wait_ge(sa_dve, 1)
            ve.tensor_reduce(sstat[:, 5:6], sstat[:, 8:16], AX.X, ALU.add).then_inc(sa_dve, 1)
            ve.wait_ge(sa_dve, 2)
            ve.tensor_scalar(srow[:, P:P + 1], sstat[:, 5:6], SCALE, None, ALU.mult).then_inc(sa_dve, 1)
            ve.wait_ge(sa_ps, 10)
            ve.tensor_scalar(srow[:, 0:P], ps[:, 2, 0:P], SCALE, None, ALU.mult).then_inc(sa_dve, 1)
            ve.wait_ge(sa_dve, 4)
            ve.tensor_reduce(sstat[:, 0:1], srow[:, 0:WIN + 1], AX.X, ALU.max).then_inc(sa_dve, 1)
            ve.wait_ge(sa_dve, 5)
            ve.scalar_tensor_tensor(sstat[:, 1:2], sstat[:, 0:1], -1.0, nsink[:, 16:17], ALU.mult, ALU.min)\
              .then_inc(sa_dve, 1)
            ve.wait_ge(sa_dve, 6)
            ve.tensor_tensor(sstat[:, 2:3], sstat[:, 1:2], prm[:, Q_SINKR:Q_SINKR + 1], ALU.add).then_inc(sa_dve, 1)
            ve.wait_ge(sa_act, 6)
            ve.tensor_tensor(sstat[:, 5:6], sstat[:, 3:4], sstat[:, 4:5], ALU.add).then_inc(sa_dve, 1)
            ve.wait_ge(sa_dve, 8)
            ve.reciprocal(sstat[:, 6:7], sstat[:, 5:6]).then_inc(sa_dve, 1)
            ve.wait_ge(sa_dve, 9)
            ve.tensor_scalar(srow[:, 0:WIN + 1], srow[:, 0:WIN + 1], sstat[:, 6:7], None, ALU.mult).then_inc(sa_dve, 1)
            ve.wait_ge(sa_dve, 10)
            ve.tensor_scalar(sstat[:, 8:16], con[:, C_BM:C_BM + NS], srow[:, P:P + 1], None, ALU.mult).then_inc(sa_dve, 1)
            ve.wait_ge(sa_act, 8)
            for p in range(2):
                last = ve.tensor_tensor(oalo[:, 4 * p:4 * p + 4, SEQ:T],
                                        ps[:, 6, 32 * p:32 * p + 32].rearrange("p (b j) -> p j b", j=4),
                                        oahi[:, 4 * p:4 * p + 4, SEQ:T].bitcast(F32), ALU.subtract)
            last.then_inc(sa_dve, 1)
            ve.wait_ge(sa_ps, 29)
            ve.tensor_reduce(sstat[0:32, 0:1], ps[0:32, 2, 0:NMEM], AX.X, ALU.max).then_inc(sa_dve, 1)
            ve.wait_ge(sa_dve, 13)
            ve.tensor_scalar(sstat[0:32, 1:2], sstat[0:32, 0:1], -SCALE, None, ALU.mult).then_inc(sa_dve, 1)
            ve.wait_ge(sa_act, 18)
            ve.reciprocal(sstat[0:32, 6:7], sstat[0:32, 3:4]).then_inc(sa_dve, 1)
            ve.wait_ge(sa_dve, 15)
            ve.tensor_scalar(srow[0:32, 0:NMEM], srow[0:32, 0:NMEM], sstat[0:32, 6:7], None, ALU.mult)\
              .then_inc(sa_dve, 1)
            ve.wait_ge(sa_act, 20)
            ve.tensor_tensor(oclo[:, :, SEQ:T], ps[:, 6, 64:80].rearrange("p (t b) -> p t b", t=2),
                             ochi[:, :, SEQ:T].bitcast(F32), ALU.subtract).then_inc(sa_dve, 1)

            def merge(i, more):
                if more:
                    split(2 * i + N_G + 2, N_G % 2, MPW)
                ve.wait_ge(m_lo, i)
                ve.wait_ge(prod_ps, 5 * i + 4)
                ve.tensor_tensor(halves(mval[:, :]), pair(0), halves(gate[0][:, :]), ALU.mult).then_inc(m_step, 1)
                ve.wait_ge(prod_ps, 5 * i + 5)
                ve.tensor_tensor(halves(gate[1][:, :]), pair(1), halves(gate[1][:, :]), ALU.mult).then_inc(m_step, 1)
                ve.wait_ge(m_step, 4 * i + 2)
                ve.tensor_tensor(mval[:, :], mval[:, :], gate[1][:, :], ALU.add).then_inc(m_step, 1)
                ve.wait_ge(piece_used, 2 * i + N_G + 2)
                ve.wait_ge(gate_out, 3 * i + 3)
                ve.tensor_tensor(halves(gate[2][:, :]), pair(2), halves(gate[2][:, :]), ALU.mult).then_inc(m_step, 1)
                ve.wait_ge(m_step, 4 * i + 4)
                ve.tensor_tensor(mval[:, :], mval[:, :], gate[2][:, :], ALU.add).then_inc(m_val, 1)
                if more:
                    split(2 * i + N_G + 3, (N_G + 1) % 2, MPW)
                ve.wait_ge(m_hi, i + 1)
                ve.tensor_tensor(mlo[:, bass.ds(i, 1), :].rearrange("p a c -> p (a c)"), mval[:, :],
                                 mhi[:, bass.ds(i, 1), :].rearrange("p a c -> p (a c)").bitcast(F32),
                                 ALU.subtract).then_inc(m_lo, 1)

            with ve.Fori(0, KD - 1) as i:
                merge(i, True)
            merge(KD - 1, False)
            for j in range(4):
                n = N_O + j
                split(n, n % 2, PW, True, out=wolo[:, 2 * j:2 * j + 2, :].rearrange("p k n -> p (k n)"),
                      hi=wohi[:, 2 * j:2 * j + 2, :].rearrange("p k n -> p (k n)"))

            ls = lstat[0:TR]

            def norm(x, t, step, before, nrm, root, done):
                k = 10 * t
                for h in range(2):
                    ve.bn_stats(ls[:, 6 * h:6 * h + 6], x[:, 512 * h:512 * h + 512]).then_inc(step, 1)
                ve.wait_ge(step, k + 2)
                ve.bn_aggr(ls[:, 12:14], ls[:, 0:12]).then_inc(step, 1)
                ve.wait_ge(step, k + 3)
                ve.tensor_scalar(ls[:, 14:15], ls[:, 13:14], EPS, None, ALU.add).then_inc(step, 1)
                ve.wait_ge(sq_out, root)
                ve.reciprocal(ls[:, 16:17], ls[:, 15:16]).then_inc(step, 1)
                ve.wait_ge(step, k + 5)
                ve.tensor_scalar(ls[:, 17:18], ls[:, 16:17], ls[:, 16:17], ls[:, 14:15], ALU.mult, ALU.mult)\
                  .then_inc(step, 1)
                ve.wait_ge(step, k + 6)
                ve.tensor_scalar(ls[:, 19:20], ls[:, 17:18], -0.5, 1.5, ALU.mult, ALU.add).then_inc(step, 1)
                ve.wait_ge(step, k + 7)
                ve.tensor_tensor(ls[:, 18:19], ls[:, 19:20], ls[:, 16:17], ALU.mult).then_inc(step, 1)
                ve.wait_ge(step, k + 8)
                ve.scalar_tensor_tensor(ls[:, 20:21], ls[:, 12:13], -1.0, ls[:, 18:19], ALU.mult, ALU.mult)\
                  .then_inc(step, 1)
                ve.wait_ge(nrm, t + 1)
                ve.tensor_tensor(x, x, lng[0:TR, :], ALU.mult).then_inc(step, 1)
                ve.wait_ge(step, k + 10)
                ve.tensor_tensor(x, x, lnb[0:TR, :], ALU.add).then_inc(done, 1)

            ve.wait_ge(ln_in, 32)
            for t in range(TT):
                ve.wait_ge(xrow_in[t % 2], 16 * (t // 2 + 1) + 16 * (t == TT - 1))
                ve.wait_ge(h_ps, t + 1)
                ve.scalar_tensor_tensor(hall[:, t, :], xrow[t % 2][:, :], ALPHA,
                                        ps[0:TR, 2 * (t % 2):2 * (t % 2) + 2, :].rearrange("p a n -> p (a n)"),
                                        ALU.mult, ALU.add).then_inc(h_sum, 1)
                ve.wait_ge(h_sum, t + 1)
                norm(hall[:, t, :], t, h_stat, None, h_nrm, t + 1, h_done)

            def esplit(n, s, first=False):
                ve.wait_ge(ehi_ok, n + 1)
                if not first:
                    ve.wait_ge(e_used, n - 2)
                ve.tensor_tensor(elo[s % 3][:, :], eraw[s][:, :], ehi[s % 3][:, :].bitcast(F32), ALU.subtract)\
                  .then_inc(elo_ok, 1)

            count = [0]

            def link(ins):
                count[0] += 1
                ins.then_inc(rd, 1)
                ve.wait_ge(rd, count[0])

            def over(x, n):
                return x[:, :].rearrange("p (t a) -> p t a", a=1).broadcast_to([TR, TT, n])

            i4, i16 = both_dims(con[0:TR, C_I4:C_I4 + 4], 4), both_dims(con[0:TR, C_I16:C_I16 + 16], 16)
            ve.wait_ge(lg_ps, TT)
            ve.wait_ge(h_done, TT)
            link(ve.tensor_tensor(lg[:, :, :], ps[0:TR, 6, 0:20 * TT].rearrange("p (t n) -> p t n", t=TT),
                                  both_dims(prm[0:TR, Q_BIAS:Q_BIAS + 20], 20), ALU.add))
            link(ve.tensor_reduce(gm[:, :], lg[:, :, 0:4], AX.X, ALU.max))
            link(ve.tensor_tensor(gd[:, :, :], lg[:, :, 0:4], over(gm, 4), ALU.subtract))
            link(ve.tensor_tensor(gk[:, :, :], lg[:, :, 0:4], over(gm, 4), ALU.is_lt))
            link(ve.tensor_scalar(gk[:, :, :], gk[:, :, :], 100.0, None, ALU.mult))
            link(ve.tensor_tensor(gk[:, :, :], gk[:, :, :], i4, ALU.add))
            link(ve.tensor_reduce(gi[:, :], gk[:, :, :], AX.X, ALU.min))
            link(ve.tensor_tensor(gk[:, :, :], i4, over(gi, 4), ALU.is_equal))
            link(ve.tensor_scalar(gk[:, :, :], gk[:, :, :], -1.0, -NEG, ALU.add, ALU.mult))
            link(ve.tensor_tensor(em[:, :, :].rearrange("p t (g e) -> p t g e", g=4),
                                  lg[:, :, 4:20].rearrange("p t (g e) -> p t g e", g=4),
                                  gk[:, :, :].rearrange("p t (g a) -> p t g a", a=1).broadcast_to([TR, TT, 4, 4]), ALU.add))

            def best(value, index, onehot):
                link(ve.tensor_reduce(value[:, :], em[:, :, :], AX.X, ALU.max))
                link(ve.tensor_tensor(cd[:, :, :], em[:, :, :], over(value, NE), ALU.is_lt))
                link(ve.tensor_scalar(cd[:, :, :], cd[:, :, :], 100.0, None, ALU.mult))
                link(ve.tensor_tensor(cd[:, :, :], cd[:, :, :], i16, ALU.add))
                link(ve.tensor_reduce(index[:, :], cd[:, :, :], AX.X, ALU.min))
                link(ve.tensor_tensor(onehot[:, :, :], i16, over(index, NE), ALU.is_equal))

            best(m1, i1, one1)
            link(ve.tensor_scalar(cd[:, :, :], one1[:, :, :], NEG, None, ALU.mult))
            link(ve.tensor_tensor(em[:, :, :], em[:, :, :], cd[:, :, :], ALU.add))
            best(m2, i2, one2)
            link(ve.tensor_tensor(m2[:, :], m2[:, :], m1[:, :], ALU.subtract))
            assert count[0] == R_DD
            ve.tensor_tensor(both[:, :, :], one1[:, :, :], one2[:, :, :], ALU.add).then_inc(both_ok, 1)
            ve.wait_ge(r_exp, 2)
            link(ve.tensor_reduce(gs[:, :], gd[:, :, :], AX.X, ALU.add))
            link(ve.tensor_scalar(m1[:, :], m2[:, :], 1.0, None, ALU.add))
            link(ve.tensor_tensor(m1[:, :], m1[:, :], gs[:, :], ALU.mult))
            link(ve.reciprocal(w1[:, :], m1[:, :]))
            link(ve.tensor_tensor(w2[:, :], m2[:, :], w1[:, :], ALU.mult))
            ve.wait_ge(rank_ps, 1)
            link(ve.tensor_copy(slotf[:, :, :], ps[0:TR, 7, 0:TT * NE].rearrange("p (t n) -> p t n", t=TT)))
            link(ve.tensor_copy(cnt[:, :], ps[:, 7, TT * NE:TT * NE + NE]))
            link(ve.tensor_scalar(oc[:, :], cnt[:, :], float(CAP), None, ALU.is_gt))
            for m in range(2, TT):
                link(ve.tensor_scalar(inc[0][:, :], cnt[:, :], float(CAP * m), None, ALU.is_gt))
                link(ve.tensor_tensor(oc[:, :], oc[:, :], inc[0][:, :], ALU.add))
            src = oc
            for k, d in enumerate((1, 2, 4, 8)):
                dst = inc[k % 2]
                link(ve.tensor_copy(dst[:, 0:d], src[:, 0:d]))
                link(ve.tensor_tensor(dst[:, d:NE], src[:, d:NE], src[:, 0:NE - d], ALU.add))
                src = dst
            link(ve.tensor_tensor(base2[:, :], src[:, :], oc[:, :], ALU.subtract))
            link(ve.tensor_scalar(base2[:, :], base2[:, :], float(CAP), float(NE * CAP - CAP), ALU.mult, ALU.add))
            link(ve.tensor_tensor(base2[:, :], base2[:, :], con[:, C_B1:C_B1 + NE], ALU.subtract))
            link(ve.tensor_scalar(sltmp[:, :, :], slotf[:, :, :], float(CAP), None, ALU.is_ge))
            link(ve.tensor_tensor(sltmp[:, :, :], sltmp[:, :, :], both_dims(base2[0:TR, :], NE), ALU.mult))
            link(ve.tensor_tensor(slotf[:, :, :], slotf[:, :, :], sltmp[:, :, :], ALU.add))
            link(ve.tensor_tensor(slotf[:, :, :], slotf[:, :, :], both_dims(con[0:TR, C_B1:C_B1 + NE], NE), ALU.add))
            for onehot, sf, si in ((one1, s1f, s1), (one2, s2f, s2)):
                link(ve.tensor_tensor(sltmp[:, :, :], slotf[:, :, :], onehot[:, :, :], ALU.mult))
                link(ve.tensor_reduce(sf[:, :], sltmp[:, :, :], AX.X, ALU.add))
                link(ve.tensor_copy(si[:, :], sf[:, :]))
            link(ve.tensor_tensor(ovf[:, :, :], con[:, C_I8:C_I8 + 8].rearrange("p (j a) -> p j a", a=1).broadcast_to([P, 8, NE]),
                                  src[:, :].rearrange("p (a e) -> p a e", a=1).broadcast_to([P, 8, NE]), ALU.is_ge))
            link(ve.tensor_reduce(ovi[:, :], ovf[:, :, :], AX.X, ALU.add))
            link(ve.tensor_scalar(ove[:, 0:8], ovi[:, :], float(NE - 1), None, ALU.min))
            ve.tensor_copy(ove[:, 8:9], src[:, NE - 1:NE]).then_inc(slots_ok, 1)
            for n in range(3):
                esplit(n, n, True)
            ve.wait_ge(slot_ps, 1)
            ve.tensor_copy(slots[:, :], ps[:, 6, P:P + NE + NOVER]).then_inc(slot_ok, 1)

            def xet(c):
                ve.wait_ge(xet_hi, c + 1)
                ve.tensor_tensor(xetlo[:, :, :].rearrange("p (a k) c -> p a (k c)", a=2), ps[:, 4:6, :],
                                 xethi[:, :, :].rearrange("p (a k) c -> p a (k c)", a=2).bitcast(F32), ALU.subtract)\
                  .then_inc(xet_lo, 1)

            def silu(c):
                ve.wait_ge(sig_ok, c + 1)
                ve.wait_ge(hid_ok, c)
                ve.tensor_tensor(act[:, :], ps[:, 0, :], sig[:, :], ALU.mult).then_inc(act_ok, 1)

            def hidden(c, ready, first=False):
                ve.wait_ge(e_used, ready)
                ve.wait_ge(act_ok, c + 1)
                if not first:
                    ve.wait_ge(hidt_ps, c)
                ve.tensor_tensor(hid[:, :], ps[:, 1, :], act[:, :], ALU.mult).then_inc(hid_ok, 1)

            def hidt(c):
                ve.wait_ge(hidt_hi, c + 1)
                ve.tensor_tensor(htlo[:, :, :].rearrange("p j c -> p (j c)"), ps[:, 6, :],
                                 hthi[:, :, :].rearrange("p j c -> p (j c)").bitcast(F32), ALU.subtract)\
                  .then_inc(hidt_lo, 1)

            def expert(e, more=True):
                esplit(6 * e, 0)
                esplit(6 * e + 1, 1)
                silu(e)
                hidt(e - 1)
                esplit(6 * e + 2, 2)
                esplit(6 * e + 3, 3)
                hidden(e, 6 * e + 2)
                if more:
                    xet(e + 1)
                esplit(6 * e + 4, 4)
                esplit(6 * e + 5, 5)

            xet(0)
            esplit(3, 3)
            silu(0)
            esplit(4, 4)
            esplit(5, 5)
            hidden(0, 4, True)
            xet(1)
            with ve.Fori(1, NE - 1) as e:
                expert(e)
            expert(NE - 1, False)
            hidt(NE - 1)
            n_over = ve.value_load(ove[0:1, 8:9], min_val=0, max_val=NOVER)
            with ve.Fori(0, NOVER) as j:
                with ve.If(j < n_over):
                    n, c = 6 * j + 6 * NE, j + NE
                    xet(c)
                    for k in range(4):
                        esplit(n + k, k)
                    silu(c)
                    esplit(n + 4, 4)
                    esplit(n + 5, 5)
                    hidden(c, n + 4)
                    hidt(c)

            ve.wait_ge(ln2_in, 32)
            for t in range(TT):
                s = t % 2
                ve.wait_ge(ya_in[s], 32 * (t // 2 + 1))
                ve.tensor_scalar(ya[s][:, :], ya[s][:, :], w1[:, t:t + 1], None, ALU.mult).then_inc(f_step, 1)
                if t >= 2:
                    ve.wait_ge(f_sent[s], 16 * (t // 2))
                ve.wait_ge(f_step, 2 * t + 1)
                ve.scalar_tensor_tensor(res[s][:, :], hall[:, t, :], ALPHA, ya[s][:, :], ALU.mult, ALU.add)\
                  .then_inc(f_step, 1)
                ve.wait_ge(f_step, 2 * t + 2)
                ve.scalar_tensor_tensor(res[s][:, :], yb[s][:, :], w2[:, t:t + 1], res[s][:, :], ALU.mult, ALU.add)\
                  .then_inc(f_sum, 1)
                ve.wait_ge(f_sum, t + 1)
                norm(res[s][:, :], t, f_stat, None, f_nrm, TT + t + 1, f_done)

        @block.gpsimd
        def _(gp):
            gp.memset(xhi[:, KD * T:XPAD].bitcast(F32), 0.0).then_inc(pad_zero, 1)
            gp.memset(xlo[:, KD * T:XPAD].bitcast(F32), 0.0).then_inc(pad_zero, 1)
            gp.memset(zslot[:, :], 0.0).then_inc(z_slot, 1)
            gp.wait_ge(z_slot, 1)
            gp.dma_start(slot_dram.rearrange("(c p) a -> c (p a)", p=P), zslot[:, :]).then_inc(z_sent, 16)
            gp.memset(zrow[:, :], 0.0).then_inc(z_slot, 1)
            gp.wait_ge(z_slot, 2)
            for c in range(NE, NE + NOVER):
                gp.dma_start(y_dram[c * CAP:c * CAP + CAP, :], zrow[:, :]).then_inc(z_sent, 16)
            gp.wait_ge(con_in, 64)
            gp.wait_ge(xt_hi, KD + 1)
            gp.wait_ge(xt_lo, KD + 1)
            gp.wait_ge(z_out, ZK)
            gp.wait_ge(st_out, 1)
            count = [0]

            def link(ins):
                count[0] += 1
                ins.then_inc(pool_step, 1)
                gp.wait_ge(pool_step, count[0])

            link(gp.tensor_copy(pext[:, :, :, PST], z[:, ZU:ZU + 4, SEQ:T]))
            for g, w in enumerate(POOL_W):
                src, d, k = z[:, ZU + g, :], 1, 0
                while d < w:
                    dst = pbuf[k % 2]
                    link(gp.tensor_copy(dst[:, 0:d], src[:, 0:d]))
                    link(gp.tensor_tensor(dst[:, d:SEQ], src[:, d:SEQ], src[:, 0:SEQ - d], ALU.add))
                    src, d, k = dst, 2 * d, k + 1
                cur, n = pext[:, g, :, PST + 1 - w:PST + 1], w
                while n > 1:
                    half = pext[:, g, :, PST + 1 - w:PST + 1 - w + n // 2]
                    link(gp.tensor_tensor(half, cur[:, :, 0:n // 2], cur[:, :, n // 2:n], ALU.add))
                    cur, n = half, n // 2
                link(gp.tensor_copy(src[:, SEQ:T], cur[:, :, 0]))
                link(gp.tensor_tensor(src[:, 0:16], src[:, 0:16], con[:, C_POOL + 16 * g:C_POOL + 16 * g + 16], ALU.mult))
                link(gp.tensor_scalar(src[:, 0:T], src[:, 0:T], 1.0 / w, None, ALU.mult))
                gp.tensor_tensor(pooled[:, g, :], src[:, 0:T], z[:, ZU + g, :], ALU.subtract).then_inc(pooled_in, 1)
                gp.wait_ge(pooled_in, g + 1)
            for r, t in enumerate((0, 1, 2, 3, 4, 5, 6, 7, ZK, ZK + 1)):
                gp.wait_ge(rot_ps, r + 1)
                gp.tensor_tensor(z[:, t, :], z[:, t, :], con[:, C_COS:C_COS + T], ALU.mult).then_inc(rot_cos, 1)
            for t in range(TT):
                gp.wait_ge(h_done, t + 1)
                gp.dma_start(h_dram[t * TR:t * TR + TR, :], hall[:, t, :]).then_inc(h_sent, 16)
            gp.wait_ge(slots_ok, 1)
            gp.wait_ge(z_sent, 16 * (NOVER + 1))
            for t in range(TT):
                for s in (s1, s2):
                    gp.indirect_dma_start(out=slot_dram, out_offset=bass.IndirectOffsetOnAxis(ap=s[:, t:t + 1], axis=0),
                                          in_=con[0:TR, C_TOK + t:C_TOK + t + 1], in_offset=None).then_inc(slot_sent, 16)
            gp.wait_ge(slot_sent, 16 * 2 * TT)
            gp.dma_start(slrow[:, :], slot_dram.rearrange("(c p) a -> c (p a)", p=P)).then_inc(slot_in, 16)
            gp.wait_ge(slot_ok, 1)
            gp.wait_ge(h_sent, 16 * TT)

            def gather(c, first=False):
                if not first:
                    gp.wait_ge(xe_in, 16 * c)
                    gp.wait_ge(xet_ps, c)
                gp.tensor_copy(slotc[:, :], slots[:, bass.ds(c, 1)]).then_inc(slc_ok, 1)
                gp.wait_ge(slc_ok, c + 1)
                gp.sem_inc(slc_seen, 1)
                gp.indirect_dma_start(out=xe[:, :], out_offset=None, in_=h_dram,
                                      in_offset=bass.IndirectOffsetOnAxis(ap=slotc[:, :], axis=0)).then_inc(xe_in, 16)

            gather(0, True)
            with gp.Fori(1, NE) as c:
                gather(c)
            n_over = gp.value_load(ove[0:1, 8:9], min_val=0, max_val=NOVER)
            with gp.Fori(0, NOVER) as j:
                with gp.If(j < n_over):
                    gather(j + NE)
            gp.wait_ge(moe_done, 1)
            for t in range(TT):
                if t >= 2:
                    gp.wait_ge(f_sum, t - 1)
                for dst, s in ((ya, s1), (yb, s2)):
                    gp.indirect_dma_start(out=dst[t % 2][:, :], out_offset=None, in_=y_dram,
                                          in_offset=bass.IndirectOffsetOnAxis(ap=s[:, t:t + 1], axis=0))\
                      .then_inc(ya_in[t % 2], 16)


def constants():
    import numpy as np

    c = np.zeros((P, C_END), np.float32)
    c[:, C_ID:C_ID + P] = np.eye(P)
    half = HD // 8
    for head in range(2):
        for d in range(half):
            c[head * HD + d + half, C_ROT + head * HD + d] = -1.0
            c[head * HD + d, C_ROT + head * HD + d + half] = 1.0
    pos = np.concatenate([np.arange(SEQ), np.full(NS, 2048)]).astype(np.float32)
    inv = np.power(np.float32(500000.0), -np.arange(half, dtype=np.float32) * np.float32(2.0 / (2 * half)))
    ang = pos[None, :] * inv.astype(np.float32)[:, None]
    c[:, C_COS:C_COS + T] = 1.0
    for head in range(2):
        for rep in range(2):
            r = head * HD + rep * half
            c[r:r + half, C_COS:C_COS + T] = np.cos(ang)
            c[r:r + half, C_SIN:C_SIN + T] = np.sin(ang)
    i, k = np.arange(P)[:, None], np.arange(2 * P)[None, :]
    c[:, C_MASK:C_MASK + 2 * P] = np.where((k <= P + i) & (k >= i), 0.0, NEG)
    t = np.arange(16)
    for g, w in enumerate(POOL_W):
        c[:, C_POOL + 16 * g:C_POOL + 16 * g + 16] = w / np.minimum(t + 1, w)
    c[:TR, C_UP:C_UP + TR] = np.triu(np.ones((TR, TR)), 1)
    c[:, C_ONE:C_ONE + P] = 1.0
    c[:, C_I4:C_I4 + 4] = np.arange(4)
    c[:, C_I16:C_I16 + 16] = np.arange(16)
    c[:, C_B1:C_B1 + NE] = np.arange(NE) * CAP
    c[:TR, C_TOK:C_TOK + TT] = np.arange(TT)[None, :] * TR + np.arange(TR)[:, None]
    c[:, C_BM:C_BM + NS] = (np.arange(P)[:, None] % 32 // 4) == np.arange(NS)[None, :]
    c[:, C_I8:C_I8 + 8] = np.arange(8)
    return c


def kernel(**inputs):
    import numpy as np
    import concourse.bacc as bacc
    from concourse.bass_utils import run_bass_kernel_spmd

    x = {k: np.asarray(w) for k, w in inputs.items()}
    w_in = x["w_in"][0]
    heads = [8 * (t // 4) + t % 4 + 4 * s for t in range(8) for s in range(2)]
    q0, k0, v0, u0, c0, g0 = 0, 1024, 1280, 1536, 2048, 2304
    qcols = [q0 + h * HD + d for h in heads for d in range(HD)]
    zcols = qcols + list(range(u0, c0)) + list(range(k0, v0)) + list(range(c0, g0))

    def blocks(w):
        return w.reshape(w.shape[0] // P, P, w.shape[1] // P, P).transpose(2, 1, 0, 3)

    wz = blocks(w_in[:, zcols]).reshape(ZP, 2, P, KD * P).transpose(0, 2, 1, 3).reshape(ZP, P, PW)
    wv = w_in[:, v0:u0].reshape(KD, P, 256).transpose(1, 0, 2).reshape(P, PW)
    wmem = np.concatenate([x["w_mem_k"][0], x["w_mem_v"][0]], 1).reshape(2, 4, P, 512).transpose(0, 2, 1, 3)
    wa = x["w_branch_a"][0][qcols]
    parts = [w_in[:, g0 + D * g:g0 + D * g + D] for g in range(3)] + [wa, x["w_branch_b"][0], x["w_branch_c"][0]]
    wm = np.concatenate([blocks(w) for w in parts], 2).reshape(KD, P, 2, MPW).transpose(0, 2, 1, 3)
    sinks = x["sinks"][0]
    params = np.concatenate([
        np.broadcast_to(sinks, (P, NH)),
        sinks.reshape(NKV, 1, GRP).repeat(NS, 1).reshape(P, 1),
        x["pool_scale"][0].reshape(4, P).T,
        np.broadcast_to(np.concatenate([x["b_group"][0], x["b_router"][0].reshape(-1)]), (P, 20)),
    ], 1)
    w_route = np.concatenate([x["w_group"][0], x["w_router"][0].reshape(D, NE)], 1)
    data = {
        "consts": constants(),
        "params": params,
        "x_prompt": x["x_prompt"].reshape(SEQ, D),
        "x_sample": x["x_sample"].reshape(NS, D),
        "cache_win_k": x["cache_win_k"].reshape(NS, WIN, 256),
        "cache_win_v": x["cache_win_v"].reshape(NS, WIN, 256),
        "state_pool": x["state_pool"].reshape(NS, PST, 512),
        "cache_mem_k": x["cache_mem_k"].reshape(NS, NMEM, 256),
        "cache_mem_v": x["cache_mem_v"].reshape(NS, NMEM, 256),
        "mem_prompt": x["mem_prompt"].reshape(NMEM, D),
        "wz": wz, "wv": wv, "wmem": wmem.reshape(2, P, PW), "wm": wm.reshape(2 * KD, P, MPW),
        "wo": x["w_out"][0].reshape(4, 2, P, D).transpose(0, 2, 1, 3).reshape(4, P, PW),
        "w_pool_mix": x["w_pool_mix"][0],
        "w_route": w_route.reshape(KD, P, 20).transpose(1, 0, 2),
        "ln1_g": x["ln1_g"], "ln1_b": x["ln1_b"], "ln2_g": x["ln2_g"], "ln2_b": x["ln2_b"],
        "w_gate": x["w_gate"][0], "w_up": x["w_up"][0], "w_down": x["w_down"][0],
    }
    outs = {
        "y_prompt": (SEQ, D), "y_sample": (NS, D),
        "new_k_prompt": (WIN, 256), "new_v_prompt": (WIN, 256), "new_pool_prompt": (PST, 512),
        "new_mem_k": (NMEM, 256), "new_mem_v": (NMEM, 256),
        "new_k_sample": (NS, WIN, 256), "new_v_sample": (NS, WIN, 256), "new_pool_sample": (NS, PST, 512),
    }
    shapes = [
        (1, SEQ, D), (NS, 1, D), (1, 1, WIN, NKV, HD), (1, 1, WIN, NKV, HD), (1, 1, PST, 512),
        (1, 1, NMEM, MH, HD), (1, 1, NMEM, MH, HD), (1, NS, WIN, NKV, HD), (1, NS, WIN, NKV, HD), (1, NS, PST, 512),
    ]
    nc = bacc.Bacc("TRN2", target_bir_lowering=False, num_devices=1)
    arrays, a, o = {}, {}, {}
    for name, w in data.items():
        arrays[name + "_in"] = np.ascontiguousarray(w)
        a[name] = nc.dram_tensor(name + "_in", w.shape, F32, kind="ExternalInput").ap()
    for name, shape in outs.items():
        o[name] = nc.dram_tensor(name, shape, F32, kind="ExternalOutput").ap()
    decoder_step(nc, a, o)
    r = run_bass_kernel_spmd(nc, [arrays], core_ids=[0]).results[0]
    return tuple(r[name].reshape(shape) for name, shape in zip(outs, shapes))
```

```python
from contextlib import ExitStack

import concourse.bass as bass
from concourse import mybir

F32 = mybir.dt.float32
F32R = mybir.dt.float32r
I32 = mybir.dt.int32
ALU = mybir.AluOpType
ACT = mybir.ActivationFunctionType
AX = mybir.AxisListType

P = 128
D = 1024
KD = D // P
SEQ, NS = 512, 8
T = SEQ + NS
TH = T // 2
TT = 5
TR = T // TT
NB = SEQ // P
HD, NH, NKV, GRP = 64, 16, 4, 4
WIN = 128
NMEM, MH = 256, 4
POOL_W = (2, 4, 8, 16)
PST = 15
NG, EG = 4, 4
NE = NG * EG
DE = 512
CAP = P
NOVER = 8
NSLOT = (NE + NOVER) * CAP
ALPHA = 2.0 ** 0.25
EPS = 1e-5
SCALE = HD ** -0.5
NEG = -1.0e30
R_DD = 25

ZU, ZK, ZC, ZQ = 0, 4, 6, 8
ZT = 16
ZP = ZT * KD * P // 2048
MT = 3 * KD + 8 + 4 + 2
MPW = MT // 2 * P
PW = 2048

C_ID, C_ROT, C_COS, C_SIN, C_MASK = 0, 128, 256, 776, 1296
C_POOL, C_UP, C_ONE, C_I4, C_I16, C_B1, C_TOK, C_BM, C_I8, C_END = (
    1552, 1616, 1720, 1848, 1852, 1868, 1884, 1889, 1897, 1905)
Q_SINK, Q_SINKR, Q_PSC, Q_BIAS, Q_END = 0, 16, 17, 21, 41


def decoder_step(nc, a, o):
    ctx = ExitStack()
    with ctx:
        def sem(name):
            return ctx.enter_context(nc.semaphore(name))

        def at(name, offset, shape, dt=F32):
            return nc.alloc_sbuf_tensor_at(name, shape, dt, offset=offset)

        RING, X, Z, OAL = 16512, 74880, 109120, 142400
        OB, OC, ML, CON, PRM, VV, TAIL = 159040, 175680, 184000, 200640, 208320, 211200, 222464
        SL = MPW * 4
        raw = [at(f"raw{s}", RING + s * SL, [P, MPW]) for s in range(2)]
        whi = [at(f"whi{s}", RING + (2 + s) * SL, [P, MPW], F32R) for s in range(2)]
        wlo = [at(f"wlo{s}", RING + (4 + s) * SL, [P, MPW], F32R) for s in range(2)]
        XPAD = KD * T + P - NS
        xhi = at("xhi", X, [P, XPAD], F32R)
        xlo = at("xlo", X + 17120, [P, XPAD], F32R)
        z = at("z", Z, [P, ZT, T])
        oahi = at("oahi", Z + 16640, [P, 8, T], F32R)
        mhi = at("mhi", Z, [P, 8, T], F32R)
        oalo = at("oalo", OAL, [P, 8, T], F32R)
        obhi = at("obhi", OB, [P, 4, T], F32R)
        oblo = at("oblo", OB + 8320, [P, 4, T], F32R)
        ochi = at("ochi", OC, [P, 2, T], F32R)
        oclo = at("oclo", OC + 4160, [P, 2, T], F32R)
        mlo = at("mlo", ML, [P, 8, T], F32R)
        con = at("con", CON, [P, C_END])
        prm = at("prm", PRM, [P, Q_END])
        wmix = at("wmix", PRM + 192, [P, 4, P])
        wrt = at("wrt", PRM + 192 + 2048, [P, KD, 20])
        xtok = at("xtok", OAL, [P, NB, D])
        xsam = at("xsam", OAL + 16384, [NS, D])
        mtok = at("mtok", OAL + 20480, [P, 2, D])
        mthi = at("mthi", ML, [P, KD, NMEM], F32R)
        mtlo = at("mtlo", ML + 8192, [P, KD, NMEM], F32R)
        pooled = at("pooled", OAL, [P, 4, T])
        pbuf = [at(f"pbuf{s}", OAL + 8320 + s * 2080, [P, T]) for s in range(2)]
        pstate = at("pstate", OAL + 12480, [NS * PST, 512])
        pext = at("pext", OAL + 14528, [P, 4, NS, PST + 1])
        rtmp = [at(f"rtmp{s}", OAL + 8320 + s * 2080, [P, T]) for s in range(2)]
        v = at("v", VV, [P, NB + 1, NKV * HD])
        mkv = at("mkv", VV + 5120, [P, 2, 512])
        kodd = at("kodd", OC + 4160, [P, 2, T])
        mkt = at("mkt", VV + 9216, [P, 2, NMEM])
        mkodd = at("mkodd", ML + 12288, [P, 2, NMEM])
        probs = [at(f"probs{s}", ML + s * 4096, [P, GRP, 2 * P]) for s in range(2)]
        pt = at("pt", ML + 8192, [P, 2, GRP * P])
        stat = at("stat", TAIL + 512, [P, 2, 8, 4])
        nsink = at("nsink", TAIL + 768, [P, 17])
        kvrow = at("kvrow", TAIL + 1024, [P, 512])
        CACHE = RING + 2 * SL
        cach_k = at("cach_k", CACHE, [P, NS, 256])
        cach_v = at("cach_v", CACHE + 8192, [P, NS, 256])
        cm_k = [at("cm_k", CACHE + 16384, [P, NS, 256]), cach_k]
        cm_v = [at("cm_v", CACHE + 24576, [P, NS, 256]), cach_v]
        kt = at("kt", ML + 14336, [P, 512])
        srow = at("srow", TAIL + 3072, [P, 264])
        scol = at("scol", TAIL + 4160, [P, P + NS])
        pcol = at("pcol", TAIL + 4704, [P, P])
        pnew = at("pnew", TAIL + 5216, [P, P])
        sstat = at("sstat", TAIL + 5728, [P, 16])
        qsp = at("qsp", TAIL + 5792, [P, 2, 2, NS, GRP])
        cqp = at("cqp", TAIL + 6304, [P, 2, 2, NS])
        kns = at("kns", TAIL + 6432, [P, 2, NS])
        urow = at("urow", TAIL + 3072, [P, 512])
        gate = [at(f"gate{s}", VV + s * 2080, [P, T]) for s in range(3)]
        zrow = at("zrow", VV, [P, D])
        mval = at("mval", VV + 6240, [P, T])
        wohi = at("wohi", X, [P, KD, D], F32R)
        wolo = at("wolo", OAL, [P, KD, D], F32R)
        hall = at("hall", RING + 2 * SL, [TR, TT, D])
        xrow = [at(f"xrow{s}", RING + 2 * SL + 20480 + s * 4096, [TR, D]) for s in range(2)]
        ht = at("ht", RING + 2 * SL + 28672, [P, KD, TR])
        lng = at("lng", VV, [P, D])
        lnb = at("lnb", VV + 4096, [P, D])
        lstat = at("lstat", VV + 8192, [P, 32])
        R0 = ML
        K0 = VV + 8448

        def rt(name, k, shape, dt=F32):
            return at(name, R0 + k * 320, shape, dt)
        lg = at("lg", R0, [TR, TT, 20])
        gm, gd, gs = rt("gm", 2, [TR, TT]), rt("gd", 3, [TR, TT, 4]), rt("gs", 4, [TR, TT])
        gi, gk = rt("gi", 5, [TR, TT]), rt("gk", 6, [TR, TT, 4])
        em, cd = rt("em", 7, [TR, TT, NE]), rt("cd", 8, [TR, TT, NE])
        one1, one2 = rt("one1", 9, [TR, TT, NE]), rt("one2", 10, [TR, TT, NE])
        both = rt("both", 11, [TR, TT, NE])
        m1, m2, i1, i2 = (rt(n, 12 + k, [TR, TT]) for k, n in enumerate(("m1", "m2", "i1", "i2")))
        w1, w2 = at("w1", K0, [TR, TT]), at("w2", K0 + 32, [TR, TT])
        slotf, sltmp = rt("slotf", 18, [TR, TT, NE]), rt("sltmp", 19, [TR, TT, NE])
        s1f, s2f = rt("s1f", 20, [TR, TT]), rt("s2f", 21, [TR, TT])
        s1, s2 = at("s1", K0 + 64, [TR, TT], I32), at("s2", K0 + 96, [TR, TT], I32)
        cnt, oc = rt("cnt", 24, [P, NE]), rt("oc", 25, [P, NE])
        inc = [rt(f"inc{k}", 26 + k, [P, NE]) for k in range(2)]
        base2, ovf = rt("base2", 28, [P, NE]), rt("ovf", 29, [P, 8, NE])
        ovi = at("ovi", R0 + 32 * 320, [P, 8])
        ove = at("ove", K0 + 128, [P, 16], I32)
        slots = at("slots", K0 + 192, [P, NE + NOVER], I32)
        slrow = at("slrow", R0 + 33 * 320, [NE + NOVER, P])
        zslot = at("zslot", TAIL, [NE + NOVER, P])
        MR = 8192
        eraw = [at(f"eraw{s}", X + s * MR, [P, PW]) for s in range(6)]
        ehi = [at(f"ehi{s}", X + (6 + s) * MR, [P, PW], F32R) for s in range(3)]
        elo = [at(f"elo{s}", X + (9 + s) * MR, [P, PW], F32R) for s in range(3)]
        E0 = X + 12 * MR
        xe = at("xe", E0, [P, D])
        xethi = at("xethi", E0 + 4096, [P, KD, P], F32R)
        xetlo = at("xetlo", E0 + 8192, [P, KD, P], F32R)
        sig = at("sig", E0 + 12288, [P, DE])
        act = at("act", E0 + 14336, [P, DE])
        hid = at("hid", E0 + 16384, [P, DE])
        hthi = at("hthi", E0 + 18432, [P, 4, P], F32R)
        htlo = at("htlo", E0 + 20480, [P, 4, P], F32R)
        yout = at("yout", E0 + 22528, [P, D])
        slotc = at("slotc", E0 + 26624, [P, 1], I32)
        ya = [at(f"ya{s}", X + s * 8192, [TR, D]) for s in range(2)]
        yb = [at(f"yb{s}", X + s * 8192 + 4096, [TR, D]) for s in range(2)]
        res = [at(f"res{s}", X + 16384 + s * 4096, [TR, D]) for s in range(2)]

        ps = ctx.enter_context(nc.psum_tensor("ps", [P, 8, 512], F32))
        h_dram = nc.dram_tensor("h_dram", (T, D), F32, kind="Internal").ap()
        slot_dram = nc.dram_tensor("slot_dram", (NSLOT, 1), F32, kind="Internal").ap()
        y_dram = nc.dram_tensor("y_dram", (NSLOT, D), F32, kind="Internal").ap()

        ident = con[:, C_ID:C_ID + P]
        upper = con[0:TR, C_UP:C_UP + TR]
        ones = con[0:TR, C_ONE:C_ONE + P]

        id_in, con_in, x_in, m_in = sem("id_in"), sem("con_in"), sem("x_in"), sem("m_in")
        st_in, win_in, winv_in, cmv_in = (sem(n) for n in ("st_in", "win_in", "winv_in", "cmv_in"))
        cm_in = [sem(f"cm_in{q}") for q in range(2)]
        raw_in = [sem(f"raw_in{s}") for s in range(2)]
        hi_split, lo_split, piece_used = sem("hi_split"), sem("lo_split"), sem("piece_used")
        pad_zero = sem("pad_zero")
        xt_ps, xt_hi, xt_lo = sem("xt_ps"), sem("xt_hi"), sem("xt_lo")
        z_even, z_out = sem("z_even"), sem("z_out")
        v_out, mkv_out, mkt_ps, mkt_out = sem("v_out"), sem("mkv_out"), sem("mkt_ps"), sem("mkt_out")
        v_ps, pads, kodd_ok = sem("v_ps"), sem("pads"), sem("kodd_ok")
        rot_ps, rot_mul, rot_cos, roped = sem("rot_ps"), sem("rot_mul"), sem("rot_cos"), sem("roped")
        row_ps, row_out, rows_sent = sem("row_ps"), sem("row_out"), sem("rows_sent")
        st_ps, st_out, pool_step, pooled_in = sem("st_ps"), sem("st_out"), sem("pool_step"), sem("pooled_in")
        mix_ps, mix_hi, mix_lo = sem("mix_ps"), sem("mix_hi"), sem("mix_lo")
        prep = sem("prep")
        sc_ps, sc_row, sc_max, sc_neg, sc_snk, sc_exp, sc_den, sc_rec, sc_nrm = (sem(n) for n in (
            "sc_ps", "sc_row", "sc_max", "sc_neg", "sc_snk", "sc_exp", "sc_den", "sc_rec", "sc_nrm"))
        pt_ps, pt_act, pt_dve, o_ps, o_hi, o_lo = (sem(n) for n in (
            "pt_ps", "pt_act", "pt_dve", "o_ps", "o_hi", "o_lo"))
        qs_ok, kt_ps, kt_ok, ks_ps = sem("qs_ok"), sem("kt_ps"), sem("kt_ok"), sem("ks_ps")
        sw_ps, sw_act, sw_dve = sem("sw_ps"), sem("sw_act"), sem("sw_dve")
        sm_ps, sm_act, sm_dve = sem("sm_ps"), sem("sm_act"), sem("sm_dve")
        prod_ps, gate_out, m_step, m_val, m_hi, m_lo = (sem(n) for n in (
            "prod_ps", "gate_out", "m_step", "m_val", "m_hi", "m_lo"))
        ln_in, xrow_in = sem("ln_in"), [sem(f"xrow_in{s}") for s in range(2)]
        h_ps, h_sum, h_stat, h_nrm, h_done, h_sent = (sem(n) for n in (
            "h_ps", "h_sum", "h_stat", "h_nrm", "h_done", "h_sent"))
        sq_in, sq_out = sem("sq_in"), sem("sq_out")
        ht_ps, ht_out, lg_ps, lg_out = sem("ht_ps"), sem("ht_out"), sem("lg_ps"), sem("lg_out")
        rd, r_exp, both_ok, rank_ps, slots_ok, z_slot, z_sent = (sem(n) for n in (
            "rd", "r_exp", "both_ok", "rank_ps", "slots_ok", "z_slot", "z_sent"))
        slot_sent, slot_in, slot_ps, slot_ok = sem("slot_sent"), sem("slot_in"), sem("slot_ps"), sem("slot_ok")
        eraw_in = [sem(f"eraw_in{s}") for s in range(6)]
        ehi_ok, elo_ok, e_used = sem("ehi_ok"), sem("elo_ok"), sem("e_used")
        slc_seen = sem("slc_seen")
        slc_ok, xe_in, xet_ps, xet_hi, xet_lo = (sem(n) for n in ("slc_ok", "xe_in", "xet_ps", "xet_hi", "xet_lo"))
        g_ps, sig_ok, act_ok, hid_ok, hidt_ps, hidt_hi, hidt_lo = (sem(n) for n in (
            "g_ps", "sig_ok", "act_ok", "hid_ok", "hidt_ps", "hidt_hi", "hidt_lo"))
        y_out, y_sent, moe_done = sem("y_out"), sem("y_sent"), sem("moe_done")
        ln2_in, ya_in = sem("ln2_in"), [sem(f"ya_in{s}") for s in range(2)]
        f_step, f_sum, f_stat, f_nrm, f_done = (sem(n) for n in ("f_step", "f_sum", "f_stat", "f_nrm", "f_done"))
        f_sent = [sem(f"f_sent{s}") for s in range(2)]
        copied = sem("copied")

        groups = [("swa", b, 2 * p + s) for p in range(2) for b in range(NB) for s in range(2)] \
            + [("mem", b, 0) for b in range(NB)]
        NGR = len(groups)
        MEM_ORDER = (0, 2, 1, 3)
        ROT = (ZK, ZK + 1) + tuple(range(ZQ, ZQ + 8))
        NKT = 4 + NS
        S_T1, S_T2, S_PV = 5, 7, 8
        M_T1, M_T2, M_PV = 13, 15, 16
        N_V, N_M, N_G = ZP, ZP + 1, ZP + 3
        N_O = N_G + 2 * KD

        def both_dims(src, n):
            return src.rearrange("p (a n) -> p a n", a=1).broadcast_to([TR, TT, n])

        def halves(ap):
            return ap.rearrange("p (h c) -> p h c", h=2)

        def pair(s, rows=slice(0, P)):
            return ps[rows, 2 * s:2 * s + 2, 0:TH]

        block = ctx.enter_context(nc.Block())

        @block.sync
        def _(sp):
            sp.dma_start(con[:, 0:P], a["consts"][:, 0:P]).then_inc(id_in, 16)
            xp = a["x_prompt"].rearrange("(t p) d -> p t d", p=P)
            for t in range(NB):
                sp.dma_start(xtok[:, t, :], xp[:, t, :]).then_inc(x_in, 16)
            sp.dma_start(xsam[:, :], a["x_sample"]).then_inc(x_in, 16)

            def piece(n, src, width, first=False):
                if not first:
                    sp.wait_ge(hi_split, n - 1)
                    sp.wait_ge(lo_split, n - 1)
                sp.dma_start(raw[n % 2][:, 0:width], src).then_inc(raw_in[n % 2], 16)

            for n in range(2):
                piece(n, a["wz"][n], PW, True)
            sp.dma_start(mtok[:, :, :], a["mem_prompt"].rearrange("(t p) d -> p t d", p=P)).then_inc(m_in, 16)
            sp.dma_start(con[:, P:C_END], a["consts"][:, P:C_END]).then_inc(con_in, 16)
            sp.dma_start(prm[:, :], a["params"]).then_inc(con_in, 16)
            sp.dma_start(wmix[:, :, :], a["w_pool_mix"].rearrange("g c d -> c g d")).then_inc(con_in, 16)
            sp.dma_start(wrt[:, :, :], a["w_route"]).then_inc(con_in, 16)
            sp.wait_ge(xt_lo, KD + 1)
            sp.wait_ge(xt_hi, KD + 1)
            sp.dma_start(pstate[:, :], a["state_pool"].rearrange("b r c -> (b r) c")).then_inc(st_in, 16)
            with sp.Fori(1, ZP // 2) as i:
                for j in range(2):
                    sp.wait_ge(hi_split, 2 * i + j - 1)
                    sp.wait_ge(lo_split, 2 * i + j - 1)
                    sp.dma_start(raw[j][:, 0:PW], a["wz"][bass.ds(2 * i + j, 1)].rearrange("a p n -> (a p) n"))\
                      .then_inc(raw_in[j], 16)
            piece(N_V, a["wv"], PW)
            for j in range(2):
                piece(N_M + j, a["wmem"][j], PW)
            for j in range(2):
                piece(N_G + j, a["wm"][j], MPW)
            sp.wait_ge(piece_used, N_M + 2)
            sp.dma_start(cach_k[:, :, :], a["cache_win_k"].rearrange("b k d -> k b d")).then_inc(win_in, 16)
            sp.dma_start(cach_v[:, :, :], a["cache_win_v"].rearrange("b k d -> k b d")).then_inc(winv_in, 16)
            ck = a["cache_mem_k"].rearrange("b (t p) d -> p b t d", p=P)
            cv = a["cache_mem_v"].rearrange("b (t p) d -> p b t d", p=P)

            def half_cache(dst, src, q, arrived):
                for t in range(2):
                    sp.dma_start(dst[q][:, :, :].rearrange("p (b t) d -> p b t d", t=2)[:, :, t, :],
                                 src[:, 4 * q:4 * q + 4, t, :]).then_inc(arrived, 16)

            half_cache(cm_k, ck, 0, cm_in[0])
            half_cache(cm_v, cv, 0, cmv_in)
            sp.wait_ge(v_out, 3)
            sp.dma_start(o["new_v_prompt"], v[:, NB - 1, :]).then_inc(copied, 16)
            sp.dma_start(o["new_v_sample"][:, WIN - 1, :], v[0:NS, NB, :]).then_inc(copied, 16)
            sp.wait_ge(mkv_out, 2)
            sp.dma_start(o["new_mem_k"].rearrange("(t p) d -> p t d", p=P), mkv[:, :, 0:256]).then_inc(copied, 16)
            sp.dma_start(o["new_mem_v"].rearrange("(t p) d -> p t d", p=P), mkv[:, :, 256:512]).then_inc(copied, 16)
            sp.dma_start(o["new_k_sample"][:, 0:WIN - 1, :], a["cache_win_k"][:, 1:WIN, :]).then_inc(copied, 16)
            sp.dma_start(o["new_v_sample"][:, 0:WIN - 1, :], a["cache_win_v"][:, 1:WIN, :]).then_inc(copied, 16)
            sp.dma_start(o["new_pool_sample"][:, 0:PST - 1, :], a["state_pool"][:, 1:PST, :]).then_inc(copied, 16)
            sp.wait_ge(row_out, 2)
            sp.dma_start(o["new_k_prompt"], kvrow[:, 0:256]).then_inc(rows_sent, 16)
            sp.dma_start(o["new_k_sample"][:, WIN - 1, :], kvrow[0:NS, 256:512]).then_inc(rows_sent, 16)
            sp.wait_ge(row_out, 3)
            sp.dma_start(o["new_pool_prompt"], urow[0:PST, :]).then_inc(rows_sent, 16)
            sp.dma_start(o["new_pool_sample"][:, PST - 1, :], urow[PST:PST + NS, :]).then_inc(rows_sent, 16)
            sp.wait_ge(kt_ps, 4)
            half_cache(cm_k, ck, 1, cm_in[1])
            sp.wait_ge(sw_ps, 4)
            half_cache(cm_v, cv, 1, cmv_in)
            with sp.Fori(1, KD) as i:
                for j in range(2):
                    s = (N_G + j) % 2
                    sp.wait_ge(hi_split, 2 * i + N_G + j - 1)
                    sp.wait_ge(lo_split, 2 * i + N_G + j - 1)
                    sp.dma_start(raw[s][:, :], a["wm"][bass.ds(2 * i + j, 1)].rearrange("a p n -> (a p) n"))\
                      .then_inc(raw_in[s], 16)
            for j in range(4):
                piece(N_O + j, a["wo"][j], PW)
            sp.wait_ge(m_hi, KD)
            sp.wait_ge(m_lo, KD)
            sp.dma_start(lng[:, :], a["ln1_g"].broadcast_to([P, D])).then_inc(ln_in, 16)
            sp.dma_start(lnb[:, :], a["ln1_b"].broadcast_to([P, D])).then_inc(ln_in, 16)
            for t in range(TT):
                if t >= 2:
                    sp.wait_ge(h_sum, t - 1)
                n = min(TR, SEQ - t * TR)
                sp.dma_start(xrow[t % 2][0:n, :], a["x_prompt"][t * TR:t * TR + n, :]).then_inc(xrow_in[t % 2], 16)
                if n < TR:
                    sp.dma_start(xrow[t % 2][n:TR, :], a["x_sample"]).then_inc(xrow_in[t % 2], 16)

            def expert_piece(n, s, src, first=False):
                if not first:
                    sp.wait_ge(ehi_ok, n - 5)
                    sp.wait_ge(elo_ok, n - 5)
                sp.dma_start(eraw[s][:, :], src).then_inc(eraw_in[s], 16)

            wg = a["w_gate"].rearrange("e (p h k) n -> e h p (k n)", h=2, k=4)
            wu = a["w_up"].rearrange("e (p h k) n -> e h p (k n)", h=2, k=4)
            wd = a["w_down"].rearrange("e (p h k) n -> e h p (k n)", h=2, k=2)

            def of(w, e, h):
                return w[bass.ds(e, 1), h].rearrange("a p n -> (a p) n")

            sp.wait_ge(h_ps, TT)
            for n in range(4):
                expert_piece(n, n, (wg if n < 2 else wu)[0, n % 2], True)
            for n in range(2):
                expert_piece(4 + n, 4 + n, wg[1, n], True)
            for n in range(2):
                expert_piece(6 + n, n, wu[1, n])
            for n in range(2):
                expert_piece(8 + n, 2 + n, wd[0, n])
            with sp.Fori(2, NE) as e:
                for k, w in enumerate((wg, wg, wu, wu)):
                    expert_piece(6 * e - 2 + k, (4 + k) % 6, of(w, e, k % 2))
                for k in range(2):
                    expert_piece(6 * e + 2 + k, 2 + k, of(wd, e - 1, k))
            for k in range(2):
                expert_piece(6 * NE - 2 + k, 4 + k, wd[NE - 1, k])
            sp.wait_ge(h_done, TT)
            sp.dma_start(lng[:, :], a["ln2_g"].broadcast_to([P, D])).then_inc(ln2_in, 16)
            sp.dma_start(lnb[:, :], a["ln2_b"].broadcast_to([P, D])).then_inc(ln2_in, 16)
            sp.wait_ge(slots_ok, 1)
            n_over = sp.value_load(ove[0:1, 8:9], min_val=0, max_val=NOVER)
            with sp.Fori(0, NOVER) as j:
                e = sp.value_load(ove[0:1, bass.ts(j, 1)], min_val=0, max_val=NE - 1)
                with sp.If(j < n_over):
                    for k, w in enumerate((wg, wg, wu, wu, wd, wd)):
                        expert_piece(6 * NE + 6 * j + k, k, of(w, e, k % 2))
            for t in range(TT):
                sp.wait_ge(f_done, t + 1)
                n = min(TR, SEQ - t * TR)
                sp.dma_start(o["y_prompt"][t * TR:t * TR + n, :], res[t % 2][0:n, :]).then_inc(f_sent[t % 2], 16)
                if n < TR:
                    sp.dma_start(o["y_sample"], res[t % 2][n:TR, :]).then_inc(f_sent[t % 2], 16)
            sp.wait_ge(f_sent[0], 16 * 4)
            sp.wait_ge(f_sent[1], 16 * 2)
            sp.wait_ge(copied, 16 * 7)
            sp.wait_ge(rows_sent, 16 * 4)

        @block.scalar
        def _(ac):
            for k in range(KD):
                ac.wait_ge(xt_ps, k + 1)
                ac.activation(xhi[:, k * T:k * T + SEQ], ps[:, 4 + k % 2, :], ACT.Copy).then_inc(xt_hi, 1)
            ac.wait_ge(xt_ps, KD + 1)
            ac.activation(xhi[:, 0:KD * T].rearrange("p (k t) -> p k t", k=KD)[:, :, SEQ:T],
                          ps[:, 6, 0:KD * NS].rearrange("p (k t) -> p k t", k=KD), ACT.Copy).then_inc(xt_hi, 1)

            def split(n, s, width, arrived, first=False, out=None):
                ac.wait_ge(raw_in[s], arrived)
                if not first:
                    ac.wait_ge(piece_used, n - 1)
                ac.activation(whi[s][:, 0:width] if out is None else out, raw[s][:, 0:width], ACT.Copy)\
                  .then_inc(hi_split, 1)

            def z_tile(t, s):
                ac.activation(z[:, bass.ds(t, 1), :].rearrange("p a (h c) -> p (a h) c", h=2), pair(s),
                              ACT.Copy).then_inc(z_out, 1)

            split(0, 0, PW, 16, True)
            split(1, 1, PW, 16, True)

            def z_pair(i):
                for j in range(2):
                    ac.wait_ge(z_even, 2 * i + j + 1)
                    z_tile(4 * i + 2 * j, 0)
                    ac.wait_ge(piece_used, 2 * i + j + 1)
                    z_tile(4 * i + 2 * j + 1, 1)
                    split(2 * i + j + 2, j, PW, 16 * i + 32)

            for j in range(2):
                ac.wait_ge(z_even, j + 1)
                ac.activation(z[:, 2 * j, :].rearrange("p (h c) -> p h c", h=2), pair(0), ACT.Copy).then_inc(z_out, 1)
                ac.wait_ge(piece_used, j + 1)
                ac.activation(z[:, 2 * j + 1, :].rearrange("p (h c) -> p h c", h=2), pair(1), ACT.Copy).then_inc(z_out, 1)
                split(j + 2, j, PW, 32)
            ac.wait_ge(st_ps, 1)
            ac.activation(pext[:, :, :, :].rearrange("p g b r -> p (g b) r")[:, :, 0:PST],
                          ps[:, 7, 0:4 * NS * PST].rearrange("p (g r) -> p g r", r=PST), ACT.Copy).then_inc(st_out, 1)
            with ac.Fori(1, ZP // 2) as i:
                z_pair(i)

            def mixed(g):
                ac.wait_ge(mix_ps, g + 1)
                ac.activation(halves(obhi[:, g, :]), pair(g % 2), ACT.Identity,
                              scale=prm[:, Q_PSC + g:Q_PSC + g + 1]).then_inc(mix_hi, 1)

            def memt(k):
                ac.wait_ge(xt_ps, KD + 2 + k)
                ac.activation(mthi[:, 2 * k:2 * k + 2, :], ps[:, 4 + k % 2, :].rearrange("p (k m) -> p k m", k=2),
                              ACT.Copy).then_inc(xt_hi, 1)

            ac.wait_ge(con_in, 64)
            for k in range(4):
                memt(k)
            for k in range(4):
                mixed(k)
            ac.wait_ge(z_sent, 16 * (NOVER + 1))
            for k in range(2):
                ac.wait_ge(v_ps, k + 1)
                ac.activation(v[:, 2 * k:2 * k + 2, :], ps[:, 4 + k, :].rearrange("p (b d) -> p b d", b=2),
                              ACT.Copy).then_inc(v_out, 1)
            ac.wait_ge(piece_used, N_V + 1)
            ac.activation(v[0:NS, NB, :], ps[0:NS, 6, 0:256], ACT.Copy).then_inc(v_out, 1)
            split(N_M + 1, 0, PW, 16 * ((N_M + 1) // 2 + 1))
            ac.wait_ge(row_ps, 2)
            ac.activation(kvrow[:, 0:256], ps[:, 6, 0:256], ACT.Copy).then_inc(row_out, 1)
            ac.activation(kvrow[0:NS, 256:512], ps[0:NS, 6, 256:512], ACT.Copy).then_inc(row_out, 1)
            ac.wait_ge(piece_used, N_M + 2)
            for m in range(2):
                ac.activation(mkv[:, m, :], ps[:, (7, 4)[m], :], ACT.Copy).then_inc(mkv_out, 1)
            ac.wait_ge(mkt_ps, 1)
            ac.wait_ge(pads, 4)
            for r, dst in ((0, mkt), (64, mkodd)):
                ac.activation(dst[r:r + 64, :, :], ps[r:r + 64, 5, :].rearrange("p (t m) -> p t m", t=2), ACT.Copy)\
                  .then_inc(mkt_out, 1)
            ac.wait_ge(row_ps, 3)
            ac.activation(urow[0:PST + NS, :], ps[0:PST + NS, 7, :], ACT.Copy).then_inc(row_out, 1)

            def exps(g):
                kind, b, h = groups[g]
                s, w = g % 2, P if kind == "swa" and b == 0 else 2 * P
                ac.wait_ge(sc_neg, g + 1)
                for j in range(GRP):
                    last = ac.activation(probs[s][:, j, 0:w], probs[s][:, j, 0:w], ACT.Exp, bias=stat[:, s, 1, j:j + 1],
                                         accum_out=stat[:, s, 3, j:j + 1])
                if kind == "swa":
                    ac.wait_ge(sc_snk, g + 1)
                    last = ac.activation(stat[:, s, 4, :], stat[:, s, 2, :], ACT.Exp)
                last.then_inc(sc_exp, 1)

            def quadrants(dst, src):
                for r in range(2):
                    last = ac.activation(dst[64 * r:64 * r + 64], src[64 * r:64 * r + 64, r], ACT.Copy)
                return last

            def sample(i):
                if i == S_T1:
                    ac.wait_ge(rows_sent, 64)
                    ac.wait_ge(sw_dve, 7)
                    ac.activation(srow[:, 0:WIN + 1], srow[:, 0:WIN + 1], ACT.Exp, bias=sstat[:, 1:2],
                                  accum_out=sstat[:, 3:4])
                    ac.activation(sstat[:, 4:5], sstat[:, 2:3], ACT.Exp).then_inc(sw_act, 1)
                if i == S_T2:
                    ac.wait_ge(sw_ps, 3)
                    ac.activation(pcol[:, :], ps[:, 7, 0:P], ACT.Copy)
                    ac.activation(pnew[0:NS, :], ps[0:NS, 7, P:2 * P], ACT.Copy).then_inc(sw_act, 1)
                if i == S_PV:
                    ac.wait_ge(sw_ps, 4)
                    quadrants(oahi[:, :, SEQ:T].rearrange("q (p j) b -> q p j b", p=2),
                              ps[:, 7, 3 * P:4 * P].rearrange("q (p a b j) -> q a p j b", p=2, a=2, b=NS))\
                        .then_inc(sw_act, 1)
                if i == M_T1:
                    ac.wait_ge(sm_dve, 2)
                    ac.activation(srow[0:32, 0:NMEM], ps[0:32, 3, P:P + NMEM], ACT.Exp, bias=sstat[0:32, 1:2],
                                  scale=SCALE, accum_out=sstat[0:32, 3:4]).then_inc(sm_act, 1)
                if i == M_T2:
                    ac.wait_ge(sm_ps, 2)
                    ac.activation(pcol[:, 0:64], ps[:, 3, 3 * P:3 * P + 64], ACT.Copy).then_inc(sm_act, 1)
                if i == M_PV:
                    ac.wait_ge(sm_ps, 3)
                    quadrants(ochi[:, :, SEQ:T], ps[:, 3, 3 * P + 64:3 * P + 96].rearrange("q (t a b) -> q a t b", t=2, a=2))\
                        .then_inc(sm_act, 1)
                if M_PV < i <= M_PV + 2:
                    n = N_G + i - M_PV - 1
                    split(n, n % 2, MPW, 16 * (n // 2 + 1))
                if i < NKT:
                    ac.wait_ge(kt_ps, i + 1)
                    if i:
                        ac.wait_ge(ks_ps, i)
                    ac.activation(kt[:, :], ps[:, 2, :], ACT.Copy).then_inc(kt_ok, 1)
                if i == 4:
                    ac.wait_ge(rows_sent, 64)
                    ac.wait_ge(sw_ps, 1)
                    ac.activation(scol[:, :], ps[:, 7, 0:P + NS], ACT.Copy).then_inc(sw_act, 1)
                if i == NKT:
                    ac.wait_ge(ks_ps, NKT)
                    ac.activation(scol[:, 0:64], ps[:, 3, 0:64], ACT.Copy).then_inc(sm_act, 1)

            exps(0)
            for g, (kind, b, h) in enumerate(groups):
                ac.wait_ge(pt_ps, g + 1)
                if g:
                    ac.wait_ge(o_ps, g)
                n = 256 if kind == "swa" and b == 0 else 512
                ac.activation(pt[:, 0, 0:n], ps[:, 4, 0:n], ACT.Copy).then_inc(pt_act, 1)
                if g + 1 < NGR:
                    exps(g + 1)
                ac.wait_ge(o_ps, g + 1)
                if kind == "swa":
                    r, p = 64 * (h % 2), h // 2
                    ac.activation(oahi[r:r + 64, 4 * p:4 * p + 4, b * P:b * P + P],
                                  ps[r:r + 64, 6, :].rearrange("p (j q) -> p j q", j=4), ACT.Copy).then_inc(o_hi, 1)
                else:
                    quadrants(ochi[:, :, b * P:b * P + P],
                              ps[:, 6, :].rearrange("p (a t q) -> p a t q", a=2, t=2)).then_inc(o_hi, 1)
                sample(g)

            def merge(i, more):
                for s in range(3):
                    ac.wait_ge(prod_ps, 5 * i + s + 1)
                    ac.activation(halves(gate[s][:, :]), pair(s), ACT.Sigmoid).then_inc(gate_out, 1)
                    if s == 1 and more:
                        split(2 * i + N_G + 2, N_G % 2, MPW, 16 * i + 16 * ((N_G + 2) // 2 + 1))
                if more:
                    split(2 * i + N_G + 3, (N_G + 1) % 2, MPW, 16 * i + 16 * ((N_G + 3) // 2 + 1))
                ac.wait_ge(m_val, i + 1)
                ac.activation(mhi[:, bass.ds(i, 1), :].rearrange("p a c -> p (a c)"), mval[:, :], ACT.Copy)\
                  .then_inc(m_hi, 1)

            with ac.Fori(0, KD - 1) as i:
                merge(i, True)
            merge(KD - 1, False)
            ac.wait_ge(piece_used, N_O)
            for j in range(4):
                n = N_O + j
                split(n, n % 2, PW, 16 * (n // 2 + 1), True,
                      out=wohi[:, 2 * j:2 * j + 2, :].rearrange("p k n -> p (k n)"))
            for t in range(TT):
                ac.wait_ge(h_stat, 10 * t + 4)
                ac.activation(lstat[0:TR, 15:16], lstat[0:TR, 14:15], ACT.Sqrt).then_inc(sq_out, 1)
                ac.wait_ge(h_stat, 10 * t + 9)
                ac.activation(hall[:, t, :], hall[:, t, :], ACT.Identity, bias=lstat[0:TR, 20:21],
                              scale=lstat[0:TR, 18:19]).then_inc(h_nrm, 1)
                ac.wait_ge(ht_ps, t + 1)
                if t:
                    ac.wait_ge(lg_ps, t)
                ac.activation(ht[:, :, :].rearrange("p (a k) c -> p a (k c)", a=2), ps[:, 4:6, 0:4 * TR], ACT.Copy)\
                  .then_inc(ht_out, 1)

            def esplit(n, s, arrived, first=False):
                ac.wait_ge(eraw_in[s], arrived)
                if not first:
                    ac.wait_ge(e_used, n - 2)
                ac.activation(ehi[s % 3][:, :], eraw[s][:, :], ACT.Copy).then_inc(ehi_ok, 1)

            def xet(c):
                ac.wait_ge(xet_ps, c + 1)
                ac.activation(xethi[:, :, :].rearrange("p (a k) c -> p a (k c)", a=2), ps[:, 4:6, :], ACT.Copy)\
                  .then_inc(xet_hi, 1)

            def gated(c, ready):
                ac.wait_ge(e_used, ready)
                ac.activation(sig[:, :], ps[:, 0, :], ACT.Sigmoid).then_inc(sig_ok, 1)

            def hidt(c):
                ac.wait_ge(hidt_ps, c + 1)
                ac.activation(hthi[:, :, :].rearrange("p j c -> p (j c)"), ps[:, 6, :], ACT.Copy).then_inc(hidt_hi, 1)

            def y_copy(c, ready, first=False):
                ac.wait_ge(e_used, ready)
                if not first:
                    ac.wait_ge(y_sent, 16 * c)
                ac.activation(yout[:, :].rearrange("p (h n) -> p h n", h=2), ps[:, 2:4, :], ACT.Copy).then_inc(y_out, 1)

            def y_send(c):
                ac.wait_ge(y_out, c + 1)
                ac.dma_start(y_dram[bass.ds(c * CAP, CAP), :], yout[:, :]).then_inc(y_sent, 16)

            def expert(e, y=True, more=True):
                esplit(6 * e, 0, 16 * e + 16)
                if y:
                    y_copy(e - 2, 6 * e - 2, y == "first")
                esplit(6 * e + 1, 1, 16 * e + 16)
                if y:
                    y_send(e - 2)
                gated(e, 6 * e)
                hidt(e - 1)
                esplit(6 * e + 2, 2, 16 * e + 16)
                esplit(6 * e + 3, 3, 16 * e + 16)
                if more:
                    xet(e + 1)
                esplit(6 * e + 4, 4, 16 * e + 16)
                esplit(6 * e + 5, 5, 16 * e + 16)

            ac.wait_ge(h_ps, TT)
            for n in range(3):
                esplit(n, n, 16, True)
            ac.wait_ge(rd, 3)
            ac.activation(gd[:, :, :], gd[:, :, :], ACT.Exp).then_inc(r_exp, 1)
            ac.wait_ge(rd, R_DD)
            ac.activation(m2[:, :], m2[:, :], ACT.Exp).then_inc(r_exp, 1)
            xet(0)
            esplit(3, 3, 16)
            gated(0, 2)
            esplit(4, 4, 16)
            esplit(5, 5, 16)
            xet(1)
            expert(1, False)
            expert(2, "first")
            with ac.Fori(3, NE - 1) as e:
                expert(e)
            expert(NE - 1, True, False)
            y_copy(NE - 2, 6 * NE - 2)
            y_send(NE - 2)
            hidt(NE - 1)
            y_copy(NE - 1, 6 * NE)
            y_send(NE - 1)
            ac.wait_ge(y_sent, 16 * NE)
            n_over = ac.value_load(ove[0:1, 8:9], min_val=0, max_val=NOVER)
            with ac.Fori(0, NOVER) as j:
                with ac.If(j < n_over):
                    n, c = 6 * j + 6 * NE, j + NE
                    xet(c)
                    for k in range(4):
                        esplit(n + k, k, 16 * c + 16)
                    gated(c, n + 2)
                    esplit(n + 4, 4, 16 * c + 16)
                    esplit(n + 5, 5, 16 * c + 16)
                    hidt(c)
                    y_copy(c, n + 6)
                    y_send(c)
            ac.wait_ge(y_sent, 16 * n_over + 16 * NE)
            ac.sem_inc(moe_done, 1)
            for t in range(TT):
                ac.wait_ge(f_stat, 10 * t + 4)
                ac.activation(lstat[0:TR, 15:16], lstat[0:TR, 14:15], ACT.Sqrt).then_inc(sq_out, 1)
                ac.wait_ge(f_stat, 10 * t + 9)
                ac.activation(res[t % 2][:, :], res[t % 2][:, :], ACT.Identity, bias=lstat[0:TR, 20:21],
                              scale=lstat[0:TR, 18:19]).then_inc(f_nrm, 1)

        @block.tensor
        def _(pe):
            pe.wait_ge(id_in, 16)
            pe.wait_ge(x_in, 16 * (NB + 1))
            for k in range(KD):
                if k >= 2:
                    pe.wait_ge(xt_hi, k - 1)
                    pe.wait_ge(xt_lo, k - 1)
                for t in range(NB):
                    last = pe.transpose(ps[:, 4 + k % 2, t * P:t * P + P], xtok[:, t, k * P:k * P + P], ident)
                last.then_inc(xt_ps, 1)
            for k in range(KD):
                last = pe.transpose(ps[:, 6, k * NS:k * NS + NS], xsam[:, k * P:k * P + P], ident[0:NS, 0:NS])
            last.then_inc(xt_ps, 1)

            def product(outs, parts, start=True, stop=True):
                for n, out in enumerate(outs):
                    for k, (sh, sl, mh, ml) in enumerate(parts):
                        pe.matmul(out, sh, mh[n], start=start and k == 0, stop=False)
                        pe.matmul(out, sl, mh[n], start=False, stop=False)
                        last = pe.matmul(out, sh, ml[n], start=False, stop=stop and k == len(parts) - 1)
                return last

            def cols(w, n):
                return w[:, n * P:n * P + P]

            def by_half(ap):
                return [ap[:, 0:TH], ap[:, TH:T]]

            def tokens(s):
                return [ps[:, 2 * s + h, 0:TH] for h in range(2)]

            def xk(t, k):
                return by_half(t[:, k * T:k * T + T])

            pe.wait_ge(xt_hi, KD + 1)
            pe.wait_ge(xt_lo, KD + 1)

            def z_piece(n, s, first=False):
                pe.wait_ge(lo_split, n + 1)
                for u in range(2):
                    if not first:
                        pe.wait_ge(z_out, 2 * n + u - 1)
                    last = product(tokens(u), [(cols(whi[s], 8 * u + k), cols(wlo[s], 8 * u + k), xk(xhi, k), xk(xlo, k))
                                               for k in range(KD)])
                    last.then_inc(piece_used if u else z_even, 1)

            z_piece(0, 0, True)
            z_piece(1, 1)
            pe.wait_ge(st_in, 16)
            n = NS * PST
            for g in range(4):
                last = pe.transpose(ps[:, 7, g * n:g * n + n], pstate[:, g * P:g * P + P], ident[0:n, 0:n])
            last.then_inc(st_ps, 1)
            with pe.Fori(1, ZP // 2) as i:
                for j in range(2):
                    z_piece(2 * i + j, j)
            pe.wait_ge(m_in, 16)
            for g in range(4):
                if g >= 2:
                    pe.wait_ge(xt_hi, KD + g)
                    pe.wait_ge(xt_lo, KD + g)
                for u in range(4):
                    last = pe.transpose(ps[:, 4 + g % 2, u * P:u * P + P],
                                        mtok[:, u % 2, (2 * g + u // 2) * P:(2 * g + u // 2) * P + P], ident)
                last.then_inc(xt_ps, 1)
            pe.wait_ge(con_in, 64)
            for g in range(4):
                pe.wait_ge(pooled_in, g + 1)
                if g < 2:
                    pe.wait_ge(z_out, ZT - 1 + g)
                else:
                    pe.wait_ge(mix_hi, g - 1)
                    pe.wait_ge(mix_lo, g - 1)
                for h in range(2):
                    last = pe.matmul(ps[:, 2 * (g % 2) + h, 0:TH], wmix[:, g, :],
                                     pooled[:, g, h * TH:h * TH + TH], start=True, stop=True)
                last.then_inc(mix_ps, 1)

            def rotate(r):
                if r < 2:
                    pe.wait_ge(mix_hi, r + 3)
                    pe.wait_ge(mix_lo, r + 3)
                else:
                    pe.wait_ge(rot_mul, r - 1)
                for h in range(2):
                    last = pe.matmul(ps[:, 2 * (r % 2) + h, 0:TH], con[:, C_ROT:C_ROT + P],
                                     z[:, ROT[r], h * TH:h * TH + TH], start=True, stop=True)
                last.then_inc(rot_ps, 1)

            pe.wait_ge(xt_hi, KD + 5)
            pe.wait_ge(xt_lo, KD + 5)
            pe.wait_ge(pad_zero, 2)
            pe.wait_ge(lo_split, N_V + 1)
            for b in range(NB + 1):
                out = ps[:, 4 + b // 2, (b % 2) * 256:(b % 2) * 256 + 256]
                last = product([out], [(xhi[:, k * T + b * P:k * T + b * P + P], xlo[:, k * T + b * P:k * T + b * P + P],
                                        [whi[0][:, k * 256:k * 256 + 256]], [wlo[0][:, k * 256:k * 256 + 256]])
                                       for k in range(KD)])
                if b % 2:
                    last.then_inc(v_ps, 1)
                if b == NB:
                    last.then_inc(piece_used, 1)
                rotate(b)
            pe.wait_ge(roped, 2)
            pe.wait_ge(v_out, 3)
            for p in range(2):
                last = pe.transpose(ps[:, 6, p * P:p * P + P], z[:, ZK + p, SEQ - P:SEQ], ident)
            last.then_inc(row_ps, 1)
            for p in range(2):
                last = pe.transpose(ps[0:NS, 6, 256 + p * P:256 + p * P + P], z[:, ZK + p, SEQ:T], ident)
            last.then_inc(row_ps, 1)
            pe.wait_ge(st_out, 1)
            for j in range(2):
                n = N_M + j
                pe.wait_ge(lo_split, n + 1)
                for m in range(2):
                    last = product([ps[:, (7, 4)[m], :]],
                                   [(mthi[:, 4 * j + k, m * P:m * P + P], mtlo[:, 4 * j + k, m * P:m * P + P],
                                     [whi[n % 2][:, k * 512:k * 512 + 512]], [wlo[n % 2][:, k * 512:k * 512 + 512]])
                                    for k in range(4)], start=j == 0, stop=j == 1)
                    if m == 1:
                        last.then_inc(piece_used, 1)
                    rotate(NB + 1 + 2 * j + m)
            rotate(9)
            pe.wait_ge(mkv_out, 2)
            for t in range(2):
                for m in range(2):
                    last = pe.transpose(ps[:, 5, t * 256 + m * P:t * 256 + m * P + P], mkv[:, m, t * P:t * P + P], ident)
            last.then_inc(mkt_ps, 1)
            for g in range(4):
                last = pe.transpose(ps[0:PST + NS, 7, g * P:g * P + P], z[:, ZU + g, SEQ - PST:T], ident)
            last.then_inc(row_ps, 1)

            def scores(g):
                kind, b, h = groups[g]
                if g:
                    pe.wait_ge(sc_row, g)
                for j in range(GRP):
                    if kind == "swa":
                        p = h // 2
                        k0, w = (0, P) if b == 0 else ((b - 1) * P, 2 * P)
                        q = z[:, ZQ + 4 * p + j, b * P:b * P + P]
                        k = (kodd[:, p, k0:k0 + w] if h % 2 else z[:, ZK + p, k0:k0 + w])
                    else:
                        m, w = MEM_ORDER[j], NMEM
                        q, k = z[:, ZC + m // 2, b * P:b * P + P], (mkodd if m % 2 else mkt)[:, m // 2, :]
                    last = pe.matmul(ps[:, j // 2, (j % 2) * 256:(j % 2) * 256 + w], q, k, start=True, stop=True)
                last.then_inc(sc_ps, 1)

            def sample_keys(n):
                if n == 0:
                    pe.wait_ge(win_in, 16)
                else:
                    pe.wait_ge(kt_ok, n)
                b = n - 4
                if b >= 0:
                    pe.wait_ge(cm_in[b // 4], 32)
                for u in range(4):
                    src = cach_k[:, 2 * n + u // 2] if b < 0 else cm_k[b // 4][:, 2 * (b % 4) + u // 2]
                    last = pe.transpose(ps[:, 2, u * P:u * P + P], src[:, (u % 2) * P:(u % 2) * P + P], ident)
                last.then_inc(kt_ps, 1)

            def sample_scores(n):
                pe.wait_ge(kt_ok, n + 1)
                if n == 0:
                    pe.wait_ge(qs_ok, 3)
                for u in range(4):
                    if n < 4:
                        b, p = 2 * n + u // 2, u % 2
                        out = ps[:, 7, 64 * p:64 * p + 64].rearrange("q (a b j) -> q a b j", a=2, b=NS)[:, :, b, :]
                        last = pe.matmul(out, kt[:, u * P:u * P + P], qsp[:, p, :, b, :], start=True, stop=True)
                    else:
                        b, k, t = n - 4, u // 2, u % 2
                        out = ps[:, 3, 32 * k + 16 * t:32 * k + 16 * t + 16].rearrange("q (a b) -> q a b", a=2)[:, :, b]
                        last = pe.matmul(out, kt[:, u * P:u * P + P], cqp[:, t, :, b], start=True, stop=True)
                last.then_inc(ks_ps, 1)

            def sample(i):
                if 1 <= i <= NKT:
                    sample_scores(i - 1)
                if i == 4:
                    for p in range(2):
                        last = pe.matmul(ps[64 * p:64 * p + 64, 7, P:P + NS],
                                         qsp[:, p, :, :, :].rearrange("q a b j -> q (a b j)"), kns[:, p, :],
                                         start=True, stop=True)
                    last.then_inc(sw_ps, 1)
                if i == S_T1:
                    pe.wait_ge(sw_act, 1)
                    pe.transpose(ps[:, 7, 2 * P:3 * P], scol[:, 0:P], ident).then_inc(sw_ps, 1)
                if i == S_T2:
                    pe.wait_ge(sw_dve, 11)
                    pe.transpose(ps[:, 7, 0:P], srow[:, 0:P], ident)
                    pe.transpose(ps[0:NS, 7, P:2 * P], sstat[:, 8:16], ident).then_inc(sw_ps, 1)
                if i == S_PV:
                    pe.wait_ge(sw_act, 3)
                    pe.wait_ge(winv_in, 16)
                    for p in range(2):
                        out = ps[:, 7, 3 * P + 64 * p:3 * P + 64 * p + 64]
                        pe.matmul(out, v[0:NS, NB, p * P:p * P + P], pnew[0:NS, 64 * p:64 * p + 64],
                                  start=p == 0, stop=False, skip_group_check=True)
                    for p in range(2):
                        out = ps[:, 7, 3 * P + 64 * p:3 * P + 64 * p + 64].rearrange("q (a b j) -> q a b j", a=2, b=NS)
                        prob = pcol[:, 64 * p:64 * p + 64].rearrange("q (a b j) -> q a b j", a=2, b=NS)
                        for b in range(NS):
                            last = pe.matmul(out[:, :, b, :], cach_v[:, b, p * P:p * P + P], prob[:, :, b, :],
                                             start=False, stop=b == NS - 1, skip_group_check=True)
                    last.then_inc(sw_ps, 1)
                if i == M_T1:
                    pe.wait_ge(sm_act, 1)
                    for k in range(2):
                        last = pe.transpose(ps[0:32, 3, P + k * P:2 * P + k * P], scol[:, 32 * k:32 * k + 32], ident)
                    last.then_inc(sm_ps, 1)
                if i == M_T2:
                    pe.wait_ge(sm_dve, 4)
                    for k in range(2):
                        last = pe.transpose(ps[:, 3, 3 * P + 32 * k:3 * P + 32 * k + 32], srow[0:32, k * P:k * P + P],
                                            ident[0:32, 0:32])
                    last.then_inc(sm_ps, 1)
                if i == M_PV:
                    pe.wait_ge(sm_act, 3)
                    pe.wait_ge(cmv_in, 64)
                    for b in range(NS):
                        for t in range(2):
                            c = 3 * P + 64 + 16 * t
                            for k in range(2):
                                prob = pcol[:, 32 * k + 16 * t:32 * k + 16 * t + 16].rearrange("q (a b) -> q a b", a=2)
                                last = pe.matmul(ps[:, 3, c:c + 16].rearrange("q (a b) -> q a b", a=2)[:, :, b],
                                                 cm_v[b // 4][:, 2 * (b % 4) + k, t * P:t * P + P], prob[:, :, b],
                                                 start=k == 0, stop=k == 1)
                    last.then_inc(sm_ps, 1)
                if i < NKT:
                    sample_keys(i)

            pe.wait_ge(mkt_out, 2)
            pe.wait_ge(row_out, 3)
            pe.wait_ge(roped, 10)
            pe.wait_ge(kodd_ok, 1)
            pe.wait_ge(pads, 5)
            scores(0)
            scores(1)
            for g, (kind, b, h) in enumerate(groups):
                nk = 1 if kind == "swa" and b == 0 else 2
                pe.wait_ge(sc_nrm, g + 1)
                if g:
                    pe.wait_ge(pt_act, g)
                    pe.wait_ge(pt_dve, g)
                for k in range(nk):
                    for j in range(GRP):
                        last = pe.transpose(ps[:, 4 + k, j * P:j * P + P], probs[g % 2][:, j, k * P:k * P + P], ident)
                last.then_inc(pt_ps, 1)
                if g + 2 < NGR:
                    scores(g + 2)
                pe.wait_ge(pt_act, g + 1)
                pe.wait_ge(pt_dve, g + 1)
                if g:
                    pe.wait_ge(o_hi, g)
                    pe.wait_ge(o_lo, g)
                if kind == "swa":
                    for k in range(nk):
                        last = pe.matmul(ps[:, 6, :], v[:, b - nk + 1 + k, (h // 2) * P:(h // 2) * P + P], pt[:, k, :],
                                         start=k == 0, stop=k == nk - 1)
                else:
                    for j, m in enumerate(MEM_ORDER):
                        for k in range(2):
                            last = pe.matmul(ps[:, 6, j * P:j * P + P],
                                             mkv[:, k, 256 + (m // 2) * P:256 + (m // 2) * P + P],
                                             pt[:, k, j * P:j * P + P], start=k == 0, stop=k == 1)
                last.then_inc(o_ps, 1)
                sample(g)

            pe.wait_ge(o_hi, NGR)
            pe.wait_ge(o_lo, NGR)
            pe.wait_ge(sm_act, 4)
            pe.wait_ge(sm_dve, 5)
            A, B = N_G % 2, (N_G + 1) % 2

            def block_of(n):
                return (A, n) if n < MT // 2 else (B, n - MT // 2)

            def merge(i, first=False):
                n = 0
                for u, (hi, lo, nk) in enumerate(((None, None, KD),) * 3 + ((oahi, oalo, 8), (obhi, oblo, 4), (ochi, oclo, 2))):
                    if u == 0:
                        pe.wait_ge(lo_split, 2 * i + N_G + 1)
                        if not first:
                            pe.wait_ge(m_step, 4 * i - 3)
                    if u == 1 and not first:
                        pe.wait_ge(m_step, 4 * i - 1)
                    if u == 2 and not first:
                        pe.wait_ge(m_val, i)
                    if u >= 3:
                        pe.wait_ge(gate_out, 3 * i + u - 2)
                    for half in range(2):
                        for k in range(nk):
                            s, q = block_of(n + k)
                            if s == B and half == 0 and q == 0:
                                pe.wait_ge(lo_split, 2 * i + N_G + 2)
                            if u < 3:
                                mh, ml = xk(xhi, k)[half], xk(xlo, k)[half]
                            else:
                                mh, ml = by_half(hi[:, k, :])[half], by_half(lo[:, k, :])[half]
                            out = ps[:, 2 * (u % 3) + half, 0:TH]
                            pe.matmul(out, cols(whi[s], q), mh, start=k == 0, stop=False)
                            pe.matmul(out, cols(wlo[s], q), mh, start=False, stop=False)
                            last = pe.matmul(out, cols(whi[s], q), ml, start=False, stop=k == nk - 1)
                            if half == 1 and n + k == MT // 2 - 1:
                                last.then_inc(piece_used, 1)
                    last.then_inc(prod_ps if u < 5 else piece_used, 1)
                    n += nk

            merge(0, True)
            with pe.Fori(1, KD) as i:
                merge(i)

            def project(t):
                if t >= 2:
                    pe.wait_ge(h_sum, t - 1)
                for k in range(KD):
                    if t == 0:
                        pe.wait_ge(lo_split, N_O + k // 2 + 1)
                    for h in range(2):
                        out = ps[0:TR, 2 * (t % 2) + h, :]
                        mt = slice(t * TR, t * TR + TR)
                        pe.matmul(out, mhi[:, k, mt], wohi[:, k, h * 512:h * 512 + 512], start=k == 0, stop=False)
                        pe.matmul(out, mlo[:, k, mt], wohi[:, k, h * 512:h * 512 + 512], start=False, stop=False)
                        last = pe.matmul(out, mhi[:, k, mt], wolo[:, k, h * 512:h * 512 + 512], start=False,
                                         stop=k == KD - 1)
                last.then_inc(h_ps, 1)

            def route(t):
                pe.wait_ge(h_done, t + 1)
                if t:
                    pe.wait_ge(ht_out, t)
                for k in range(KD):
                    last = pe.transpose(ps[:, 4 + k // 4, (k % 4) * TR:(k % 4) * TR + TR],
                                        hall[:, t, k * P:k * P + P], ident[0:TR, 0:TR])
                last.then_inc(ht_ps, 1)
                pe.wait_ge(ht_out, t + 1)
                for k in range(KD):
                    last = pe.matmul(ps[0:TR, 6, t * 20:t * 20 + 20], ht[:, k, :], wrt[:, k, :],
                                     start=k == 0, stop=k == KD - 1)
                last.then_inc(lg_ps, 1)

            pe.wait_ge(m_hi, KD)
            pe.wait_ge(m_lo, KD)
            project(0)
            for t in range(TT):
                if t + 1 < TT:
                    project(t + 1)
                route(t)
            pe.wait_ge(both_ok, 1)
            for t in range(TT):
                for u in range(t + 1):
                    pe.matmul(ps[0:TR, 7, t * NE:t * NE + NE], ones[:, 0:TR] if u < t else upper, both[:, u, :],
                              start=u == 0, stop=u == t)
            for u in range(TT):
                last = pe.matmul(ps[:, 7, TT * NE:TT * NE + NE], ones, both[:, u, :], start=u == 0, stop=u == TT - 1)
            last.then_inc(rank_ps, 1)
            pe.wait_ge(slot_in, 16)
            pe.wait_ge(slots_ok, 1)
            n = NE + NOVER
            pe.transpose(ps[:, 6, P:P + n], slrow[:, :], ident[0:n, 0:n]).then_inc(slot_ps, 1)

            def xet(c, first=False):
                pe.wait_ge(xe_in, 16 * c + 16)
                if not first:
                    pe.wait_ge(xet_hi, c)
                    pe.wait_ge(xet_lo, c)
                for k in range(KD):
                    last = pe.transpose(ps[:, 4 + k // 4, (k % 4) * P:(k % 4) * P + P],
                                        xe[:, :].rearrange("p (c k) -> p k c", k=KD)[:, k, :], ident)
                last.then_inc(xet_ps, 1)

            def wide(n, s, bank, first=False, free=None):
                if free is not None:
                    pe.wait_ge(*free)
                for j in range(2):
                    pe.wait_ge(elo_ok, n + j + 1)
                    for q in range(4):
                        k, w = 4 * j + q, slice(q * 512, q * 512 + 512)
                        pe.matmul(ps[:, bank, :], xethi[:, k, :], ehi[s[j]][:, w], start=k == 0, stop=False)
                        pe.matmul(ps[:, bank, :], xetlo[:, k, :], ehi[s[j]][:, w], start=False, stop=False)
                        last = pe.matmul(ps[:, bank, :], xethi[:, k, :], elo[s[j]][:, w], start=False, stop=k == KD - 1)
                    last.then_inc(e_used, 1)

            def hidt(c, first=False):
                pe.wait_ge(hid_ok, c + 1)
                if not first:
                    pe.wait_ge(hidt_hi, c)
                    pe.wait_ge(hidt_lo, c)
                for j in range(4):
                    last = pe.transpose(ps[:, 6, j * P:j * P + P], hid[:, :].rearrange("p (c j) -> p j c", j=4)[:, j, :],
                                        ident)
                last.then_inc(hidt_ps, 1)

            def down(c, n, s, first=False):
                pe.wait_ge(hidt_hi, c + 1)
                pe.wait_ge(hidt_lo, c + 1)
                if not first:
                    pe.wait_ge(y_out, c)
                for j in range(2):
                    pe.wait_ge(elo_ok, n + j + 1)
                    for q in range(2):
                        f = 2 * j + q
                        for h in range(2):
                            w = slice(q * D + h * 512, q * D + h * 512 + 512)
                            pe.matmul(ps[:, 2 + h, :], hthi[:, f, :], ehi[s[j]][:, w], start=f == 0, stop=False)
                            pe.matmul(ps[:, 2 + h, :], htlo[:, f, :], ehi[s[j]][:, w], start=False, stop=False)
                            last = pe.matmul(ps[:, 2 + h, :], hthi[:, f, :], elo[s[j]][:, w], start=False, stop=f == 3)
                    last.then_inc(e_used, 1)

            def expert(e, first=False, more=True):
                pe.wait_ge(xet_hi, e + 1)
                pe.wait_ge(xet_lo, e + 1)
                wide(6 * e - 2, (1, 2), 0, free=(act_ok, e))
                hidt(e - 1, first)
                wide(6 * e, (0, 1), 1, free=(hid_ok, e))
                if more:
                    xet(e + 1)
                down(e - 1, 6 * e + 2, (2, 0), first)

            xet(0, True)
            pe.wait_ge(xet_hi, 1)
            pe.wait_ge(xet_lo, 1)
            wide(0, (0, 1), 0)
            wide(2, (2, 0), 1)
            xet(1)
            expert(1, True)
            with pe.Fori(2, NE - 1) as e:
                expert(e)
            expert(NE - 1, more=False)
            hidt(NE - 1)
            down(NE - 1, 6 * NE - 2, (1, 2))
            n_over = pe.value_load(ove[0:1, 8:9], min_val=0, max_val=NOVER)
            with pe.Fori(0, NOVER) as j:
                with pe.If(j < n_over):
                    n, c = 6 * j + 6 * NE, j + NE
                    xet(c)
                    pe.wait_ge(xet_hi, c + 1)
                    pe.wait_ge(xet_lo, c + 1)
                    wide(n, (0, 1), 0, free=(act_ok, c))
                    wide(n + 2, (2, 0), 1, free=(hid_ok, c))
                    hidt(c)
                    down(c, n + 4, (1, 2))

        @block.vector
        def _(ve):
            for k in range(KD):
                ve.wait_ge(xt_hi, k + 1)
                ve.tensor_tensor(xlo[:, k * T:k * T + SEQ], ps[:, 4 + k % 2, :], xhi[:, k * T:k * T + SEQ].bitcast(F32),
                                 ALU.subtract).then_inc(xt_lo, 1)
            ve.wait_ge(xt_hi, KD + 1)
            ve.tensor_tensor(xlo[:, 0:KD * T].rearrange("p (k t) -> p k t", k=KD)[:, :, SEQ:T],
                             ps[:, 6, 0:KD * NS].rearrange("p (k t) -> p k t", k=KD),
                             xhi[:, 0:KD * T].rearrange("p (k t) -> p k t", k=KD)[:, :, SEQ:T].bitcast(F32),
                             ALU.subtract).then_inc(xt_lo, 1)

            def split(n, s, width, first=False, out=None, hi=None):
                ve.wait_ge(hi_split, n + 1)
                if not first:
                    ve.wait_ge(piece_used, n - 1)
                ve.tensor_tensor(wlo[s][:, 0:width] if out is None else out, raw[s][:, 0:width],
                                 (whi[s][:, 0:width] if hi is None else hi).bitcast(F32), ALU.subtract)\
                  .then_inc(lo_split, 1)

            split(0, 0, PW, True)
            split(1, 1, PW, True)
            with ve.Fori(0, ZP // 2) as i:
                for j in range(2):
                    split(2 * i + j + 2, j, PW)
            ve.wait_ge(con_in, 64)
            ve.tensor_scalar(nsink[:, :], prm[:, 0:17], -1.0, None, ALU.mult).then_inc(prep, 1)
            for k in range(4):
                ve.wait_ge(xt_hi, KD + 2 + k)
                ve.tensor_tensor(mtlo[:, 2 * k:2 * k + 2, :], ps[:, 4 + k % 2, :].rearrange("p (k m) -> p k m", k=2),
                                 mthi[:, 2 * k:2 * k + 2, :].bitcast(F32), ALU.subtract).then_inc(xt_lo, 1)
            for k in range(4):
                ve.wait_ge(mix_hi, k + 1)
                ve.scalar_tensor_tensor(halves(oblo[:, k, :]), pair(k % 2), prm[:, Q_PSC + k:Q_PSC + k + 1],
                                        halves(obhi[:, k, :].bitcast(F32)), ALU.mult, ALU.subtract).then_inc(mix_lo, 1)

            for r, t in enumerate(ROT):
                s = r % 2
                ve.wait_ge(rot_ps, r + 1)
                ve.tensor_tensor(halves(rtmp[s][:, :]), pair(s), halves(con[:, C_SIN:C_SIN + T]), ALU.mult)\
                  .then_inc(rot_mul, 1)
                ve.wait_ge(rot_mul, r + 1)
                ve.wait_ge(rot_cos, r + 1)
                ve.tensor_tensor(z[:, t, :], z[:, t, :], rtmp[s][:, :], ALU.add).then_inc(roped, 1)
                if r == 4:
                    split(N_M + 1, 0, PW)
                if r == 5:
                    ve.wait_ge(roped, 2)
                    ve.wait_ge(pads, 2)
                    ve.tensor_copy(kodd[64:P, :, :], z[64:P, ZK:ZK + 2, :]).then_inc(kodd_ok, 1)
                    ve.tensor_copy(kns[:, :, :], z[:, ZK:ZK + 2, SEQ:T]).then_inc(qs_ok, 1)
            ve.wait_ge(roped, 10)
            for r in range(2):
                last = ve.tensor_copy(qsp[64 * r:64 * r + 64, :, r, :, :],
                                      z[64 * r:64 * r + 64, ZQ:ZQ + 8, SEQ:T].rearrange("q (p j) b -> q p b j", p=2))
            last.then_inc(qs_ok, 1)
            for r in range(2):
                last = ve.tensor_copy(cqp[64 * r:64 * r + 64, :, r, :], z[64 * r:64 * r + 64, ZC:ZC + 2, SEQ:T])
            last.then_inc(qs_ok, 1)
            ve.wait_ge(prep, 1)

            def scaled(g):
                kind, b, h = groups[g]
                s = g % 2
                src = ps[:, 0:2, :].rearrange("p a (j w) -> p (a j) w", j=2)
                ve.wait_ge(sc_ps, g + 1)
                if kind == "swa":
                    w = P if b == 0 else 2 * P
                    mask = con[:, C_MASK + 2 * P - w:C_MASK + 2 * P].rearrange("p (a w) -> p a w", a=1)
                    ve.scalar_tensor_tensor(probs[s][:, :, 0:w], src[:, :, 0:w], SCALE, mask.broadcast_to([P, GRP, w]),
                                            ALU.mult, ALU.add).then_inc(sc_row, 1)
                else:
                    ve.tensor_scalar(probs[s][:, :, :], src, SCALE, None, ALU.mult).then_inc(sc_row, 1)

            def row_max(g):
                kind, b, h = groups[g]
                s = g % 2
                st = stat[:, s]
                w = P if kind == "swa" and b == 0 else 2 * P
                ve.wait_ge(sc_row, g + 1)
                ve.tensor_reduce(st[:, 0, :], probs[s][:, :, 0:w], AX.X, ALU.max).then_inc(sc_max, 1)
                ve.wait_ge(sc_max, g + 1)
                if kind == "swa":
                    ve.scalar_tensor_tensor(st[:, 1, :], st[:, 0, :], -1.0, nsink[:, 4 * h:4 * h + 4], ALU.mult,
                                            ALU.min).then_inc(sc_neg, 1)
                    ve.wait_ge(sc_neg, g + 1)
                    ve.tensor_tensor(st[:, 2, :], st[:, 1, :], prm[:, 4 * h:4 * h + 4], ALU.add).then_inc(sc_snk, 1)
                else:
                    ve.tensor_scalar(st[:, 1, :], st[:, 0, :], -1.0, None, ALU.mult).then_inc(sc_neg, 1)

            def inverse(g):
                st = stat[:, g % 2]
                ve.wait_ge(sc_exp, g + 1)
                den = 3
                if groups[g][0] == "swa":
                    ve.tensor_tensor(st[:, 5, :], st[:, 3, :], st[:, 4, :], ALU.add).then_inc(sc_den, 1)
                    ve.wait_ge(sc_den, g + 1)
                    den = 5
                ve.reciprocal(st[:, 6, :], st[:, den, :]).then_inc(sc_rec, 1)

            def rest(g):
                kind, b, h = groups[g]
                ve.wait_ge(o_hi, g + 1)
                if kind == "swa":
                    r, p = 64 * (h % 2), h // 2
                    dst = (slice(r, r + 64), slice(4 * p, 4 * p + 4), slice(b * P, b * P + P))
                    ve.tensor_tensor(oalo[dst], ps[r:r + 64, 6, :].rearrange("p (j q) -> p j q", j=4),
                                     oahi[dst].bitcast(F32), ALU.subtract).then_inc(o_lo, 1)
                else:
                    dst = (slice(0, P), slice(0, 2), slice(b * P, b * P + P))
                    quadrants(oclo[dst], ps[:, 6, :].rearrange("p (a t q) -> p a t q", a=2, t=2), ochi[dst])\
                        .then_inc(o_lo, 1)

            def quadrants(dst, src, head):
                for r in range(2):
                    rows = slice(64 * r, 64 * r + 64)
                    last = ve.tensor_tensor(dst[rows], src[rows, r], head[rows].bitcast(F32), ALU.subtract)
                return last

            def sample(i):
                if i == 4:
                    ve.wait_ge(sw_act, 1)
                    ve.tensor_tensor(sstat[:, 8:16], scol[:, P:P + NS], con[:, C_BM:C_BM + NS], ALU.mult)\
                      .then_inc(sw_dve, 1)
                    ve.wait_ge(sw_dve, 1)
                    ve.tensor_reduce(sstat[:, 5:6], sstat[:, 8:16], AX.X, ALU.add).then_inc(sw_dve, 1)
                    ve.wait_ge(sw_dve, 2)
                    ve.tensor_scalar(srow[:, P:P + 1], sstat[:, 5:6], SCALE, None, ALU.mult).then_inc(sw_dve, 1)
                if i == S_T1:
                    ve.wait_ge(sw_ps, 2)
                    ve.tensor_scalar(srow[:, 0:P], ps[:, 7, 2 * P:3 * P], SCALE, None, ALU.mult).then_inc(sw_dve, 1)
                    ve.wait_ge(sw_dve, 4)
                    ve.tensor_reduce(sstat[:, 0:1], srow[:, 0:WIN + 1], AX.X, ALU.max).then_inc(sw_dve, 1)
                    ve.wait_ge(sw_dve, 5)
                    ve.scalar_tensor_tensor(sstat[:, 1:2], sstat[:, 0:1], -1.0, nsink[:, 16:17], ALU.mult, ALU.min)\
                      .then_inc(sw_dve, 1)
                    ve.wait_ge(sw_dve, 6)
                    ve.tensor_tensor(sstat[:, 2:3], sstat[:, 1:2], prm[:, Q_SINKR:Q_SINKR + 1], ALU.add)\
                      .then_inc(sw_dve, 1)
                if i == S_T1 + 1:
                    ve.wait_ge(sw_act, 2)
                    ve.tensor_tensor(sstat[:, 5:6], sstat[:, 3:4], sstat[:, 4:5], ALU.add).then_inc(sw_dve, 1)
                    ve.wait_ge(sw_dve, 8)
                    ve.reciprocal(sstat[:, 6:7], sstat[:, 5:6]).then_inc(sw_dve, 1)
                    ve.wait_ge(sw_dve, 9)
                    ve.tensor_scalar(srow[:, 0:WIN + 1], srow[:, 0:WIN + 1], sstat[:, 6:7], None, ALU.mult)\
                      .then_inc(sw_dve, 1)
                    ve.wait_ge(sw_dve, 10)
                    ve.tensor_scalar(sstat[:, 8:16], con[:, C_BM:C_BM + NS], srow[:, P:P + 1], None, ALU.mult)\
                      .then_inc(sw_dve, 1)
                if i == S_PV:
                    ve.wait_ge(sw_act, 4)
                    quadrants(oalo[:, :, SEQ:T].rearrange("q (p j) b -> q p j b", p=2),
                              ps[:, 7, 3 * P:4 * P].rearrange("q (p a b j) -> q a p j b", p=2, a=2, b=NS),
                              oahi[:, :, SEQ:T].rearrange("q (p j) b -> q p j b", p=2)).then_inc(sw_dve, 1)
                if i == M_T1:
                    ve.wait_ge(sm_ps, 1)
                    ve.tensor_reduce(sstat[0:32, 0:1], ps[0:32, 3, P:P + NMEM], AX.X, ALU.max).then_inc(sm_dve, 1)
                    ve.wait_ge(sm_dve, 1)
                    ve.tensor_scalar(sstat[0:32, 1:2], sstat[0:32, 0:1], -SCALE, None, ALU.mult).then_inc(sm_dve, 1)
                if i == M_T1 + 1:
                    ve.wait_ge(sm_act, 2)
                    ve.reciprocal(sstat[0:32, 6:7], sstat[0:32, 3:4]).then_inc(sm_dve, 1)
                    ve.wait_ge(sm_dve, 3)
                    ve.tensor_scalar(srow[0:32, 0:NMEM], srow[0:32, 0:NMEM], sstat[0:32, 6:7], None, ALU.mult)\
                      .then_inc(sm_dve, 1)
                if i == M_PV:
                    ve.wait_ge(sm_act, 4)
                    quadrants(oclo[:, :, SEQ:T],
                              ps[:, 3, 3 * P + 64:3 * P + 96].rearrange("q (t a b) -> q a t b", t=2, a=2),
                              ochi[:, :, SEQ:T]).then_inc(sm_dve, 1)
                if M_PV < i <= M_PV + 2:
                    n = N_G + i - M_PV - 1
                    split(n, n % 2, MPW)

            scaled(0)
            row_max(0)
            scaled(1)
            inverse(0)
            row_max(1)
            for g, (kind, b, h) in enumerate(groups):
                ve.wait_ge(pt_ps, g + 1)
                if g:
                    ve.wait_ge(o_ps, g)
                if kind == "swa" and b == 0:
                    ve.wait_ge(pt_act, g + 1)
                    ve.tensor_copy(pt[:, 0, 256:512], ps[:, 4, 256:512]).then_inc(pt_dve, 1)
                else:
                    ve.tensor_copy(pt[:, 1, :], ps[:, 5, :]).then_inc(pt_dve, 1)
                if g:
                    rest(g - 1)
                if g + 2 < NGR:
                    scaled(g + 2)
                if g + 1 < NGR:
                    inverse(g + 1)
                if g + 2 < NGR:
                    row_max(g + 2)
                sample(g)
            rest(NGR - 1)

            def merge(i, more, first=False):
                if more:
                    split(2 * i + N_G + 2, N_G % 2, MPW)
                if not first:
                    ve.wait_ge(m_lo, i)
                ve.wait_ge(prod_ps, 5 * i + 4)
                ve.tensor_tensor(halves(mval[:, :]), pair(0), halves(gate[0][:, :]), ALU.mult).then_inc(m_step, 1)
                ve.wait_ge(prod_ps, 5 * i + 5)
                ve.tensor_tensor(halves(gate[1][:, :]), pair(1), halves(gate[1][:, :]), ALU.mult).then_inc(m_step, 1)
                ve.wait_ge(m_step, 4 * i + 2)
                ve.tensor_tensor(mval[:, :], mval[:, :], gate[1][:, :], ALU.add).then_inc(m_step, 1)
                ve.wait_ge(piece_used, 2 * i + N_G + 2)
                ve.wait_ge(gate_out, 3 * i + 3)
                ve.tensor_tensor(halves(gate[2][:, :]), pair(2), halves(gate[2][:, :]), ALU.mult).then_inc(m_step, 1)
                ve.wait_ge(m_step, 4 * i + 4)
                ve.tensor_tensor(mval[:, :], mval[:, :], gate[2][:, :], ALU.add).then_inc(m_val, 1)
                if more:
                    split(2 * i + N_G + 3, (N_G + 1) % 2, MPW)
                ve.wait_ge(m_hi, i + 1)
                ve.tensor_tensor(mlo[:, bass.ds(i, 1), :].rearrange("p a c -> p (a c)"), mval[:, :],
                                 mhi[:, bass.ds(i, 1), :].rearrange("p a c -> p (a c)").bitcast(F32),
                                 ALU.subtract).then_inc(m_lo, 1)

            merge(0, True, True)
            with ve.Fori(1, KD - 1) as i:
                merge(i, True)
            merge(KD - 1, False)
            for j in range(4):
                n = N_O + j
                split(n, n % 2, PW, True, out=wolo[:, 2 * j:2 * j + 2, :].rearrange("p k n -> p (k n)"),
                      hi=wohi[:, 2 * j:2 * j + 2, :].rearrange("p k n -> p (k n)"))

            ls = lstat[0:TR]

            def norm(x, t, step, before, nrm, root, done):
                k = 10 * t
                for h in range(2):
                    ve.bn_stats(ls[:, 6 * h:6 * h + 6], x[:, 512 * h:512 * h + 512]).then_inc(step, 1)
                ve.wait_ge(step, k + 2)
                ve.bn_aggr(ls[:, 12:14], ls[:, 0:12]).then_inc(step, 1)
                ve.wait_ge(step, k + 3)
                ve.tensor_scalar(ls[:, 14:15], ls[:, 13:14], EPS, None, ALU.add).then_inc(step, 1)
                ve.wait_ge(sq_out, root)
                ve.reciprocal(ls[:, 16:17], ls[:, 15:16]).then_inc(step, 1)
                ve.wait_ge(step, k + 5)
                ve.tensor_scalar(ls[:, 17:18], ls[:, 16:17], ls[:, 16:17], ls[:, 14:15], ALU.mult, ALU.mult)\
                  .then_inc(step, 1)
                ve.wait_ge(step, k + 6)
                ve.tensor_scalar(ls[:, 19:20], ls[:, 17:18], -0.5, 1.5, ALU.mult, ALU.add).then_inc(step, 1)
                ve.wait_ge(step, k + 7)
                ve.tensor_tensor(ls[:, 18:19], ls[:, 19:20], ls[:, 16:17], ALU.mult).then_inc(step, 1)
                ve.wait_ge(step, k + 8)
                ve.scalar_tensor_tensor(ls[:, 20:21], ls[:, 12:13], -1.0, ls[:, 18:19], ALU.mult, ALU.mult)\
                  .then_inc(step, 1)
                ve.wait_ge(nrm, t + 1)
                ve.tensor_tensor(x, x, lng[0:TR, :], ALU.mult).then_inc(step, 1)
                ve.wait_ge(step, k + 10)
                ve.tensor_tensor(x, x, lnb[0:TR, :], ALU.add).then_inc(done, 1)

            ve.wait_ge(ln_in, 32)
            for t in range(TT):
                ve.wait_ge(xrow_in[t % 2], 16 * (t // 2 + 1) + 16 * (t == TT - 1))
                ve.wait_ge(h_ps, t + 1)
                ve.scalar_tensor_tensor(hall[:, t, :], xrow[t % 2][:, :], ALPHA,
                                        ps[0:TR, 2 * (t % 2):2 * (t % 2) + 2, :].rearrange("p a n -> p (a n)"),
                                        ALU.mult, ALU.add).then_inc(h_sum, 1)
                ve.wait_ge(h_sum, t + 1)
                norm(hall[:, t, :], t, h_stat, None, h_nrm, t + 1, h_done)

            def esplit(n, s, first=False):
                ve.wait_ge(ehi_ok, n + 1)
                if not first:
                    ve.wait_ge(e_used, n - 2)
                ve.tensor_tensor(elo[s % 3][:, :], eraw[s][:, :], ehi[s % 3][:, :].bitcast(F32), ALU.subtract)\
                  .then_inc(elo_ok, 1)

            count = [0]

            def link(ins):
                count[0] += 1
                ins.then_inc(rd, 1)
                ve.wait_ge(rd, count[0])

            def over(x, n):
                return x[:, :].rearrange("p (t a) -> p t a", a=1).broadcast_to([TR, TT, n])

            i4, i16 = both_dims(con[0:TR, C_I4:C_I4 + 4], 4), both_dims(con[0:TR, C_I16:C_I16 + 16], 16)
            ve.wait_ge(lg_ps, TT)
            ve.wait_ge(h_done, TT)
            link(ve.tensor_tensor(lg[:, :, :], ps[0:TR, 6, 0:20 * TT].rearrange("p (t n) -> p t n", t=TT),
                                  both_dims(prm[0:TR, Q_BIAS:Q_BIAS + 20], 20), ALU.add))
            link(ve.tensor_reduce(gm[:, :], lg[:, :, 0:4], AX.X, ALU.max))
            link(ve.tensor_tensor(gd[:, :, :], lg[:, :, 0:4], over(gm, 4), ALU.subtract))
            link(ve.tensor_tensor(gk[:, :, :], lg[:, :, 0:4], over(gm, 4), ALU.is_lt))
            link(ve.tensor_scalar(gk[:, :, :], gk[:, :, :], 100.0, None, ALU.mult))
            link(ve.tensor_tensor(gk[:, :, :], gk[:, :, :], i4, ALU.add))
            link(ve.tensor_reduce(gi[:, :], gk[:, :, :], AX.X, ALU.min))
            link(ve.tensor_tensor(gk[:, :, :], i4, over(gi, 4), ALU.is_equal))
            link(ve.tensor_scalar(gk[:, :, :], gk[:, :, :], -1.0, -NEG, ALU.add, ALU.mult))
            link(ve.tensor_tensor(em[:, :, :].rearrange("p t (g e) -> p t g e", g=4),
                                  lg[:, :, 4:20].rearrange("p t (g e) -> p t g e", g=4),
                                  gk[:, :, :].rearrange("p t (g a) -> p t g a", a=1).broadcast_to([TR, TT, 4, 4]), ALU.add))

            def best(value, index, onehot):
                link(ve.tensor_reduce(value[:, :], em[:, :, :], AX.X, ALU.max))
                link(ve.tensor_tensor(cd[:, :, :], em[:, :, :], over(value, NE), ALU.is_lt))
                link(ve.tensor_scalar(cd[:, :, :], cd[:, :, :], 100.0, None, ALU.mult))
                link(ve.tensor_tensor(cd[:, :, :], cd[:, :, :], i16, ALU.add))
                link(ve.tensor_reduce(index[:, :], cd[:, :, :], AX.X, ALU.min))
                link(ve.tensor_tensor(onehot[:, :, :], i16, over(index, NE), ALU.is_equal))

            best(m1, i1, one1)
            link(ve.tensor_scalar(cd[:, :, :], one1[:, :, :], NEG, None, ALU.mult))
            link(ve.tensor_tensor(em[:, :, :], em[:, :, :], cd[:, :, :], ALU.add))
            best(m2, i2, one2)
            link(ve.tensor_tensor(m2[:, :], m2[:, :], m1[:, :], ALU.subtract))
            assert count[0] == R_DD
            ve.tensor_tensor(both[:, :, :], one1[:, :, :], one2[:, :, :], ALU.add).then_inc(both_ok, 1)
            ve.wait_ge(r_exp, 2)
            link(ve.tensor_reduce(gs[:, :], gd[:, :, :], AX.X, ALU.add))
            link(ve.tensor_scalar(m1[:, :], m2[:, :], 1.0, None, ALU.add))
            link(ve.tensor_tensor(m1[:, :], m1[:, :], gs[:, :], ALU.mult))
            link(ve.reciprocal(w1[:, :], m1[:, :]))
            link(ve.tensor_tensor(w2[:, :], m2[:, :], w1[:, :], ALU.mult))
            ve.wait_ge(rank_ps, 1)
            link(ve.tensor_copy(slotf[:, :, :], ps[0:TR, 7, 0:TT * NE].rearrange("p (t n) -> p t n", t=TT)))
            link(ve.tensor_copy(cnt[:, :], ps[:, 7, TT * NE:TT * NE + NE]))
            link(ve.tensor_scalar(oc[:, :], cnt[:, :], float(CAP), None, ALU.is_gt))
            for m in range(2, TT):
                link(ve.tensor_scalar(inc[0][:, :], cnt[:, :], float(CAP * m), None, ALU.is_gt))
                link(ve.tensor_tensor(oc[:, :], oc[:, :], inc[0][:, :], ALU.add))
            src = oc
            for k, d in enumerate((1, 2, 4, 8)):
                dst = inc[k % 2]
                link(ve.tensor_copy(dst[:, 0:d], src[:, 0:d]))
                link(ve.tensor_tensor(dst[:, d:NE], src[:, d:NE], src[:, 0:NE - d], ALU.add))
                src = dst
            link(ve.tensor_tensor(base2[:, :], src[:, :], oc[:, :], ALU.subtract))
            link(ve.tensor_scalar(base2[:, :], base2[:, :], float(CAP), float(NE * CAP - CAP), ALU.mult, ALU.add))
            link(ve.tensor_tensor(base2[:, :], base2[:, :], con[:, C_B1:C_B1 + NE], ALU.subtract))
            link(ve.tensor_scalar(sltmp[:, :, :], slotf[:, :, :], float(CAP), None, ALU.is_ge))
            link(ve.tensor_tensor(sltmp[:, :, :], sltmp[:, :, :], both_dims(base2[0:TR, :], NE), ALU.mult))
            link(ve.tensor_tensor(slotf[:, :, :], slotf[:, :, :], sltmp[:, :, :], ALU.add))
            link(ve.tensor_tensor(slotf[:, :, :], slotf[:, :, :], both_dims(con[0:TR, C_B1:C_B1 + NE], NE), ALU.add))
            for onehot, sf, si in ((one1, s1f, s1), (one2, s2f, s2)):
                link(ve.tensor_tensor(sltmp[:, :, :], slotf[:, :, :], onehot[:, :, :], ALU.mult))
                link(ve.tensor_reduce(sf[:, :], sltmp[:, :, :], AX.X, ALU.add))
                link(ve.tensor_copy(si[:, :], sf[:, :]))
            link(ve.tensor_tensor(ovf[:, :, :], con[:, C_I8:C_I8 + 8].rearrange("p (j a) -> p j a", a=1).broadcast_to([P, 8, NE]),
                                  src[:, :].rearrange("p (a e) -> p a e", a=1).broadcast_to([P, 8, NE]), ALU.is_ge))
            link(ve.tensor_reduce(ovi[:, :], ovf[:, :, :], AX.X, ALU.add))
            link(ve.tensor_scalar(ove[:, 0:8], ovi[:, :], float(NE - 1), None, ALU.min))
            ve.tensor_copy(ove[:, 8:9], src[:, NE - 1:NE]).then_inc(slots_ok, 1)
            for n in range(3):
                esplit(n, n, True)
            ve.wait_ge(slot_ps, 1)
            ve.tensor_copy(slots[:, :], ps[:, 6, P:P + NE + NOVER]).then_inc(slot_ok, 1)

            def xet(c):
                ve.wait_ge(xet_hi, c + 1)
                ve.tensor_tensor(xetlo[:, :, :].rearrange("p (a k) c -> p a (k c)", a=2), ps[:, 4:6, :],
                                 xethi[:, :, :].rearrange("p (a k) c -> p a (k c)", a=2).bitcast(F32), ALU.subtract)\
                  .then_inc(xet_lo, 1)

            def silu(c):
                ve.wait_ge(sig_ok, c + 1)
                ve.wait_ge(hid_ok, c)
                ve.tensor_tensor(act[:, :], ps[:, 0, :], sig[:, :], ALU.mult).then_inc(act_ok, 1)

            def hidden(c, ready, first=False):
                ve.wait_ge(e_used, ready)
                ve.wait_ge(act_ok, c + 1)
                if not first:
                    ve.wait_ge(hidt_ps, c)
                ve.tensor_tensor(hid[:, :], ps[:, 1, :], act[:, :], ALU.mult).then_inc(hid_ok, 1)

            def hidt(c):
                ve.wait_ge(hidt_hi, c + 1)
                ve.tensor_tensor(htlo[:, :, :].rearrange("p j c -> p (j c)"), ps[:, 6, :],
                                 hthi[:, :, :].rearrange("p j c -> p (j c)").bitcast(F32), ALU.subtract)\
                  .then_inc(hidt_lo, 1)

            def expert(e, more=True):
                esplit(6 * e, 0)
                esplit(6 * e + 1, 1)
                silu(e)
                hidt(e - 1)
                esplit(6 * e + 2, 2)
                esplit(6 * e + 3, 3)
                hidden(e, 6 * e + 2)
                if more:
                    xet(e + 1)
                esplit(6 * e + 4, 4)
                esplit(6 * e + 5, 5)

            xet(0)
            esplit(3, 3)
            silu(0)
            esplit(4, 4)
            esplit(5, 5)
            hidden(0, 4, True)
            xet(1)
            with ve.Fori(1, NE - 1) as e:
                expert(e)
            expert(NE - 1, False)
            hidt(NE - 1)
            n_over = ve.value_load(ove[0:1, 8:9], min_val=0, max_val=NOVER)
            with ve.Fori(0, NOVER) as j:
                with ve.If(j < n_over):
                    n, c = 6 * j + 6 * NE, j + NE
                    xet(c)
                    for k in range(4):
                        esplit(n + k, k)
                    silu(c)
                    esplit(n + 4, 4)
                    esplit(n + 5, 5)
                    hidden(c, n + 4)
                    hidt(c)

            ve.wait_ge(ln2_in, 32)
            for t in range(TT):
                s = t % 2
                ve.wait_ge(ya_in[s], 32 * (t // 2 + 1))
                ve.tensor_scalar(ya[s][:, :], ya[s][:, :], w1[:, t:t + 1], None, ALU.mult).then_inc(f_step, 1)
                if t >= 2:
                    ve.wait_ge(f_sent[s], 16 * (t // 2))
                ve.wait_ge(f_step, 2 * t + 1)
                ve.scalar_tensor_tensor(res[s][:, :], hall[:, t, :], ALPHA, ya[s][:, :], ALU.mult, ALU.add)\
                  .then_inc(f_step, 1)
                ve.wait_ge(f_step, 2 * t + 2)
                ve.scalar_tensor_tensor(res[s][:, :], yb[s][:, :], w2[:, t:t + 1], res[s][:, :], ALU.mult, ALU.add)\
                  .then_inc(f_sum, 1)
                ve.wait_ge(f_sum, t + 1)
                norm(res[s][:, :], t, f_stat, None, f_nrm, TT + t + 1, f_done)

        @block.gpsimd
        def _(gp):
            gp.memset(xhi[:, KD * T:XPAD].bitcast(F32), 0.0).then_inc(pad_zero, 1)
            gp.memset(xlo[:, KD * T:XPAD].bitcast(F32), 0.0).then_inc(pad_zero, 1)
            gp.memset(kodd[:, :, :], 0.0).then_inc(pads, 1)
            gp.memset(qsp[:, :, :, :, :], 0.0)
            gp.memset(cqp[:, :, :, :], 0.0).then_inc(pads, 1)
            gp.memset(mkt[:, :, :], 0.0).then_inc(pads, 1)
            gp.memset(zslot[:, :], 0.0).then_inc(z_slot, 1)
            gp.wait_ge(z_slot, 1)
            gp.dma_start(slot_dram.rearrange("(c p) a -> c (p a)", p=P), zslot[:, :]).then_inc(z_sent, 16)
            gp.memset(zrow[:, :], 0.0).then_inc(z_slot, 1)
            gp.wait_ge(z_slot, 2)
            for c in range(NE, NE + NOVER):
                gp.dma_start(y_dram[c * CAP:c * CAP + CAP, :], zrow[:, :]).then_inc(z_sent, 16)
            gp.wait_ge(con_in, 64)
            gp.wait_ge(xt_hi, KD + 1)
            gp.wait_ge(xt_lo, KD + 1)
            gp.wait_ge(z_out, ZU + 4)
            gp.wait_ge(st_out, 1)
            count = [0]

            def link(ins):
                count[0] += 1
                ins.then_inc(pool_step, 1)
                gp.wait_ge(pool_step, count[0])

            link(gp.tensor_copy(pext[:, :, :, PST], z[:, ZU:ZU + 4, SEQ:T]))
            for g, w in enumerate(POOL_W):
                src, d, k = z[:, ZU + g, :], 1, 0
                while d < w:
                    dst = pbuf[k % 2]
                    link(gp.tensor_copy(dst[:, 0:d], src[:, 0:d]))
                    link(gp.tensor_tensor(dst[:, d:SEQ], src[:, d:SEQ], src[:, 0:SEQ - d], ALU.add))
                    src, d, k = dst, 2 * d, k + 1
                cur, n = pext[:, g, :, PST + 1 - w:PST + 1], w
                while n > 1:
                    half = pext[:, g, :, PST + 1 - w:PST + 1 - w + n // 2]
                    link(gp.tensor_tensor(half, cur[:, :, 0:n // 2], cur[:, :, n // 2:n], ALU.add))
                    cur, n = half, n // 2
                link(gp.tensor_copy(src[:, SEQ:T], cur[:, :, 0]))
                link(gp.tensor_tensor(src[:, 0:16], src[:, 0:16], con[:, C_POOL + 16 * g:C_POOL + 16 * g + 16], ALU.mult))
                link(gp.tensor_scalar(src[:, 0:T], src[:, 0:T], 1.0 / w, None, ALU.mult))
                gp.tensor_tensor(pooled[:, g, :], src[:, 0:T], z[:, ZU + g, :], ALU.subtract).then_inc(pooled_in, 1)
                gp.wait_ge(pooled_in, g + 1)
            for r, t in enumerate(ROT):
                gp.wait_ge(z_out, ZT)
                gp.wait_ge(rot_ps, r + 1)
                gp.tensor_tensor(z[:, t, :], z[:, t, :], con[:, C_COS:C_COS + T], ALU.mult).then_inc(rot_cos, 1)
            gp.wait_ge(piece_used, N_M + 2)
            gp.memset(mkodd[:, :, :], 0.0).then_inc(pads, 1)
            gp.wait_ge(row_ps, 2)
            gp.wait_ge(kodd_ok, 1)
            gp.wait_ge(qs_ok, 1)
            gp.wait_ge(pads, 4)
            gp.memset(z[64:P, ZK:ZK + 2, :], 0.0).then_inc(pads, 1)
            gp.wait_ge(pads, 5)
            for g, (kind, b, h) in enumerate(groups):
                s, w = g % 2, P if kind == "swa" and b == 0 else 2 * P
                gp.wait_ge(sc_rec, g + 1)
                gp.tensor_tensor(probs[s][:, :, 0:w], probs[s][:, :, 0:w],
                                 stat[:, s, 6, :].rearrange("p (j w) -> p j w", w=1).broadcast_to([P, GRP, w]), ALU.mult)\
                  .then_inc(sc_nrm, 1)
            for t in range(TT):
                gp.wait_ge(h_done, t + 1)
                gp.dma_start(h_dram[t * TR:t * TR + TR, :], hall[:, t, :]).then_inc(h_sent, 16)
            gp.wait_ge(slots_ok, 1)
            gp.wait_ge(z_sent, 16 * (NOVER + 1))
            for t in range(TT):
                for s in (s1, s2):
                    gp.indirect_dma_start(out=slot_dram, out_offset=bass.IndirectOffsetOnAxis(ap=s[:, t:t + 1], axis=0),
                                          in_=con[0:TR, C_TOK + t:C_TOK + t + 1], in_offset=None).then_inc(slot_sent, 16)
            gp.wait_ge(slot_sent, 16 * 2 * TT)
            gp.dma_start(slrow[:, :], slot_dram.rearrange("(c p) a -> c (p a)", p=P)).then_inc(slot_in, 16)
            gp.wait_ge(slot_ok, 1)
            gp.wait_ge(h_sent, 16 * TT)

            def gather(c, first=False):
                if not first:
                    gp.wait_ge(xe_in, 16 * c)
                    gp.wait_ge(xet_ps, c)
                gp.tensor_copy(slotc[:, :], slots[:, bass.ds(c, 1)]).then_inc(slc_ok, 1)
                gp.wait_ge(slc_ok, c + 1)
                gp.sem_inc(slc_seen, 1)
                gp.indirect_dma_start(out=xe[:, :], out_offset=None, in_=h_dram,
                                      in_offset=bass.IndirectOffsetOnAxis(ap=slotc[:, :], axis=0)).then_inc(xe_in, 16)

            gather(0, True)
            with gp.Fori(1, NE) as c:
                gather(c)
            n_over = gp.value_load(ove[0:1, 8:9], min_val=0, max_val=NOVER)
            with gp.Fori(0, NOVER) as j:
                with gp.If(j < n_over):
                    gather(j + NE)
            gp.wait_ge(moe_done, 1)
            for t in range(TT):
                if t >= 2:
                    gp.wait_ge(f_sum, t - 1)
                for dst, s in ((ya, s1), (yb, s2)):
                    gp.indirect_dma_start(out=dst[t % 2][:, :], out_offset=None, in_=y_dram,
                                          in_offset=bass.IndirectOffsetOnAxis(ap=s[:, t:t + 1], axis=0))\
                      .then_inc(ya_in[t % 2], 16)


def constants():
    import numpy as np

    c = np.zeros((P, C_END), np.float32)
    c[:, C_ID:C_ID + P] = np.eye(P)
    half = HD // 8
    for head in range(2):
        for d in range(half):
            c[head * HD + d + half, C_ROT + head * HD + d] = -1.0
            c[head * HD + d, C_ROT + head * HD + d + half] = 1.0
    pos = np.concatenate([np.arange(SEQ), np.full(NS, 2048)]).astype(np.float32)
    inv = np.power(np.float32(500000.0), -np.arange(half, dtype=np.float32) * np.float32(2.0 / (2 * half)))
    ang = pos[None, :] * inv.astype(np.float32)[:, None]
    c[:, C_COS:C_COS + T] = 1.0
    for head in range(2):
        for rep in range(2):
            r = head * HD + rep * half
            c[r:r + half, C_COS:C_COS + T] = np.cos(ang)
            c[r:r + half, C_SIN:C_SIN + T] = np.sin(ang)
    i, k = np.arange(P)[:, None], np.arange(2 * P)[None, :]
    c[:, C_MASK:C_MASK + 2 * P] = np.where((k <= P + i) & (k >= i), 0.0, NEG)
    t = np.arange(16)
    for g, w in enumerate(POOL_W):
        c[:, C_POOL + 16 * g:C_POOL + 16 * g + 16] = w / np.minimum(t + 1, w)
    c[:TR, C_UP:C_UP + TR] = np.triu(np.ones((TR, TR)), 1)
    c[:, C_ONE:C_ONE + P] = 1.0
    c[:, C_I4:C_I4 + 4] = np.arange(4)
    c[:, C_I16:C_I16 + 16] = np.arange(16)
    c[:, C_B1:C_B1 + NE] = np.arange(NE) * CAP
    c[:TR, C_TOK:C_TOK + TT] = np.arange(TT)[None, :] * TR + np.arange(TR)[:, None]
    c[:, C_BM:C_BM + NS] = (np.arange(P)[:, None] % 32 // 4) == np.arange(NS)[None, :]
    c[:, C_I8:C_I8 + 8] = np.arange(8)
    return c


def kernel(**inputs):
    import numpy as np
    import concourse.bacc as bacc
    from concourse.bass_utils import run_bass_kernel_spmd

    x = {k: np.asarray(w) for k, w in inputs.items()}
    w_in = x["w_in"][0]
    heads = [8 * (t // 4) + t % 4 + 4 * s for t in range(8) for s in range(2)]
    q0, k0, v0, u0, c0, g0 = 0, 1024, 1280, 1536, 2048, 2304
    qcols = [q0 + h * HD + d for h in heads for d in range(HD)]
    zcols = list(range(u0, c0)) + list(range(k0, v0)) + list(range(c0, g0)) + qcols

    def blocks(w):
        return w.reshape(w.shape[0] // P, P, w.shape[1] // P, P).transpose(2, 1, 0, 3)

    wz = blocks(w_in[:, zcols]).reshape(ZP, 2, P, KD * P).transpose(0, 2, 1, 3).reshape(ZP, P, PW)
    wv = w_in[:, v0:u0].reshape(KD, P, 256).transpose(1, 0, 2).reshape(P, PW)
    wmem = np.concatenate([x["w_mem_k"][0], x["w_mem_v"][0]], 1).reshape(2, 4, P, 512).transpose(0, 2, 1, 3)
    wa = x["w_branch_a"][0][qcols]
    parts = [w_in[:, g0 + D * g:g0 + D * g + D] for g in range(3)] + [wa, x["w_branch_b"][0], x["w_branch_c"][0]]
    wm = np.concatenate([blocks(w) for w in parts], 2).reshape(KD, P, 2, MPW).transpose(0, 2, 1, 3)
    sinks = x["sinks"][0]
    params = np.concatenate([
        np.broadcast_to(sinks, (P, NH)),
        sinks.reshape(NKV, 1, GRP).repeat(NS, 1).reshape(P, 1),
        x["pool_scale"][0].reshape(4, P).T,
        np.broadcast_to(np.concatenate([x["b_group"][0], x["b_router"][0].reshape(-1)]), (P, 20)),
    ], 1)
    w_route = np.concatenate([x["w_group"][0], x["w_router"][0].reshape(D, NE)], 1)
    data = {
        "consts": constants(),
        "params": params,
        "x_prompt": x["x_prompt"].reshape(SEQ, D),
        "x_sample": x["x_sample"].reshape(NS, D),
        "cache_win_k": x["cache_win_k"].reshape(NS, WIN, 256),
        "cache_win_v": x["cache_win_v"].reshape(NS, WIN, 256),
        "state_pool": x["state_pool"].reshape(NS, PST, 512),
        "cache_mem_k": x["cache_mem_k"].reshape(NS, NMEM, 256),
        "cache_mem_v": x["cache_mem_v"].reshape(NS, NMEM, 256),
        "mem_prompt": x["mem_prompt"].reshape(NMEM, D),
        "wz": wz, "wv": wv, "wmem": wmem.reshape(2, P, PW), "wm": wm.reshape(2 * KD, P, MPW),
        "wo": x["w_out"][0].reshape(4, 2, P, D).transpose(0, 2, 1, 3).reshape(4, P, PW),
        "w_pool_mix": x["w_pool_mix"][0],
        "w_route": w_route.reshape(KD, P, 20).transpose(1, 0, 2),
        "ln1_g": x["ln1_g"], "ln1_b": x["ln1_b"], "ln2_g": x["ln2_g"], "ln2_b": x["ln2_b"],
        "w_gate": x["w_gate"][0], "w_up": x["w_up"][0], "w_down": x["w_down"][0],
    }
    outs = {
        "y_prompt": (SEQ, D), "y_sample": (NS, D),
        "new_k_prompt": (WIN, 256), "new_v_prompt": (WIN, 256), "new_pool_prompt": (PST, 512),
        "new_mem_k": (NMEM, 256), "new_mem_v": (NMEM, 256),
        "new_k_sample": (NS, WIN, 256), "new_v_sample": (NS, WIN, 256), "new_pool_sample": (NS, PST, 512),
    }
    shapes = [
        (1, SEQ, D), (NS, 1, D), (1, 1, WIN, NKV, HD), (1, 1, WIN, NKV, HD), (1, 1, PST, 512),
        (1, 1, NMEM, MH, HD), (1, 1, NMEM, MH, HD), (1, NS, WIN, NKV, HD), (1, NS, WIN, NKV, HD), (1, NS, PST, 512),
    ]
    nc = bacc.Bacc("TRN2", target_bir_lowering=False, num_devices=1)
    arrays, a, o = {}, {}, {}
    for name, w in data.items():
        arrays[name + "_in"] = np.ascontiguousarray(w)
        a[name] = nc.dram_tensor(name + "_in", w.shape, F32, kind="ExternalInput").ap()
    for name, shape in outs.items():
        o[name] = nc.dram_tensor(name, shape, F32, kind="ExternalOutput").ap()
    decoder_step(nc, a, o)
    r = run_bass_kernel_spmd(nc, [arrays], core_ids=[0]).results[0]
    return tuple(r[name].reshape(shape) for name, shape in zip(outs, shapes))
```

```python
from contextlib import ExitStack

import concourse.bass as bass
from concourse import mybir

F32 = mybir.dt.float32
F32R = mybir.dt.float32r
I32 = mybir.dt.int32
ALU = mybir.AluOpType
ACT = mybir.ActivationFunctionType
AX = mybir.AxisListType

P = 128
D = 1024
KD = D // P
SEQ, NS = 512, 8
T = SEQ + NS
TH = T // 2
TT = 5
TR = T // TT
NB = SEQ // P
HD, NH, NKV, GRP = 64, 16, 4, 4
WIN = 128
NMEM, MH = 256, 4
POOL_W = (2, 4, 8, 16)
PST = 15
NG, EG = 4, 4
NE = NG * EG
DE = 512
CAP = P
NOVER = 8
NSLOT = (NE + NOVER) * CAP
ALPHA = 2.0 ** 0.25
EPS = 1e-5
SCALE = HD ** -0.5
NEG = -1.0e30

ZU, ZK, ZC, ZQ = 0, 4, 6, 8
ZT = 16
ZP = ZT * KD * P // 2048
MT = 3 * KD + 8 + 4 + 2
MPW = MT // 2 * P
PW = 2048

C_ID, C_ROT, C_COS, C_SIN, C_MASK = 0, 128, 256, 776, 1296
C_POOL, C_UP, C_ONE, C_I4, C_I16, C_B1, C_TOK, C_BM, C_I8, C_END = (
    1552, 1616, 1720, 1848, 1852, 1868, 1884, 1889, 1897, 1905)
NCH = NE + NOVER
G_LT, G_BK, G_CH, G_ROW, G_END = 0, 256, 272, 272 + NCH + 1, 272 + NCH + 1 + CAP
Q_SINK, Q_SINKR, Q_PSC, Q_BIAS, Q_END = 0, 16, 17, 21, 41


def decoder_step(nc, a, o):
    ctx = ExitStack()
    with ctx:
        def sem(name):
            return ctx.enter_context(nc.semaphore(name))

        def at(name, offset, shape, dt=F32):
            return nc.alloc_sbuf_tensor_at(name, shape, dt, offset=offset)

        RING, X, Z, OAL = 16512, 74880, 109120, 142400
        OB, OC, ML, CON, PRM, VV, TAIL = 159040, 175680, 184000, 200640, 208320, 211200, 222464
        SL = MPW * 4
        raw = [at(f"raw{s}", RING + s * SL, [P, MPW]) for s in range(2)]
        whi = [at(f"whi{s}", RING + (2 + s) * SL, [P, MPW], F32R) for s in range(2)]
        wlo = [at(f"wlo{s}", RING + (4 + s) * SL, [P, MPW], F32R) for s in range(2)]
        XPAD = KD * T + P - NS
        xhi = at("xhi", X, [P, XPAD], F32R)
        xlo = at("xlo", X + 17120, [P, XPAD], F32R)
        z = at("z", Z, [P, ZT, T])
        oahi = at("oahi", Z + 16640, [P, 8, T], F32R)
        mhi = at("mhi", Z, [P, 8, T], F32R)
        oalo = at("oalo", OAL, [P, 8, T], F32R)
        obhi = at("obhi", OB, [P, 4, T], F32R)
        oblo = at("oblo", OB + 8320, [P, 4, T], F32R)
        ochi = at("ochi", OC, [P, 2, T], F32R)
        oclo = at("oclo", OC + 4160, [P, 2, T], F32R)
        mlo = at("mlo", ML, [P, 8, T], F32R)
        con = at("con", CON, [P, C_END])
        prm = at("prm", PRM, [P, Q_END])
        wmix = at("wmix", PRM + 192, [P, 4, P])
        wrt = at("wrt", PRM + 192 + 2048, [P, KD, 20])
        xtok = at("xtok", OAL, [P, NB, D])
        xsam = at("xsam", OAL + 16384, [NS, D])
        mtok = at("mtok", OAL + 20480, [P, 2, D])
        mthi = at("mthi", ML, [P, KD, NMEM], F32R)
        mtlo = at("mtlo", ML + 8192, [P, KD, NMEM], F32R)
        pooled = at("pooled", OAL, [P, 4, T])
        pbuf = [at(f"pbuf{s}", OAL + 8320 + s * 2080, [P, T]) for s in range(2)]
        pstate = at("pstate", OAL + 12480, [NS * PST, 512])
        pext = at("pext", OAL + 14528, [P, 4, NS, PST + 1])
        rtmp = [at(f"rtmp{s}", OAL + 8320 + s * 2080, [P, T]) for s in range(2)]
        v = at("v", VV, [P, NB + 1, NKV * HD])
        mkv = at("mkv", VV + 5120, [P, 2, 512])
        kodd = at("kodd", OC + 4160, [P, 2, T])
        mkt = at("mkt", VV + 9216, [P, 2, NMEM])
        mkodd = at("mkodd", ML + 12288, [P, 2, NMEM])
        probs = [at(f"probs{s}", ML + s * 4096, [P, GRP, 2 * P]) for s in range(2)]
        pt = at("pt", ML + 8192, [P, 2, GRP * P])
        stat = at("stat", TAIL + 512, [P, 2, 8, 4])
        nsink = at("nsink", TAIL + 768, [P, 17])
        kvrow = at("kvrow", TAIL + 1024, [P, 512])
        CACHE = RING + 2 * SL
        cach_v = at("cach_v", CACHE, [P, NS, 256])
        cach_k = at("cach_k", CACHE + SL, [P, NS, 256])
        cm_v = [at("cm_v", CACHE + 2 * SL, [P, NS, 256]), cach_v]
        cm_k = [at("cm_k", CACHE + 3 * SL, [P, NS, 256]), cach_k]
        kt = at("kt", ML + 14336, [P, 512])
        srow = at("srow", TAIL + 3072, [P, 264])
        scol = at("scol", TAIL + 4160, [P, P + NS])
        pcol = at("pcol", TAIL + 4704, [P, P])
        pnew = at("pnew", TAIL + 5216, [P, P])
        sstat = at("sstat", TAIL + 5728, [P, 16])
        qsp = at("qsp", TAIL + 5792, [P, 2, 2, NS, GRP])
        cqp = at("cqp", TAIL + 6304, [P, 2, 2, NS])
        kns = at("kns", TAIL + 6432, [P, 2, NS])
        urow = at("urow", TAIL + 3072, [P, 512])
        gate = [at(f"gate{s}", VV + s * 2080, [P, T]) for s in range(3)]
        zrow = at("zrow", VV, [P, D])
        mval = at("mval", VV + 6240, [P, T])
        wohi = at("wohi", X, [P, KD, D], F32R)
        wolo = at("wolo", OAL, [P, KD, D], F32R)
        hall = at("hall", RING + 2 * SL, [TR, TT, D])
        xrow = [at(f"xrow{s}", RING + 2 * SL + 20480 + s * 4096, [TR, D]) for s in range(2)]
        ht = at("ht", RING + 2 * SL + 28672, [P, KD, TR])
        lng = at("lng", VV, [P, D])
        lnb = at("lnb", VV + 4096, [P, D])
        lstat = [at(f"lstat{s}", VV + 8192 + s * 128, [P, 32]) for s in range(2)]
        R0 = ML
        K0 = VV + 8448

        def rt(name, k, shape, dt=F32):
            return at(name, R0 + k * 320, shape, dt)
        lg = at("lg", R0, [TR, TT, 20])
        gm, gd, gs = rt("gm", 2, [TR, TT]), rt("gd", 3, [TR, TT, 4]), rt("gs", 4, [TR, TT])
        gi, gk = rt("gi", 5, [TR, TT]), rt("gk", 6, [TR, TT, 4])
        em, cd = rt("em", 7, [TR, TT, NE]), rt("cd", 8, [TR, TT, NE])
        picks = at("picks", R0 + 9 * 320, [TR, 2, TT, NE])
        both = rt("both", 11, [TR, TT, NE])
        m1, m2, i1, i2 = (rt(n, 12 + k, [TR, TT]) for k, n in enumerate(("m1", "m2", "i1", "i2")))
        w1, w2 = at("w1", K0, [TR, TT]), at("w2", K0 + 32, [TR, TT])
        rankb, past = rt("rankb", 16, [TR, TT, NE]), rt("past", 17, [TR, TT, NE])
        picked = at("picked", R0 + 18 * 320, [TR, 2, TT, NE])
        slotf = rt("slotf", 20, [TR, 2, TT])
        nfull, place = rt("nfull", 21, [TR, 2, TT]), rt("place", 22, [TR, 2, TT])
        s12 = at("s12", K0 + 64, [TR, 2, TT], I32)
        oc, excl, base2, incl = (rt(n, 23 + k, [TR, NE]) for k, n in enumerate(("oc", "excl", "base2", "incl")))
        ocl = at("ocl", R0 + 27 * 320, [TR, NE, NE])
        ovf, ovi = rt("ovf", 31, [TR, 8, NE]), at("ovi", R0 + 33 * 320, [TR, 8])
        rcon = at("rcon", R0 + 34 * 320, [P, G_END])
        atleast = at("atleast", R0 + 40 * 320, [TR, 2, TT, NCH + 1])
        chunk = at("chunk", R0 + 44 * 320, [TR, 2, TT, NCH])
        chunkr = at("chunkr", R0 + 47 * 320, [TR, 2, TT, NCH], F32R)
        rowhot = at("rowhot", TAIL, [TR, 2, TT, CAP], F32R)
        ove = at("ove", K0 + 128, [P, 16], I32)
        slots = at("slots", K0 + 192, [P, NCH], I32)
        MR = 8192
        HALL = RING + 2 * SL
        ER = 12
        eraw = [at(f"eraw{s}", offset, [P, PW]) for s, offset in enumerate(
            [RING + SL, RING, HALL + 20480, VV, HALL, HALL + MR] + [X + s * MR for s in range(6)])]
        assert (ZP + 3 + 2 * KD) % 2 == 1
        ehi = [at(f"ehi{s}", X + (6 + s) * MR, [P, PW], F32R) for s in range(3)]
        elo = [at(f"elo{s}", X + (9 + s) * MR, [P, PW], F32R) for s in range(3)]
        E0 = X + 12 * MR
        xe = [at("xe0", E0, [P, D]), at("xe1", HALL + 2 * MR, [P, D])]
        xethi = at("xethi", E0 + 4096, [P, KD, P], F32R)
        xetlo = at("xetlo", E0 + 8192, [P, KD, P], F32R)
        sig = at("sig", E0 + 12288, [P, DE])
        act = at("act", E0 + 14336, [P, DE])
        hid = at("hid", E0 + 16384, [P, DE])
        hthi = at("hthi", E0 + 18432, [P, 4, P], F32R)
        htlo = at("htlo", E0 + 20480, [P, 4, P], F32R)
        yout = [at("yout0", E0 + 22528, [P, D]), at("yout1", TAIL, [P, D])]
        slotc = [at(f"slotc{q}", E0 + 26624 + 32 * q, [P, 1], I32) for q in range(2)]
        ya, yb, res = ([at(f"{n}{t}", X + (5 * k + t) * 4096, [TR, D]) for t in range(TT)]
                       for k, n in enumerate(("ya", "yb", "res")))

        ps = ctx.enter_context(nc.psum_tensor("ps", [P, 8, 512], F32))
        h_dram = nc.dram_tensor("h_dram", (T, D), F32, kind="Internal").ap()
        y_dram = nc.dram_tensor("y_dram", (NSLOT, D), F32, kind="Internal").ap()

        ident = con[:, C_ID:C_ID + P]
        upper = con[0:TR, C_UP:C_UP + TR]
        ones = con[0:TR, C_ONE:C_ONE + P]

        id_in, con_in, x_in, m_in = sem("id_in"), sem("con_in"), sem("x_in"), sem("m_in")
        st_in, win_in, winv_in, cmv_in = (sem(n) for n in ("st_in", "win_in", "winv_in", "cmv_in"))
        cm_in = [sem(f"cm_in{q}") for q in range(2)]
        raw_in = [sem(f"raw_in{s}") for s in range(2)]
        hi_split, lo_split, piece_used = sem("hi_split"), sem("lo_split"), sem("piece_used")
        pad_zero = sem("pad_zero")
        xt_ps, xt_hi, xt_lo = sem("xt_ps"), sem("xt_hi"), sem("xt_lo")
        z_even, z_out = sem("z_even"), sem("z_out")
        v_out, mkv_out, mkt_ps, mkt_out = sem("v_out"), sem("mkv_out"), sem("mkt_ps"), sem("mkt_out")
        v_ps, pads, kodd_ok = sem("v_ps"), sem("pads"), sem("kodd_ok")
        rot_ps, rot_mul, rot_cos, roped = sem("rot_ps"), sem("rot_mul"), sem("rot_cos"), sem("roped")
        row_ps, row_out, rows_sent = sem("row_ps"), sem("row_out"), sem("rows_sent")
        st_ps, st_out, pool_step, pooled_in = sem("st_ps"), sem("st_out"), sem("pool_step"), sem("pooled_in")
        mix_ps, mix_hi, mix_lo = sem("mix_ps"), sem("mix_hi"), sem("mix_lo")
        prep = sem("prep")
        sc_ps, sc_row, sc_max, sc_neg, sc_snk, sc_exp, sc_den, sc_rec, sc_nrm = (sem(n) for n in (
            "sc_ps", "sc_row", "sc_max", "sc_neg", "sc_snk", "sc_exp", "sc_den", "sc_rec", "sc_nrm"))
        pt_ps, pt_act, pt_dve, o_ps, o_hi, o_lo = (sem(n) for n in (
            "pt_ps", "pt_act", "pt_dve", "o_ps", "o_hi", "o_lo"))
        qs_ok, kt_ps, kt_ok, ks_ps = sem("qs_ok"), sem("kt_ps"), sem("kt_ok"), sem("ks_ps")
        sw_ps, sw_act, sw_dve = sem("sw_ps"), sem("sw_act"), sem("sw_dve")
        sm_ps, sm_act, sm_dve = sem("sm_ps"), sem("sm_act"), sem("sm_dve")
        prod_ps, gate_out, m_step, m_val, m_hi, m_lo = (sem(n) for n in (
            "prod_ps", "gate_out", "m_step", "m_val", "m_hi", "m_lo"))
        ln_in, xrow_in = sem("ln_in"), [sem(f"xrow_in{s}") for s in range(2)]
        h_ps, h_sum, h_stat, h_root, h_fac, h_nrm, h_gain, h_done, h_last, h_sent = (sem(n) for n in (
            "h_ps", "h_sum", "h_stat", "h_root", "h_fac", "h_nrm", "h_gain", "h_done", "h_last", "h_sent"))
        ht_ps, ht_out, lg_ps, lg_out = sem("ht_ps"), sem("ht_out"), sem("lg_ps"), sem("lg_out")
        rc_in, rd, gd_ok, dist_ok, r_exp, both_ok, rank_ps, list_ok, over_ok, z_row, z_sent = (sem(n) for n in (
            "rc_in", "rd", "gd_ok", "dist_ok", "r_exp", "both_ok", "rank_ps", "list_ok", "over_ok", "z_row", "z_sent"))
        slot_ps, slot_ok, s12_ok = sem("slot_ps"), sem("slot_ok"), sem("s12_ok")
        eraw_in = [sem(f"eraw_in{s}") for s in range(ER)]
        ehi_ok, elo_ok, e_used = sem("ehi_ok"), sem("elo_ok"), sem("e_used")
        slc_seen = sem("slc_seen")
        slc_ok, xet_ps, xet_hi, xet_lo = (sem(n) for n in ("slc_ok", "xet_ps", "xet_hi", "xet_lo"))
        xe_in, y_sent = ([sem(f"{n}{q}") for q in range(2)] for n in ("xe_in", "y_sent"))
        g_ps, sig_ok, act_ok, hid_ok, hidt_ps, hidt_hi, hidt_lo = (sem(n) for n in (
            "g_ps", "sig_ok", "act_ok", "hid_ok", "hidt_ps", "hidt_hi", "hidt_lo"))
        y_out, moe_done = sem("y_out"), sem("moe_done")
        ln2_in, ya_in = sem("ln2_in"), [sem(f"ya_in{t}") for t in range(TT)]
        h_back, ya_w, f_part, f_sum, f_stat, f_root, f_fac, f_nrm, f_gain, f_done, f_last, f_sent = (sem(n) for n in (
            "h_back", "ya_w", "f_part", "f_sum", "f_stat", "f_root", "f_fac", "f_nrm", "f_gain", "f_done", "f_last",
            "f_sent"))
        copied = sem("copied")

        groups = [("swa", b, 2 * p + s) for p in range(2) for b in range(NB) for s in range(2)] \
            + [("mem", b, 0) for b in range(NB)]
        NGR = len(groups)
        MEM_ORDER = (0, 2, 1, 3)

        def narrow(g):
            return groups[g][0] == "swa" and groups[g][1] == 0

        def act_copies(g):
            return sum(not narrow(n) for n in range(g))

        ROT = (ZK, ZK + 1) + tuple(range(ZQ, ZQ + 8))
        NKT = 4 + NS
        S_T1, S_T2, S_PV = 5, 7, 8
        S_OUT = S_PV + 3
        M_T1, M_T2, M_PV = 13, 15, 16
        M_OUT = M_PV + 1
        HALF_A = NKT + 2, NKT + 3
        LAST = M_OUT + 1
        N_V, N_M, N_G = ZP, ZP + 1, ZP + 3
        N_O = N_G + 2 * KD

        def both_dims(src, n):
            return src.rearrange("p (a n) -> p a n", a=1).broadcast_to([TR, TT, n])

        def halves(ap):
            return ap.rearrange("p (h c) -> p h c", h=2)

        def pair(s, rows=slice(0, P)):
            return ps[rows, 2 * s:2 * s + 2, 0:TH]

        block = ctx.enter_context(nc.Block())

        @block.sync
        def _(sp):
            sp.dma_start(con[:, 0:P], a["consts"][:, 0:P]).then_inc(id_in, 16)
            xp = a["x_prompt"].rearrange("(t p) d -> p t d", p=P)
            for t in range(NB):
                sp.dma_start(xtok[:, t, :], xp[:, t, :]).then_inc(x_in, 16)
            sp.dma_start(xsam[:, :], a["x_sample"]).then_inc(x_in, 16)

            def piece(n, src, width, first=False):
                if not first:
                    sp.wait_ge(hi_split, n - 1)
                    sp.wait_ge(lo_split, n - 1)
                sp.dma_start(raw[n % 2][:, 0:width], src).then_inc(raw_in[n % 2], 16)

            for n in range(2):
                piece(n, a["wz"][n], PW, True)
            sp.dma_start(mtok[:, :, :], a["mem_prompt"].rearrange("(t p) d -> p t d", p=P)).then_inc(m_in, 16)
            sp.dma_start(con[:, P:C_END], a["consts"][:, P:C_END]).then_inc(con_in, 16)
            sp.dma_start(prm[:, :], a["params"]).then_inc(con_in, 16)
            sp.dma_start(wmix[:, :, :], a["w_pool_mix"].rearrange("g c d -> c g d")).then_inc(con_in, 16)
            sp.dma_start(wrt[:, :, :], a["w_route"]).then_inc(con_in, 16)
            sp.wait_ge(xt_lo, KD + 1)
            sp.wait_ge(xt_hi, KD + 1)
            sp.dma_start(pstate[:, :], a["state_pool"].rearrange("b r c -> (b r) c")).then_inc(st_in, 16)
            with sp.Fori(1, ZP // 2) as i:
                for j in range(2):
                    sp.wait_ge(hi_split, 2 * i + j - 1)
                    sp.wait_ge(lo_split, 2 * i + j - 1)
                    sp.dma_start(raw[j][:, 0:PW], a["wz"][bass.ds(2 * i + j, 1)].rearrange("a p n -> (a p) n"))\
                      .then_inc(raw_in[j], 16)
            piece(N_V, a["wv"], PW)
            for j in range(2):
                piece(N_M + j, a["wmem"][j], PW)
            for j in range(2):
                piece(N_G + j, a["wm"][j], MPW)
            sp.wait_ge(piece_used, N_M + 2)
            sp.dma_start(cach_k[:, :, :], a["cache_win_k"].rearrange("b k d -> k b d")).then_inc(win_in, 16)
            sp.dma_start(cach_v[:, :, :], a["cache_win_v"].rearrange("b k d -> k b d")).then_inc(winv_in, 16)
            ck = a["cache_mem_k"].rearrange("b (t p) d -> p b t d", p=P)
            cv = a["cache_mem_v"].rearrange("b (t p) d -> p b t d", p=P)

            def half_cache(dst, src, q, arrived):
                for t in range(2):
                    sp.dma_start(dst[q][:, :, :].rearrange("p (b t) d -> p b t d", t=2)[:, :, t, :],
                                 src[:, 4 * q:4 * q + 4, t, :]).then_inc(arrived, 16)

            half_cache(cm_k, ck, 0, cm_in[0])
            half_cache(cm_v, cv, 0, cmv_in)
            sp.wait_ge(v_out, 3)
            sp.dma_start(o["new_v_prompt"], v[:, NB - 1, :]).then_inc(copied, 16)
            sp.dma_start(o["new_v_sample"][:, WIN - 1, :], v[0:NS, NB, :]).then_inc(copied, 16)
            sp.wait_ge(mkv_out, 2)
            sp.dma_start(o["new_mem_k"].rearrange("(t p) d -> p t d", p=P), mkv[:, :, 0:256]).then_inc(copied, 16)
            sp.dma_start(o["new_mem_v"].rearrange("(t p) d -> p t d", p=P), mkv[:, :, 256:512]).then_inc(copied, 16)
            sp.dma_start(o["new_k_sample"][:, 0:WIN - 1, :], a["cache_win_k"][:, 1:WIN, :]).then_inc(copied, 16)
            sp.dma_start(o["new_v_sample"][:, 0:WIN - 1, :], a["cache_win_v"][:, 1:WIN, :]).then_inc(copied, 16)
            sp.dma_start(o["new_pool_sample"][:, 0:PST - 1, :], a["state_pool"][:, 1:PST, :]).then_inc(copied, 16)
            sp.wait_ge(row_out, 2)
            sp.dma_start(o["new_k_prompt"], kvrow[:, 0:256]).then_inc(rows_sent, 16)
            sp.dma_start(o["new_k_sample"][:, WIN - 1, :], kvrow[0:NS, 256:512]).then_inc(rows_sent, 16)
            sp.wait_ge(row_out, 3)
            sp.dma_start(o["new_pool_prompt"], urow[0:PST, :]).then_inc(rows_sent, 16)
            sp.dma_start(o["new_pool_sample"][:, PST - 1, :], urow[PST:PST + NS, :]).then_inc(rows_sent, 16)
            sp.wait_ge(kt_ps, 4)
            half_cache(cm_k, ck, 1, cm_in[1])
            sp.wait_ge(sw_ps, 4)
            half_cache(cm_v, cv, 1, cmv_in)
            with sp.Fori(1, KD) as i:
                for j in range(2):
                    s = (N_G + j) % 2
                    sp.wait_ge(hi_split, 2 * i + N_G + j - 1)
                    sp.wait_ge(lo_split, 2 * i + N_G + j - 1)
                    sp.dma_start(raw[s][:, :], a["wm"][bass.ds(2 * i + j, 1)].rearrange("a p n -> (a p) n"))\
                      .then_inc(raw_in[s], 16)
            for j in range(4):
                piece(N_O + j, a["wo"][j], PW)
            sp.wait_ge(m_hi, KD)
            sp.wait_ge(m_lo, KD)
            sp.dma_start(lng[:, :], a["ln1_g"].broadcast_to([P, D])).then_inc(ln_in, 16)
            sp.dma_start(lnb[:, :], a["ln1_b"].broadcast_to([P, D])).then_inc(ln_in, 16)
            for t in range(TT):
                if t >= 2:
                    sp.wait_ge(h_sum, t - 1)
                n = min(TR, SEQ - t * TR)
                sp.dma_start(xrow[t % 2][0:n, :], a["x_prompt"][t * TR:t * TR + n, :]).then_inc(xrow_in[t % 2], 16)
                if n < TR:
                    sp.dma_start(xrow[t % 2][n:TR, :], a["x_sample"]).then_inc(xrow_in[t % 2], 16)

            def expert_piece(n, s, src, first=False):
                if not first:
                    sp.wait_ge(ehi_ok, n + 1 - ER)
                    sp.wait_ge(elo_ok, n + 1 - ER)
                sp.dma_start(eraw[s][:, :], src).then_inc(eraw_in[s], 16)

            wg = a["w_gate"].rearrange("e (p h k) n -> e h p (k n)", h=2, k=4)
            wu = a["w_up"].rearrange("e (p h k) n -> e h p (k n)", h=2, k=4)
            wd = a["w_down"].rearrange("e (p h k) n -> e h p (k n)", h=2, k=2)

            def of(w, e, h):
                return w[bass.ds(e, 1), h].rearrange("a p n -> (a p) n")

            for n in range(2):
                sp.wait_ge(hi_split, N_O + 3 + n)
                sp.wait_ge(lo_split, N_O + 3 + n)
                expert_piece(n, n, wg[0, n], True)
            sp.wait_ge(h_sum, TT)
            expert_piece(2, 2, wu[0, 0], True)
            sp.dma_start(rcon[:, :], a["route_consts"]).then_inc(rc_in, 16)
            for n in range(2):
                expert_piece(6 + n, 6 + n, wu[1, n], True)
            sp.wait_ge(h_done, TT - 1)
            sp.wait_ge(h_last, 2)
            expert_piece(3, 3, wu[0, 1], True)
            sp.wait_ge(lg_ps, TT)
            sp.wait_ge(h_sent, 16 * TT)
            for n in range(2):
                expert_piece(4 + n, 4 + n, wg[1, n], True)
            for n in range(2):
                expert_piece(8 + n, 8 + n, wd[0, n], True)
            expert_piece(10, 10, wg[2, 0], True)
            sp.wait_ge(slc_seen, 2)
            expert_piece(11, 11, wg[2, 1], True)
            for n in range(2):
                expert_piece(12 + n, n, wu[2, n])
            for n in range(2):
                expert_piece(14 + n, 2 + n, wd[1, n])

            def weights(e, odd):
                n = 6 * odd - 2
                for k, w in enumerate((wg, wg, wu, wu)):
                    expert_piece(6 * e - 2 + k, (n + k) % ER, of(w, e, k % 2))
                for k in range(2):
                    expert_piece(6 * e + 2 + k, (n + 4 + k) % ER, of(wd, e - 1, k))

            with sp.Fori(1, NE // 2 - 1) as i:
                weights(2 * i + 1, 1)
                weights(2 * i + 2, 0)
            weights(NE - 1, 1)
            for k in range(2):
                expert_piece(6 * NE - 2 + k, ER - 2 + k, wd[NE - 1, k])
            sp.wait_ge(xet_ps, NE)
            sp.wait_ge(ehi_ok, 6 * NE - 6)
            sp.wait_ge(elo_ok, 6 * NE - 6)
            sp.dma_start(hall[:, :, :], h_dram.rearrange("(t r) d -> r t d", r=TR)).then_inc(h_back, 16)
            sp.dma_start(lng[:, :], a["ln2_g"].broadcast_to([P, D])).then_inc(ln2_in, 16)
            sp.dma_start(lnb[:, :], a["ln2_b"].broadcast_to([P, D])).then_inc(ln2_in, 16)
            sp.wait_ge(over_ok, 1)
            n_over = sp.value_load(ove[0:1, 8:9], min_val=0, max_val=NOVER)
            with sp.If(n_over > 0):
                with sp.Fori(0, NOVER) as j:
                    e = sp.value_load(ove[0:1, bass.ts(j, 1)], min_val=0, max_val=NE - 1)
                    with sp.If(j < n_over):
                        for k, w in enumerate((wg, wg, wu, wu, wd, wd)):
                            sp.wait_ge(ehi_ok, 6 * NE + 6 * j + k - 5)
                            sp.wait_ge(elo_ok, 6 * NE + 6 * j + k - 5)
                            sp.dma_start(eraw[6 + k][:, :], of(w, e, k % 2)).then_inc(eraw_in[6 + k], 16)
            for t in range(TT):
                if t < TT - 1:
                    sp.wait_ge(f_done, t + 1)
                else:
                    sp.wait_ge(f_last, 3)
                n = min(TR, SEQ - t * TR)
                sp.dma_start(o["y_prompt"][t * TR:t * TR + n, :], res[t][0:n, :]).then_inc(f_sent, 16)
                if n < TR:
                    sp.dma_start(o["y_sample"], res[t][n:TR, :]).then_inc(f_sent, 16)
            sp.wait_ge(f_sent, 16 * (TT + 1))
            sp.wait_ge(copied, 16 * 7)
            sp.wait_ge(rows_sent, 16 * 4)

        @block.scalar
        def _(ac):
            ac.wait_ge(xt_ps, 1)
            ac.activation(xhi[:, 0:KD * T].rearrange("p (k t) -> p k t", k=KD)[:, :, SEQ:T],
                          ps[:, 3, 0:KD * NS].rearrange("p (k t) -> p k t", k=KD), ACT.Copy).then_inc(xt_hi, 1)

            def split(n, s, width, arrived, first=False, out=None):
                ac.wait_ge(raw_in[s], arrived)
                if not first:
                    ac.wait_ge(piece_used, n - 1)
                ac.activation(whi[s][:, 0:width] if out is None else out, raw[s][:, 0:width], ACT.Copy)\
                  .then_inc(hi_split, 1)

            def z_tile(t, s):
                ac.activation(z[:, bass.ds(t, 1), :].rearrange("p a (h c) -> p (a h) c", h=2), pair(s),
                              ACT.Copy).then_inc(z_out, 1)

            for k in range(KD):
                if k == 4:
                    split(0, 0, PW, 16, True)
                ac.wait_ge(xt_ps, k + 2)
                ac.activation(xhi[:, k * T:k * T + SEQ], ps[:, 4 + k % 4, :], ACT.Copy).then_inc(xt_hi, 1)
            split(1, 1, PW, 16, True)

            def z_pair(i, j):
                ac.wait_ge(z_even, 2 * i + j + 1)
                z_tile(4 * i + 2 * j, 0)
                ac.wait_ge(piece_used, 2 * i + j + 1)
                z_tile(4 * i + 2 * j + 1, 1)

            for j in range(2):
                ac.wait_ge(z_even, j + 1)
                ac.activation(z[:, 2 * j, :].rearrange("p (h c) -> p h c", h=2), pair(0), ACT.Copy).then_inc(z_out, 1)
                ac.wait_ge(piece_used, j + 1)
                ac.activation(z[:, 2 * j + 1, :].rearrange("p (h c) -> p h c", h=2), pair(1), ACT.Copy).then_inc(z_out, 1)
                split(j + 2, j, PW, 32)
            ac.wait_ge(st_ps, 1)
            ac.activation(pext[:, :, :, :].rearrange("p g b r -> p (g b) r")[:, :, 0:PST],
                          ps[:, 7, 0:4 * NS * PST].rearrange("p (g r) -> p g r", r=PST), ACT.Copy).then_inc(st_out, 1)
            with ac.Fori(1, ZP // 2 - 1) as i:
                for j in range(2):
                    z_pair(i, j)
                    split(2 * i + j + 2, j, PW, 16 * i + 32)
            i = ZP // 2 - 1
            z_pair(i, 0)
            split(N_V, 0, PW, 16 * i + 32)
            z_pair(i, 1)

            def mixed(g):
                ac.wait_ge(mix_ps, g + 1)
                ac.activation(halves(obhi[:, g, :]), pair(g % 2), ACT.Identity,
                              scale=prm[:, Q_PSC + g:Q_PSC + g + 1]).then_inc(mix_hi, 1)

            def memt(k):
                ac.wait_ge(xt_ps, KD + 2 + k)
                ac.activation(mthi[:, 2 * k:2 * k + 2, :], ps[:, 4 + k, :].rearrange("p (k m) -> p k m", k=2),
                              ACT.Copy).then_inc(xt_hi, 1)

            ac.wait_ge(con_in, 64)
            for n in range(2):
                for k in range(2):
                    mixed(2 * n + k)
                for k in range(2):
                    memt(2 * n + k)
            split(N_M, 1, PW, 16 * i + 32)
            ac.wait_ge(z_sent, 16 * NOVER)
            for k in range(2):
                ac.wait_ge(v_ps, k + 1)
                ac.activation(v[:, 2 * k:2 * k + 2, :], ps[:, 4 + k, :].rearrange("p (b d) -> p b d", b=2),
                              ACT.Copy).then_inc(v_out, 1)
            ac.wait_ge(piece_used, N_V + 1)
            ac.activation(v[0:NS, NB, :], ps[0:NS, 6, 0:256], ACT.Copy).then_inc(v_out, 1)
            split(N_M + 1, 0, PW, 16 * ((N_M + 1) // 2 + 1))
            ac.wait_ge(row_ps, 2)
            ac.activation(kvrow[:, 0:256], ps[:, 6, 0:256], ACT.Copy).then_inc(row_out, 1)
            ac.activation(kvrow[0:NS, 256:512], ps[0:NS, 6, 256:512], ACT.Copy).then_inc(row_out, 1)
            ac.wait_ge(row_ps, 3)
            ac.activation(urow[0:PST + NS, :], ps[0:PST + NS, 7, :], ACT.Copy).then_inc(row_out, 1)

            def exps(g):
                kind, b, h = groups[g]
                s, w = g % 2, P if kind == "swa" and b == 0 else 2 * P
                ac.wait_ge(sc_neg, g + 1)
                for j in range(GRP):
                    last = ac.activation(probs[s][:, j, 0:w], probs[s][:, j, 0:w], ACT.Exp, bias=stat[:, s, 1, j:j + 1],
                                         accum_out=stat[:, s, 3, j:j + 1])
                if kind == "swa":
                    ac.wait_ge(sc_snk, g + 1)
                    last = ac.activation(stat[:, s, 4, :], stat[:, s, 2, :], ACT.Exp)
                last.then_inc(sc_exp, 1)

            def quadrants(dst, src):
                for r in range(2):
                    last = ac.activation(dst[64 * r:64 * r + 64], src[64 * r:64 * r + 64, r], ACT.Copy)
                return last

            def sample(i):
                if i == S_T2:
                    ac.wait_ge(sw_ps, 3)
                    ac.activation(pcol[:, :], ps[:, 7, 0:P], ACT.Copy)
                    ac.activation(pnew[0:NS, :], ps[0:NS, 7, P:2 * P], ACT.Copy).then_inc(sw_act, 1)
                if i == S_OUT:
                    ac.wait_ge(sw_ps, 4)
                    quadrants(oahi[:, :, SEQ:T].rearrange("q (p j) b -> q p j b", p=2),
                              ps[:, 7, 3 * P:4 * P].rearrange("q (p a b j) -> q a p j b", p=2, a=2, b=NS))\
                        .then_inc(sw_act, 1)
                if i == M_T2:
                    ac.wait_ge(sm_ps, 2)
                    ac.activation(pcol[:, 0:64], ps[:, 3, 3 * P:3 * P + 64], ACT.Copy).then_inc(sm_act, 1)
                if i == M_OUT:
                    ac.wait_ge(sm_ps, 3)
                    quadrants(ochi[:, :, SEQ:T], ps[:, 3, 3 * P + 64:3 * P + 96].rearrange("q (t a b) -> q a t b", t=2, a=2))\
                        .then_inc(sm_act, 1)
                if i == 1:
                    ac.wait_ge(mkt_ps, 1)
                    ac.wait_ge(pads, 5)
                    for r, dst in ((0, mkt), (64, mkodd)):
                        ac.activation(dst[r:r + 64, :, :], ps[r:r + 64, 3, :].rearrange("p (t m) -> p t m", t=2),
                                      ACT.Copy).then_inc(mkt_out, 1)
                if i < NKT:
                    ac.wait_ge(kt_ps, i + 1)
                    if i:
                        ac.wait_ge(ks_ps, i)
                    ac.activation(kt[:, :], ps[:, 2, :], ACT.Copy).then_inc(kt_ok, 1)
                if i == 4:
                    ac.wait_ge(rows_sent, 64)
                    ac.wait_ge(sw_ps, 1)
                    ac.activation(scol[:, :], ps[:, 7, 0:P + NS], ACT.Copy).then_inc(sw_act, 1)
                if i == NKT:
                    ac.wait_ge(ks_ps, NKT)
                    ac.activation(scol[:, 0:64], ps[:, 3, 0:64], ACT.Copy).then_inc(sm_act, 1)

            def sample_exps(i):
                if i == S_T1:
                    ac.wait_ge(rows_sent, 64)
                    ac.wait_ge(sw_dve, 7)
                    ac.activation(srow[:, 0:WIN + 1], srow[:, 0:WIN + 1], ACT.Exp, bias=sstat[:, 1:2],
                                  accum_out=sstat[:, 3:4])
                    ac.activation(sstat[:, 4:5], sstat[:, 2:3], ACT.Exp).then_inc(sw_act, 1)
                if i == M_T1:
                    ac.wait_ge(sm_dve, 2)
                    ac.activation(srow[0:32, 0:NMEM], ps[0:32, 3, P:P + NMEM], ACT.Exp, bias=sstat[0:32, 1:2],
                                  scale=SCALE, accum_out=sstat[0:32, 3:4]).then_inc(sm_act, 1)

            def half_split(j, half):
                n, c = N_G + j, slice(half * (MPW // 2), (half + 1) * (MPW // 2))
                if half == 0:
                    ac.wait_ge(raw_in[n % 2], 16 * (n // 2 + 1))
                    if j == 0:
                        ac.wait_ge(kt_ps, NKT)
                    else:
                        ac.wait_ge(sm_ps, 3)
                last = ac.activation(whi[n % 2][:, c], raw[n % 2][:, c], ACT.Copy)
                if half:
                    last.then_inc(hi_split, 1)

            exps(0)
            ac.wait_ge(piece_used, N_M + 2)
            for m in range(2):
                ac.activation(mkv[:, m, :], ps[:, (5, 4)[m], :], ACT.Copy).then_inc(mkv_out, 1)
            for g, (kind, b, h) in enumerate(groups):
                if g + 1 < NGR:
                    exps(g + 1)
                if g:
                    sample(g - 1)
                if not narrow(g):
                    ac.wait_ge(pt_ps, g + 1)
                    ac.wait_ge(o_ps, g)
                    ac.activation(pt[:, 0, :], ps[:, 4, :], ACT.Copy).then_inc(pt_act, 1)
                ac.wait_ge(o_ps, g + 1)
                if kind == "swa":
                    r, p = 64 * (h % 2), h // 2
                    ac.activation(oahi[r:r + 64, 4 * p:4 * p + 4, b * P:b * P + P],
                                  ps[r:r + 64, 6, :].rearrange("p (j q) -> p j q", j=4), ACT.Copy).then_inc(o_hi, 1)
                else:
                    quadrants(ochi[:, :, b * P:b * P + P],
                              ps[:, 6, :].rearrange("p (a t q) -> p a t q", a=2, t=2)).then_inc(o_hi, 1)
                sample_exps(g - 1)
                if g in HALF_A:
                    half_split(0, HALF_A.index(g))
                if g == LAST:
                    half_split(1, 0)
                    half_split(1, 1)

            def wo_split(j):
                n = N_O + j
                split(n, n % 2, PW, 16 * (n // 2 + 1), True,
                      out=wohi[:, 2 * j:2 * j + 2, :].rearrange("p k n -> p (k n)"))

            def merge(i, more):
                for s in range(3):
                    ac.wait_ge(prod_ps, 5 * i + s + 1)
                    ac.activation(halves(gate[s][:, :]), pair(s), ACT.Sigmoid).then_inc(gate_out, 1)
                    if s == 1 and more:
                        split(2 * i + N_G + 2, N_G % 2, MPW, 16 * i + 16 * ((N_G + 2) // 2 + 1))
                if more:
                    split(2 * i + N_G + 3, (N_G + 1) % 2, MPW, 16 * i + 16 * ((N_G + 3) // 2 + 1))
                else:
                    wo_split(0)
                    wo_split(1)
                ac.wait_ge(m_val, i + 1)
                ac.activation(mhi[:, bass.ds(i, 1), :].rearrange("p a c -> p (a c)"), mval[:, :], ACT.Copy)\
                  .then_inc(m_hi, 1)

            with ac.Fori(0, KD - 1) as i:
                merge(i, True)
            merge(KD - 1, False)
            wo_split(2)
            wo_split(3)
            def turned(t):
                ac.wait_ge(ht_ps, t + 1)
                if t:
                    ac.wait_ge(lg_ps, t)
                ac.activation(ht[:, :, :].rearrange("p (a k) c -> p a (k c)", a=2), ps[:, 4:6, 0:4 * TR], ACT.Copy)\
                  .then_inc(ht_out, 1)

            for t in range(TT):
                ls = lstat[t % 2][0:TR]
                ac.wait_ge(h_stat, 4 * t + 4)
                ac.activation(ls[:, 15:16], ls[:, 14:15], ACT.Sqrt).then_inc(h_root, 1)
                ac.wait_ge(h_fac, 5 * t + 5)
                ac.activation(hall[:, t, :], hall[:, t, :], ACT.Identity, bias=ls[:, 20:21], scale=ls[:, 18:19])\
                  .then_inc(h_nrm, 1)
                if t == 0:
                    continue
                turned(t - 1)
            turned(TT - 1)

            def esplit(n, s, arrived, first=False):
                ac.wait_ge(eraw_in[s], arrived)
                if not first:
                    ac.wait_ge(e_used, n - 2)
                ac.activation(ehi[s % 3][:, :], eraw[s][:, :], ACT.Copy).then_inc(ehi_ok, 1)

            def xet(c):
                ac.wait_ge(xet_ps, c + 1)
                ac.activation(xethi[:, :, :].rearrange("p (a k) c -> p a (k c)", a=2), ps[:, 4:6, :], ACT.Copy)\
                  .then_inc(xet_hi, 1)

            def gated(c, ready):
                ac.wait_ge(e_used, ready)
                ac.activation(sig[:, :], ps[:, 0, :], ACT.Sigmoid).then_inc(sig_ok, 1)

            def hidt(c):
                ac.wait_ge(hidt_ps, c + 1)
                ac.activation(hthi[:, :, :].rearrange("p j c -> p (j c)"), ps[:, 6, :], ACT.Copy).then_inc(hidt_hi, 1)

            def y_copy(q, ready, sent=None):
                ac.wait_ge(e_used, ready)
                if sent is not None:
                    ac.wait_ge(y_sent[q], sent)
                ac.activation(yout[q][:, :].rearrange("p (h n) -> p h n", h=2), ps[:, 2:4, :], ACT.Copy).then_inc(y_out, 1)

            def y_send(c, q):
                ac.wait_ge(y_out, c + 1)
                ac.dma_start(y_dram[bass.ds(c * CAP, CAP), :], yout[q][:, :]).then_inc(y_sent[q], 16)

            def expert(i, odd, y=True, more=True):
                e = 2 * i + odd

                def piece(e, k):
                    esplit(6 * e + k, 6 * odd + k, 16 * i + 16)

                piece(e, 0)
                if y:
                    y_copy(odd, 6 * e - 2, None if y == "first" else 16 * i - 16)
                piece(e, 1)
                if y:
                    y_send(e - 2, odd)
                gated(e, 6 * e)
                hidt(e - 1)
                piece(e, 2)
                piece(e, 3)
                if more:
                    xet(e + 1)
                piece(e, 4)
                piece(e, 5)

            ac.wait_ge(h_ps, TT)
            for n in range(3):
                esplit(n, n, 16, True)
            ac.wait_ge(gd_ok, 1)
            ac.activation(gd[:, :, :], gd[:, :, :], ACT.Exp).then_inc(r_exp, 1)
            ac.wait_ge(dist_ok, 1)
            ac.activation(m2[:, :], m2[:, :], ACT.Exp).then_inc(r_exp, 1)
            xet(0)
            esplit(3, 3, 16)
            gated(0, 2)
            esplit(4, 4, 16)
            esplit(5, 5, 16)
            xet(1)
            expert(0, 1, False)
            for odd in range(2):
                expert(1, odd, "first")
            with ac.Fori(2, NE // 2 - 1) as i:
                expert(i, 0)
                expert(i, 1)
            expert(NE // 2 - 1, 0)
            expert(NE // 2 - 1, 1, True, False)
            hidt(NE - 1)
            for q in range(2):
                y_copy(q, 6 * NE - 2 + 2 * q, 16 * (NE // 2 - 1))
                y_send(NE - 2 + q, q)
            ac.wait_ge(over_ok, 1)
            n_over = ac.value_load(ove[0:1, 8:9], min_val=0, max_val=NOVER)
            with ac.If(n_over > 0):
                with ac.Fori(0, NOVER) as j:
                    with ac.If(j < n_over):
                        n, c = 6 * j + 6 * NE, j + NE
                        xet(c)
                        arrived = 16 * j + 16 * (NE // 2 + 1)
                        for k in range(4):
                            esplit(n + k, 6 + k, arrived)
                        gated(c, n + 2)
                        for k in range(4, 6):
                            esplit(n + k, 6 + k, arrived)
                        hidt(c)
                        y_copy(0, n + 6, 16 * j + 16 * (NE // 2))
                        y_send(c, 0)
            ac.wait_ge(y_sent[1], 16 * (NE // 2))
            ac.wait_ge(y_sent[0], 16 * n_over + 16 * (NE // 2))
            ac.sem_inc(moe_done, 1)
            def weighted(t):
                ac.wait_ge(ya_in[t], 32)
                ac.activation(ya[t][:, :], ya[t][:, :], ACT.Identity, scale=w1[:, t:t + 1]).then_inc(ya_w, 1)

            weighted(0)
            weighted(1)
            for t in range(TT):
                ls = lstat[t % 2][0:TR]
                ac.wait_ge(f_stat, 4 * t + 4)
                ac.activation(ls[:, 15:16], ls[:, 14:15], ACT.Sqrt).then_inc(f_root, 1)
                if t + 2 < TT:
                    weighted(t + 2)
                ac.wait_ge(f_fac, 5 * t + 5)
                ac.activation(res[t][:, :], res[t][:, :], ACT.Identity, bias=ls[:, 20:21],
                              scale=ls[:, 18:19]).then_inc(f_nrm, 1)

        @block.tensor
        def _(pe):
            pe.wait_ge(id_in, 16)
            pe.wait_ge(x_in, 16 * (NB + 1))
            for k in range(KD):
                last = pe.transpose(ps[:, 3, k * NS:k * NS + NS], xsam[:, k * P:k * P + P], ident[0:NS, 0:NS])
            last.then_inc(xt_ps, 1)
            for k in range(KD):
                if k >= 4:
                    pe.wait_ge(xt_hi, k - 2)
                    pe.wait_ge(xt_lo, k - 2)
                for t in range(NB):
                    last = pe.transpose(ps[:, 4 + k % 4, t * P:t * P + P], xtok[:, t, k * P:k * P + P], ident)
                last.then_inc(xt_ps, 1)

            def product(outs, parts, start=True, stop=True, first=False):
                for n, out in enumerate(outs):
                    for k, (sh, sl, mh, ml) in enumerate(parts):
                        if first and n == 0:
                            pe.wait_ge(xt_hi, k + 2)
                            pe.wait_ge(xt_lo, k + 2)
                        pe.matmul(out, sh, mh[n], start=start and k == 0, stop=False)
                        pe.matmul(out, sl, mh[n], start=False, stop=False)
                        last = pe.matmul(out, sh, ml[n], start=False, stop=stop and k == len(parts) - 1)
                return last

            def cols(w, n):
                return w[:, n * P:n * P + P]

            def by_half(ap):
                return [ap[:, 0:TH], ap[:, TH:T]]

            def tokens(s):
                return [ps[:, 2 * s + h, 0:TH] for h in range(2)]

            def xk(t, k):
                return by_half(t[:, k * T:k * T + T])

            def z_piece(n, s, first=False):
                pe.wait_ge(lo_split, n + 1)
                for u in range(2):
                    if not first:
                        pe.wait_ge(z_out, 2 * n + u - 1)
                    last = product(tokens(u), [(cols(whi[s], 8 * u + k), cols(wlo[s], 8 * u + k), xk(xhi, k), xk(xlo, k))
                                               for k in range(KD)], first=first and u == 0)
                    last.then_inc(piece_used if u else z_even, 1)

            z_piece(0, 0, True)
            z_piece(1, 1)
            pe.wait_ge(st_in, 16)
            n = NS * PST
            for g in range(4):
                last = pe.transpose(ps[:, 7, g * n:g * n + n], pstate[:, g * P:g * P + P], ident[0:n, 0:n])
            last.then_inc(st_ps, 1)
            with pe.Fori(1, ZP // 2) as i:
                for j in range(2):
                    z_piece(2 * i + j, j)
            pe.wait_ge(m_in, 16)
            pe.wait_ge(st_out, 1)
            for g in range(4):
                for u in range(4):
                    last = pe.transpose(ps[:, 4 + g, u * P:u * P + P],
                                        mtok[:, u % 2, (2 * g + u // 2) * P:(2 * g + u // 2) * P + P], ident)
                last.then_inc(xt_ps, 1)
            pe.wait_ge(con_in, 64)
            for g in range(4):
                pe.wait_ge(pooled_in, g + 1)
                if g < 2:
                    pe.wait_ge(z_out, ZT - 1 + g)
                else:
                    pe.wait_ge(mix_hi, g - 1)
                    pe.wait_ge(mix_lo, g - 1)
                for h in range(2):
                    last = pe.matmul(ps[:, 2 * (g % 2) + h, 0:TH], wmix[:, g, :],
                                     pooled[:, g, h * TH:h * TH + TH], start=True, stop=True)
                last.then_inc(mix_ps, 1)

            def rotate(r):
                if r < 2:
                    pe.wait_ge(mix_hi, r + 3)
                    pe.wait_ge(mix_lo, r + 3)
                else:
                    pe.wait_ge(rot_mul, r - 1)
                for h in range(2):
                    last = pe.matmul(ps[:, 2 * (r % 2) + h, 0:TH], con[:, C_ROT:C_ROT + P],
                                     z[:, ROT[r], h * TH:h * TH + TH], start=True, stop=True)
                last.then_inc(rot_ps, 1)

            pe.wait_ge(xt_hi, KD + 5)
            pe.wait_ge(xt_lo, KD + 5)
            pe.wait_ge(pad_zero, 2)
            pe.wait_ge(lo_split, N_V + 1)
            for b in range(NB + 1):
                out = ps[:, 4 + b // 2, (b % 2) * 256:(b % 2) * 256 + 256]
                last = product([out], [(xhi[:, k * T + b * P:k * T + b * P + P], xlo[:, k * T + b * P:k * T + b * P + P],
                                        [whi[0][:, k * 256:k * 256 + 256]], [wlo[0][:, k * 256:k * 256 + 256]])
                                       for k in range(KD)])
                if b % 2:
                    last.then_inc(v_ps, 1)
                if b == NB:
                    last.then_inc(piece_used, 1)
                rotate(b)
            pe.wait_ge(roped, 2)
            pe.wait_ge(v_out, 3)
            for p in range(2):
                last = pe.transpose(ps[:, 6, p * P:p * P + P], z[:, ZK + p, SEQ - P:SEQ], ident)
            last.then_inc(row_ps, 1)
            for p in range(2):
                last = pe.transpose(ps[0:NS, 6, 256 + p * P:256 + p * P + P], z[:, ZK + p, SEQ:T], ident)
            last.then_inc(row_ps, 1)
            for g in range(4):
                last = pe.transpose(ps[0:PST + NS, 7, g * P:g * P + P], z[:, ZU + g, SEQ - PST:T], ident)
            last.then_inc(row_ps, 1)

            def memory(j, m):
                n = N_M + j
                pe.wait_ge(lo_split, n + 1)
                last = product([ps[:, (5, 4)[m], :]],
                               [(mthi[:, 4 * j + k, m * P:m * P + P], mtlo[:, 4 * j + k, m * P:m * P + P],
                                 [whi[n % 2][:, k * 512:k * 512 + 512]], [wlo[n % 2][:, k * 512:k * 512 + 512]])
                                for k in range(4)], start=j == 0, stop=j == 1)
                if m == 1:
                    last.then_inc(piece_used, 1)

            for n, (j, m) in enumerate(((0, 0), (0, 1), (1, 0))):
                memory(j, m)
                rotate(NB + 1 + n)
            rotate(8)

            A, B = N_G % 2, (N_G + 1) % 2
            PRODUCTS = ((None, None, KD),) * 3 + ((oahi, oalo, 8), (obhi, oblo, 4), (ochi, oclo, 2))

            def block_of(n):
                return (A, n) if n < MT // 2 else (B, n - MT // 2)

            def merge(i, products=range(6), first=False):
                for u in products:
                    hi, lo, nk = PRODUCTS[u]
                    n = sum(w[2] for w in PRODUCTS[:u])
                    if u == 0:
                        pe.wait_ge(lo_split, 2 * i + N_G + 1)
                    if first:
                        if u == 0:
                            pe.wait_ge(sc_row, NGR)
                        if u == 1:
                            pe.wait_ge(sm_act, 4)
                            pe.wait_ge(sm_dve, 5)
                        if u == 2:
                            pe.wait_ge(pt_act, act_copies(NGR))
                            pe.wait_ge(pt_dve, NGR)
                        if u == 3:
                            pe.wait_ge(o_hi, NGR)
                            pe.wait_ge(o_lo, NGR)
                    else:
                        if u == 0:
                            pe.wait_ge(m_step, 4 * i - 3)
                        if u == 1:
                            pe.wait_ge(m_step, 4 * i - 1)
                        if u == 2:
                            pe.wait_ge(m_val, i)
                    if u >= 3:
                        pe.wait_ge(gate_out, 3 * i + u - 2)
                    for half in range(2):
                        for k in range(nk):
                            s, q = block_of(n + k)
                            if s == B and half == 0 and q == 0:
                                pe.wait_ge(lo_split, 2 * i + N_G + 2)
                            if u < 3:
                                mh, ml = xk(xhi, k)[half], xk(xlo, k)[half]
                            else:
                                mh, ml = by_half(hi[:, k, :])[half], by_half(lo[:, k, :])[half]
                            out = ps[:, 2 * (u % 3) + half, 0:TH]
                            pe.matmul(out, cols(whi[s], q), mh, start=k == 0, stop=False)
                            pe.matmul(out, cols(wlo[s], q), mh, start=False, stop=False)
                            last = pe.matmul(out, cols(whi[s], q), ml, start=False, stop=k == nk - 1)
                            if half == 1 and n + k == MT // 2 - 1:
                                last.then_inc(piece_used, 1)
                    last.then_inc(prod_ps if u < 5 else piece_used, 1)

            def scores(g):
                kind, b, h = groups[g]
                if g:
                    pe.wait_ge(sc_row, g)
                if g == 2 * NB:
                    pe.wait_ge(roped, 10)
                if g == NKV * NB:
                    pe.wait_ge(mkt_out, 2)
                for j in range(GRP):
                    if kind == "swa":
                        p = h // 2
                        k0, w = (0, P) if b == 0 else ((b - 1) * P, 2 * P)
                        q = z[:, ZQ + 4 * p + j, b * P:b * P + P]
                        k = (kodd[:, p, k0:k0 + w] if h % 2 else z[:, ZK + p, k0:k0 + w])
                    else:
                        m, w = MEM_ORDER[j], NMEM
                        q, k = z[:, ZC + m // 2, b * P:b * P + P], (mkodd if m % 2 else mkt)[:, m // 2, :]
                    last = pe.matmul(ps[:, j // 2, (j % 2) * 256:(j % 2) * 256 + w], q, k, start=True, stop=True)
                last.then_inc(sc_ps, 1)

            def sample_keys(n):
                if n == 0:
                    pe.wait_ge(rot_mul, 10)
                    pe.wait_ge(win_in, 16)
                else:
                    pe.wait_ge(kt_ok, n)
                b = n - 4
                if n == NS // 2:
                    pe.wait_ge(mkt_out, 2)
                if b >= 0:
                    pe.wait_ge(cm_in[b // 4], 32)
                for u in range(4):
                    src = cach_k[:, 2 * n + u // 2] if b < 0 else cm_k[b // 4][:, 2 * (b % 4) + u // 2]
                    last = pe.transpose(ps[:, 2, u * P:u * P + P], src[:, (u % 2) * P:(u % 2) * P + P], ident)
                last.then_inc(kt_ps, 1)

            def sample_scores(n):
                pe.wait_ge(kt_ok, n + 1)
                if n == 0:
                    pe.wait_ge(qs_ok, 3)
                    pe.wait_ge(row_out, 3)
                for u in range(4):
                    if n < 4:
                        b, p = 2 * n + u // 2, u % 2
                        out = ps[:, 7, 64 * p:64 * p + 64].rearrange("q (a b j) -> q a b j", a=2, b=NS)[:, :, b, :]
                        last = pe.matmul(out, kt[:, u * P:u * P + P], qsp[:, p, :, b, :], start=True, stop=True)
                    else:
                        b, k, t = n - 4, u // 2, u % 2
                        out = ps[:, 3, 32 * k + 16 * t:32 * k + 16 * t + 16].rearrange("q (a b) -> q a b", a=2)[:, :, b]
                        last = pe.matmul(out, kt[:, u * P:u * P + P], cqp[:, t, :, b], start=True, stop=True)
                last.then_inc(ks_ps, 1)

            def sample(i):
                if 1 <= i <= NKT:
                    sample_scores(i - 1)
                if i == 1:
                    pe.wait_ge(rot_mul, 10)
                    for t in range(2):
                        for m in range(2):
                            last = pe.transpose(ps[:, 3, t * 256 + m * P:t * 256 + m * P + P],
                                                mkv[:, m, t * P:t * P + P], ident)
                    last.then_inc(mkt_ps, 1)
                if i == 4:
                    for p in range(2):
                        last = pe.matmul(ps[64 * p:64 * p + 64, 7, P:P + NS],
                                         qsp[:, p, :, :, :].rearrange("q a b j -> q (a b j)"), kns[:, p, :],
                                         start=True, stop=True)
                    last.then_inc(sw_ps, 1)
                if i == S_T1:
                    pe.wait_ge(sw_act, 1)
                    pe.transpose(ps[:, 7, 2 * P:3 * P], scol[:, 0:P], ident).then_inc(sw_ps, 1)
                if i == S_T2:
                    pe.wait_ge(sw_dve, 11)
                    pe.transpose(ps[:, 7, 0:P], srow[:, 0:P], ident)
                    pe.transpose(ps[0:NS, 7, P:2 * P], sstat[:, 8:16], ident).then_inc(sw_ps, 1)
                if i == S_PV:
                    pe.wait_ge(sw_act, 3)
                    pe.wait_ge(winv_in, 16)
                    for p in range(2):
                        out = ps[:, 7, 3 * P + 64 * p:3 * P + 64 * p + 64]
                        pe.matmul(out, v[0:NS, NB, p * P:p * P + P], pnew[0:NS, 64 * p:64 * p + 64],
                                  start=p == 0, stop=False, skip_group_check=True)
                if S_PV <= i <= S_OUT:
                    for p in range(2):
                        out = ps[:, 7, 3 * P + 64 * p:3 * P + 64 * p + 64].rearrange("q (a b j) -> q a b j", a=2, b=NS)
                        prob = pcol[:, 64 * p:64 * p + 64].rearrange("q (a b j) -> q a b j", a=2, b=NS)
                        for b in range(2 * (i - S_PV), 2 * (i - S_PV) + 2):
                            last = pe.matmul(out[:, :, b, :], cach_v[:, b, p * P:p * P + P], prob[:, :, b, :],
                                             start=False, stop=b == NS - 1, skip_group_check=True)
                    if i == S_OUT:
                        last.then_inc(sw_ps, 1)
                if i == M_T1:
                    pe.wait_ge(sm_act, 1)
                    for k in range(2):
                        last = pe.transpose(ps[0:32, 3, P + k * P:2 * P + k * P], scol[:, 32 * k:32 * k + 32], ident)
                    last.then_inc(sm_ps, 1)
                if i == M_T2:
                    pe.wait_ge(sm_dve, 4)
                    for k in range(2):
                        last = pe.transpose(ps[:, 3, 3 * P + 32 * k:3 * P + 32 * k + 32], srow[0:32, k * P:k * P + P],
                                            ident[0:32, 0:32])
                    last.then_inc(sm_ps, 1)
                if M_PV <= i <= M_OUT:
                    if i == M_PV:
                        pe.wait_ge(sm_act, 3)
                        pe.wait_ge(cmv_in, 64)
                    for b in range(4 * (i - M_PV), 4 * (i - M_PV) + 4):
                        for t in range(2):
                            c = 3 * P + 64 + 16 * t
                            for k in range(2):
                                prob = pcol[:, 32 * k + 16 * t:32 * k + 16 * t + 16].rearrange("q (a b) -> q a b", a=2)
                                last = pe.matmul(ps[:, 3, c:c + 16].rearrange("q (a b) -> q a b", a=2)[:, :, b],
                                                 cm_v[b // 4][:, 2 * (b % 4) + k, t * P:t * P + P], prob[:, :, b],
                                                 start=k == 0, stop=k == 1)
                    if i == M_OUT:
                        last.then_inc(sm_ps, 1)
                if i < NKT:
                    sample_keys(i)

            pe.wait_ge(rot_mul, 9)
            pe.wait_ge(roped, 6)
            pe.wait_ge(kodd_ok, 1)
            pe.wait_ge(pads, 4)
            scores(0)
            rotate(9)
            memory(1, 1)
            scores(1)
            for g, (kind, b, h) in enumerate(groups):
                nk = 1 if kind == "swa" and b == 0 else 2
                pe.wait_ge(sc_nrm, g + 1)
                if g:
                    if act_copies(g):
                        pe.wait_ge(pt_act, act_copies(g))
                    pe.wait_ge(pt_dve, g)
                else:
                    pe.wait_ge(mkv_out, 2)
                for k in range(nk):
                    for j in range(GRP):
                        last = pe.transpose(ps[:, 4 + k, j * P:j * P + P], probs[g % 2][:, j, k * P:k * P + P], ident)
                last.then_inc(pt_ps, 1)
                if g + 2 < NGR:
                    scores(g + 2)
                else:
                    merge(0, (g + 2 - NGR,), True)
                if not narrow(g):
                    pe.wait_ge(pt_act, act_copies(g + 1))
                pe.wait_ge(pt_dve, g + 1)
                if g:
                    pe.wait_ge(o_hi, g)
                    pe.wait_ge(o_lo, g)
                else:
                    pe.wait_ge(row_out, 3)
                if kind == "swa":
                    for k in range(nk):
                        last = pe.matmul(ps[:, 6, :], v[:, b - nk + 1 + k, (h // 2) * P:(h // 2) * P + P], pt[:, k, :],
                                         start=k == 0, stop=k == nk - 1)
                else:
                    for j, m in enumerate(MEM_ORDER):
                        for k in range(2):
                            last = pe.matmul(ps[:, 6, j * P:j * P + P],
                                             mkv[:, k, 256 + (m // 2) * P:256 + (m // 2) * P + P],
                                             pt[:, k, j * P:j * P + P], start=k == 0, stop=k == 1)
                last.then_inc(o_ps, 1)
                sample(g)

            merge(0, range(2, 6), True)
            with pe.Fori(1, KD) as i:
                merge(i)

            def project(t):
                if t >= 2:
                    pe.wait_ge(h_sum, t - 1)
                for k in range(KD):
                    if t == 0:
                        pe.wait_ge(lo_split, N_O + k // 2 + 1)
                    for h in range(2):
                        out = ps[0:TR, 2 * (t % 2) + h, :]
                        mt = slice(t * TR, t * TR + TR)
                        pe.matmul(out, mhi[:, k, mt], wohi[:, k, h * 512:h * 512 + 512], start=k == 0, stop=False)
                        pe.matmul(out, mlo[:, k, mt], wohi[:, k, h * 512:h * 512 + 512], start=False, stop=False)
                        last = pe.matmul(out, mhi[:, k, mt], wolo[:, k, h * 512:h * 512 + 512], start=False,
                                         stop=k == KD - 1)
                last.then_inc(h_ps, 1)

            def route(t):
                if t < TT - 1:
                    pe.wait_ge(h_done, t + 1)
                else:
                    pe.wait_ge(h_last, 2)
                if t:
                    pe.wait_ge(ht_out, t)
                for k in range(KD):
                    last = pe.transpose(ps[:, 4 + k // 4, (k % 4) * TR:(k % 4) * TR + TR],
                                        hall[:, t, k * P:k * P + P], ident[0:TR, 0:TR])
                last.then_inc(ht_ps, 1)
                pe.wait_ge(ht_out, t + 1)
                for k in range(KD):
                    last = pe.matmul(ps[0:TR, 6, t * 20:t * 20 + 20], ht[:, k, :], wrt[:, k, :],
                                     start=k == 0, stop=k == KD - 1)
                last.then_inc(lg_ps, 1)

            pe.wait_ge(m_hi, KD)
            pe.wait_ge(m_lo, KD)
            project(0)
            project(1)
            for t in range(TT):
                if t + 2 < TT:
                    project(t + 2)
                route(t)
            pe.wait_ge(both_ok, 1)
            flat = both[:, :, :].rearrange("p t n -> p (t n)")
            pe.matmul(ps[0:TR, 7, 0:TT * NE], upper, flat, start=True, stop=False, skip_group_check=True)
            for u in range(TT):
                last = pe.matmul(ps[0:TR, 7, (u + 1) * NE:(TT + 1) * NE].rearrange("p (t n) -> p t n", n=NE),
                                 ones[:, 0:TR], both[:, u:u + 1, :].broadcast_to([TR, TT - u, NE]),
                                 start=False, stop=u == TT - 1, skip_group_check=True)
            last.then_inc(rank_ps, 1)
            pe.wait_ge(list_ok, 2)
            for n in range(2 * TT):
                last = pe.matmul(ps[:, 6, P:P + NCH], rowhot[:, n // TT, n % TT, :], chunkr[:, n // TT, n % TT, :],
                                 start=n == 0, stop=n == 2 * TT - 1)
            last.then_inc(slot_ps, 1)

            def xet(c, q, arrived, first=False):
                pe.wait_ge(xe_in[q], arrived)
                if not first:
                    pe.wait_ge(xet_hi, c)
                    pe.wait_ge(xet_lo, c)
                for k in range(KD):
                    last = pe.transpose(ps[:, 4 + k // 4, (k % 4) * P:(k % 4) * P + P],
                                        xe[q][:, :].rearrange("p (c k) -> p k c", k=KD)[:, k, :], ident)
                last.then_inc(xet_ps, 1)

            def wide(n, s, bank, first=False, free=None):
                if free is not None:
                    pe.wait_ge(*free)
                for j in range(2):
                    pe.wait_ge(elo_ok, n + j + 1)
                    for q in range(4):
                        k, w = 4 * j + q, slice(q * 512, q * 512 + 512)
                        pe.matmul(ps[:, bank, :], xethi[:, k, :], ehi[s[j]][:, w], start=k == 0, stop=False)
                        pe.matmul(ps[:, bank, :], xetlo[:, k, :], ehi[s[j]][:, w], start=False, stop=False)
                        last = pe.matmul(ps[:, bank, :], xethi[:, k, :], elo[s[j]][:, w], start=False, stop=k == KD - 1)
                    last.then_inc(e_used, 1)

            def hidt(c, first=False):
                pe.wait_ge(hid_ok, c + 1)
                if not first:
                    pe.wait_ge(hidt_hi, c)
                    pe.wait_ge(hidt_lo, c)
                for j in range(4):
                    last = pe.transpose(ps[:, 6, j * P:j * P + P], hid[:, :].rearrange("p (c j) -> p j c", j=4)[:, j, :],
                                        ident)
                last.then_inc(hidt_ps, 1)

            def down(c, n, s, first=False):
                pe.wait_ge(hidt_hi, c + 1)
                pe.wait_ge(hidt_lo, c + 1)
                if not first:
                    pe.wait_ge(y_out, c)
                for j in range(2):
                    pe.wait_ge(elo_ok, n + j + 1)
                    for q in range(2):
                        f = 2 * j + q
                        for h in range(2):
                            w = slice(q * D + h * 512, q * D + h * 512 + 512)
                            pe.matmul(ps[:, 2 + h, :], hthi[:, f, :], ehi[s[j]][:, w], start=f == 0, stop=False)
                            pe.matmul(ps[:, 2 + h, :], htlo[:, f, :], ehi[s[j]][:, w], start=False, stop=False)
                            last = pe.matmul(ps[:, 2 + h, :], hthi[:, f, :], elo[s[j]][:, w], start=False, stop=f == 3)
                    last.then_inc(e_used, 1)

            def expert(i, odd, first=False, more=True):
                e = 2 * i + odd
                pe.wait_ge(xet_hi, e + 1)
                pe.wait_ge(xet_lo, e + 1)
                wide(6 * e - 2, (1, 2), 0, free=(act_ok, e))
                hidt(e - 1, first)
                wide(6 * e, (0, 1), 1, free=(hid_ok, e))
                if more:
                    xet(e + 1, 1 - odd, 16 * (i + odd) + 16)
                down(e - 1, 6 * e + 2, (2, 0), first)

            xet(0, 0, 16, True)
            pe.wait_ge(xet_hi, 1)
            pe.wait_ge(xet_lo, 1)
            wide(0, (0, 1), 0)
            wide(2, (2, 0), 1)
            xet(1, 1, 16)
            expert(0, 1, True)
            with pe.Fori(1, NE // 2 - 1) as i:
                expert(i, 0)
                expert(i, 1)
            expert(NE // 2 - 1, 0)
            expert(NE // 2 - 1, 1, more=False)
            hidt(NE - 1)
            down(NE - 1, 6 * NE - 2, (1, 2))
            pe.wait_ge(over_ok, 1)
            n_over = pe.value_load(ove[0:1, 8:9], min_val=0, max_val=NOVER)
            with pe.If(n_over > 0):
                with pe.Fori(0, NOVER) as j:
                    with pe.If(j < n_over):
                        n, c = 6 * j + 6 * NE, j + NE
                        xet(c, 0, 16 * j + 16 * (NE // 2) + 16)
                        pe.wait_ge(xet_hi, c + 1)
                        pe.wait_ge(xet_lo, c + 1)
                        wide(n, (0, 1), 0, free=(act_ok, c))
                        wide(n + 2, (2, 0), 1, free=(hid_ok, c))
                        hidt(c)
                        down(c, n + 4, (1, 2))
        @block.vector
        def _(ve):
            ve.wait_ge(xt_hi, 1)
            ve.tensor_tensor(xlo[:, 0:KD * T].rearrange("p (k t) -> p k t", k=KD)[:, :, SEQ:T],
                             ps[:, 3, 0:KD * NS].rearrange("p (k t) -> p k t", k=KD),
                             xhi[:, 0:KD * T].rearrange("p (k t) -> p k t", k=KD)[:, :, SEQ:T].bitcast(F32),
                             ALU.subtract).then_inc(xt_lo, 1)

            def split(n, s, width, first=False, out=None, hi=None):
                ve.wait_ge(hi_split, n + 1)
                if not first:
                    ve.wait_ge(piece_used, n - 1)
                ve.tensor_tensor(wlo[s][:, 0:width] if out is None else out, raw[s][:, 0:width],
                                 (whi[s][:, 0:width] if hi is None else hi).bitcast(F32), ALU.subtract)\
                  .then_inc(lo_split, 1)

            for k in range(KD):
                if k == 4:
                    split(0, 0, PW, True)
                ve.wait_ge(xt_hi, k + 2)
                ve.tensor_tensor(xlo[:, k * T:k * T + SEQ], ps[:, 4 + k % 4, :], xhi[:, k * T:k * T + SEQ].bitcast(F32),
                                 ALU.subtract).then_inc(xt_lo, 1)
            split(1, 1, PW, True)
            with ve.Fori(0, ZP // 2 - 1) as i:
                for j in range(2):
                    split(2 * i + j + 2, j, PW)
            split(N_V, 0, PW)
            ve.wait_ge(con_in, 64)
            ve.tensor_scalar(nsink[:, :], prm[:, 0:17], -1.0, None, ALU.mult).then_inc(prep, 1)
            for k in range(4):
                ve.wait_ge(mix_hi, k + 1)
                ve.scalar_tensor_tensor(halves(oblo[:, k, :]), pair(k % 2), prm[:, Q_PSC + k:Q_PSC + k + 1],
                                        halves(obhi[:, k, :].bitcast(F32)), ALU.mult, ALU.subtract).then_inc(mix_lo, 1)
                if k % 2:
                    for m in range(k - 1, k + 1):
                        ve.wait_ge(xt_hi, KD + 2 + m)
                        ve.tensor_tensor(mtlo[:, 2 * m:2 * m + 2, :], ps[:, 4 + m, :].rearrange("p (k m) -> p k m", k=2),
                                         mthi[:, 2 * m:2 * m + 2, :].bitcast(F32), ALU.subtract).then_inc(xt_lo, 1)
            split(N_M, 1, PW)

            def rotated(r, t):
                s = r % 2
                ve.wait_ge(rot_ps, r + 1)
                ve.tensor_tensor(halves(rtmp[s][:, :]), pair(s), halves(con[:, C_SIN:C_SIN + T]), ALU.mult)\
                  .then_inc(rot_mul, 1)
                ve.wait_ge(rot_mul, r + 1)
                ve.wait_ge(rot_cos, r + 1)
                ve.tensor_tensor(z[:, t, :], z[:, t, :], rtmp[s][:, :], ALU.add).then_inc(roped, 1)
                if r == 4:
                    split(N_M + 1, 0, PW)
                if r == 5:
                    ve.wait_ge(roped, 2)
                    ve.wait_ge(pads, 2)
                    ve.tensor_copy(kodd[64:P, :, :], z[64:P, ZK:ZK + 2, :]).then_inc(kodd_ok, 1)
                    ve.tensor_copy(kns[:, :, :], z[:, ZK:ZK + 2, SEQ:T]).then_inc(qs_ok, 1)

            for r in range(9):
                rotated(r, ROT[r])
            ve.wait_ge(prep, 1)

            def scaled(g):
                kind, b, h = groups[g]
                s = g % 2
                src = ps[:, 0:2, :].rearrange("p a (j w) -> p (a j) w", j=2)
                ve.wait_ge(sc_ps, g + 1)
                if kind == "swa":
                    w = P if b == 0 else 2 * P
                    mask = con[:, C_MASK + 2 * P - w:C_MASK + 2 * P].rearrange("p (a w) -> p a w", a=1)
                    ve.scalar_tensor_tensor(probs[s][:, :, 0:w], src[:, :, 0:w], SCALE, mask.broadcast_to([P, GRP, w]),
                                            ALU.mult, ALU.add).then_inc(sc_row, 1)
                else:
                    ve.tensor_scalar(probs[s][:, :, :], src, SCALE, None, ALU.mult).then_inc(sc_row, 1)

            def row_max(g):
                kind, b, h = groups[g]
                s = g % 2
                st = stat[:, s]
                w = P if kind == "swa" and b == 0 else 2 * P
                ve.wait_ge(sc_row, g + 1)
                ve.tensor_reduce(st[:, 0, :], probs[s][:, :, 0:w], AX.X, ALU.max).then_inc(sc_max, 1)
                ve.wait_ge(sc_max, g + 1)
                if kind == "swa":
                    ve.scalar_tensor_tensor(st[:, 1, :], st[:, 0, :], -1.0, nsink[:, 4 * h:4 * h + 4], ALU.mult,
                                            ALU.min).then_inc(sc_neg, 1)
                    ve.wait_ge(sc_neg, g + 1)
                    ve.tensor_tensor(st[:, 2, :], st[:, 1, :], prm[:, 4 * h:4 * h + 4], ALU.add).then_inc(sc_snk, 1)
                else:
                    ve.tensor_scalar(st[:, 1, :], st[:, 0, :], -1.0, None, ALU.mult).then_inc(sc_neg, 1)

            def inverse(g):
                st = stat[:, g % 2]
                ve.wait_ge(sc_exp, g + 1)
                den = 3
                if groups[g][0] == "swa":
                    ve.tensor_tensor(st[:, 5, :], st[:, 3, :], st[:, 4, :], ALU.add).then_inc(sc_den, 1)
                    ve.wait_ge(sc_den, g + 1)
                    den = 5
                ve.reciprocal(st[:, 6, :], st[:, den, :]).then_inc(sc_rec, 1)

            def rest(g):
                kind, b, h = groups[g]
                ve.wait_ge(o_hi, g + 1)
                if kind == "swa":
                    r, p = 64 * (h % 2), h // 2
                    dst = (slice(r, r + 64), slice(4 * p, 4 * p + 4), slice(b * P, b * P + P))
                    ve.tensor_tensor(oalo[dst], ps[r:r + 64, 6, :].rearrange("p (j q) -> p j q", j=4),
                                     oahi[dst].bitcast(F32), ALU.subtract).then_inc(o_lo, 1)
                else:
                    dst = (slice(0, P), slice(0, 2), slice(b * P, b * P + P))
                    quadrants(oclo[dst], ps[:, 6, :].rearrange("p (a t q) -> p a t q", a=2, t=2), ochi[dst])\
                        .then_inc(o_lo, 1)

            def quadrants(dst, src, head):
                for r in range(2):
                    rows = slice(64 * r, 64 * r + 64)
                    last = ve.tensor_tensor(dst[rows], src[rows, r], head[rows].bitcast(F32), ALU.subtract)
                return last

            def sample(i):
                if i == 4:
                    ve.wait_ge(sw_act, 1)
                    ve.tensor_tensor(sstat[:, 8:16], scol[:, P:P + NS], con[:, C_BM:C_BM + NS], ALU.mult)\
                      .then_inc(sw_dve, 1)
                    ve.wait_ge(sw_dve, 1)
                    ve.tensor_reduce(sstat[:, 5:6], sstat[:, 8:16], AX.X, ALU.add).then_inc(sw_dve, 1)
                    ve.wait_ge(sw_dve, 2)
                    ve.tensor_scalar(srow[:, P:P + 1], sstat[:, 5:6], SCALE, None, ALU.mult).then_inc(sw_dve, 1)
                if i == S_T1:
                    ve.wait_ge(sw_ps, 2)
                    ve.tensor_scalar(srow[:, 0:P], ps[:, 7, 2 * P:3 * P], SCALE, None, ALU.mult).then_inc(sw_dve, 1)
                    ve.wait_ge(sw_dve, 4)
                    ve.tensor_reduce(sstat[:, 0:1], srow[:, 0:WIN + 1], AX.X, ALU.max).then_inc(sw_dve, 1)
                    ve.wait_ge(sw_dve, 5)
                    ve.scalar_tensor_tensor(sstat[:, 1:2], sstat[:, 0:1], -1.0, nsink[:, 16:17], ALU.mult, ALU.min)\
                      .then_inc(sw_dve, 1)
                    ve.wait_ge(sw_dve, 6)
                    ve.tensor_tensor(sstat[:, 2:3], sstat[:, 1:2], prm[:, Q_SINKR:Q_SINKR + 1], ALU.add)\
                      .then_inc(sw_dve, 1)

                if i == S_OUT:
                    ve.wait_ge(sw_act, 4)
                    quadrants(oalo[:, :, SEQ:T].rearrange("q (p j) b -> q p j b", p=2),
                              ps[:, 7, 3 * P:4 * P].rearrange("q (p a b j) -> q a p j b", p=2, a=2, b=NS),
                              oahi[:, :, SEQ:T].rearrange("q (p j) b -> q p j b", p=2)).then_inc(sw_dve, 1)
                if i == M_T1:
                    ve.wait_ge(sm_ps, 1)
                    ve.tensor_reduce(sstat[0:32, 0:1], ps[0:32, 3, P:P + NMEM], AX.X, ALU.max).then_inc(sm_dve, 1)
                    ve.wait_ge(sm_dve, 1)
                    ve.tensor_scalar(sstat[0:32, 1:2], sstat[0:32, 0:1], -SCALE, None, ALU.mult).then_inc(sm_dve, 1)
                if i == M_OUT:
                    ve.wait_ge(sm_act, 4)
                    quadrants(oclo[:, :, SEQ:T],
                              ps[:, 3, 3 * P + 64:3 * P + 96].rearrange("q (t a b) -> q a t b", t=2, a=2),
                              ochi[:, :, SEQ:T]).then_inc(sm_dve, 1)

            def sample_norm(i):
                if i == S_T2:
                    ve.wait_ge(sw_act, 2)
                    ve.tensor_tensor(sstat[:, 5:6], sstat[:, 3:4], sstat[:, 4:5], ALU.add).then_inc(sw_dve, 1)
                    ve.wait_ge(sw_dve, 8)
                    ve.reciprocal(sstat[:, 6:7], sstat[:, 5:6]).then_inc(sw_dve, 1)
                    ve.wait_ge(sw_dve, 9)
                    ve.tensor_scalar(srow[:, 0:WIN + 1], srow[:, 0:WIN + 1], sstat[:, 6:7], None, ALU.mult)\
                      .then_inc(sw_dve, 1)
                    ve.wait_ge(sw_dve, 10)
                    ve.tensor_scalar(sstat[:, 8:16], con[:, C_BM:C_BM + NS], srow[:, P:P + 1], None, ALU.mult)\
                      .then_inc(sw_dve, 1)
                if i == M_T2:
                    ve.wait_ge(sm_act, 2)
                    ve.reciprocal(sstat[0:32, 6:7], sstat[0:32, 3:4]).then_inc(sm_dve, 1)
                    ve.wait_ge(sm_dve, 3)
                    ve.tensor_scalar(srow[0:32, 0:NMEM], srow[0:32, 0:NMEM], sstat[0:32, 6:7], None, ALU.mult)\
                      .then_inc(sm_dve, 1)

            def half_split(j, half):
                n, c = N_G + j, slice(half * (MPW // 2), (half + 1) * (MPW // 2))
                if half == 0:
                    ve.wait_ge(hi_split, n + 1)
                last = ve.tensor_tensor(wlo[n % 2][:, c], raw[n % 2][:, c], whi[n % 2][:, c].bitcast(F32), ALU.subtract)
                if half:
                    last.then_inc(lo_split, 1)

            scaled(0)
            row_max(0)
            rotated(9, ROT[9])
            ve.wait_ge(roped, 10)
            for r in range(2):
                last = ve.tensor_copy(qsp[64 * r:64 * r + 64, :, r, :, :],
                                      z[64 * r:64 * r + 64, ZQ:ZQ + 8, SEQ:T].rearrange("q (p j) b -> q p b j", p=2))
            last.then_inc(qs_ok, 1)
            for r in range(2):
                last = ve.tensor_copy(cqp[64 * r:64 * r + 64, :, r, :], z[64 * r:64 * r + 64, ZC:ZC + 2, SEQ:T])
            last.then_inc(qs_ok, 1)
            inverse(0)
            scaled(1)
            row_max(1)
            for g, (kind, b, h) in enumerate(groups):
                ve.wait_ge(pt_ps, g + 1)
                if g:
                    ve.wait_ge(o_ps, g)
                if narrow(g):
                    ve.tensor_copy(pt[:, 0, :], ps[:, 4, :]).then_inc(pt_dve, 1)
                else:
                    ve.tensor_copy(pt[:, 1, :], ps[:, 5, :]).then_inc(pt_dve, 1)
                if g + 1 < NGR:
                    inverse(g + 1)
                if g:
                    sample(g - 1)
                    rest(g - 1)
                if g + 2 < NGR:
                    scaled(g + 2)
                sample_norm(g)
                if g + 2 < NGR:
                    row_max(g + 2)
                if g - 2 in HALF_A:
                    half_split(0, HALF_A.index(g - 2))
            rest(NGR - 1)
            half_split(1, 0)
            half_split(1, 1)

            def wo_split(j):
                n = N_O + j
                split(n, n % 2, PW, True, out=wolo[:, 2 * j:2 * j + 2, :].rearrange("p k n -> p (k n)"),
                      hi=wohi[:, 2 * j:2 * j + 2, :].rearrange("p k n -> p (k n)"))

            def merge(i, more, first=False):
                if more:
                    split(2 * i + N_G + 2, N_G % 2, MPW)
                if not first:
                    ve.wait_ge(m_lo, i)
                ve.wait_ge(prod_ps, 5 * i + 4)
                ve.tensor_tensor(halves(mval[:, :]), pair(0), halves(gate[0][:, :]), ALU.mult).then_inc(m_step, 1)
                if not more:
                    wo_split(0)
                ve.wait_ge(prod_ps, 5 * i + 5)
                ve.tensor_tensor(halves(gate[1][:, :]), pair(1), halves(gate[1][:, :]), ALU.mult).then_inc(m_step, 1)
                ve.wait_ge(m_step, 4 * i + 2)
                ve.tensor_tensor(mval[:, :], mval[:, :], gate[1][:, :], ALU.add).then_inc(m_step, 1)
                ve.wait_ge(piece_used, 2 * i + N_G + 2)
                ve.wait_ge(gate_out, 3 * i + 3)
                ve.tensor_tensor(halves(gate[2][:, :]), pair(2), halves(gate[2][:, :]), ALU.mult).then_inc(m_step, 1)
                ve.wait_ge(m_step, 4 * i + 4)
                ve.tensor_tensor(mval[:, :], mval[:, :], gate[2][:, :], ALU.add).then_inc(m_val, 1)
                if more:
                    split(2 * i + N_G + 3, (N_G + 1) % 2, MPW)
                ve.wait_ge(m_hi, i + 1)
                ve.tensor_tensor(mlo[:, bass.ds(i, 1), :].rearrange("p a c -> p (a c)"), mval[:, :],
                                 mhi[:, bass.ds(i, 1), :].rearrange("p a c -> p (a c)").bitcast(F32),
                                 ALU.subtract).then_inc(m_lo, 1)

            merge(0, True, True)
            with ve.Fori(1, KD - 1) as i:
                merge(i, True)
            merge(KD - 1, False)
            for j in range(1, 4):
                wo_split(j)

            def spread(x, ls, step, k):
                for h in range(2):
                    ve.bn_stats(ls[:, 6 * h:6 * h + 6], x[:, 512 * h:512 * h + 512]).then_inc(step, 1)
                ve.wait_ge(step, k + 2)
                ve.bn_aggr(ls[:, 12:14], ls[:, 0:12]).then_inc(step, 1)
                ve.wait_ge(step, k + 3)
                ve.tensor_scalar(ls[:, 14:15], ls[:, 13:14], EPS, None, ALU.add).then_inc(step, 1)

            def factor(n, ls, step, k):
                if n:
                    ve.wait_ge(step, k + n)
                if n == 0:
                    ve.reciprocal(ls[:, 16:17], ls[:, 15:16]).then_inc(step, 1)
                elif n == 1:
                    ve.tensor_scalar(ls[:, 17:18], ls[:, 16:17], ls[:, 16:17], ls[:, 14:15], ALU.mult, ALU.mult)\
                      .then_inc(step, 1)
                elif n == 2:
                    ve.tensor_scalar(ls[:, 19:20], ls[:, 17:18], -0.5, 1.5, ALU.mult, ALU.add).then_inc(step, 1)
                elif n == 3:
                    ve.tensor_tensor(ls[:, 18:19], ls[:, 19:20], ls[:, 16:17], ALU.mult).then_inc(step, 1)
                else:
                    ve.scalar_tensor_tensor(ls[:, 20:21], ls[:, 12:13], -1.0, ls[:, 18:19], ALU.mult, ALU.mult)\
                      .then_inc(step, 1)

            for t in range(TT):
                ve.wait_ge(xrow_in[t % 2], 16 * (t // 2 + 1) + 16 * (t == TT - 1))
                ve.wait_ge(h_ps, t + 1)
                ve.scalar_tensor_tensor(hall[:, t, :], xrow[t % 2][:, :], ALPHA,
                                        ps[0:TR, 2 * (t % 2):2 * (t % 2) + 2, :].rearrange("p a n -> p (a n)"),
                                        ALU.mult, ALU.add).then_inc(h_sum, 1)
                ve.wait_ge(h_sum, t + 1)
                if t >= 2:
                    ve.wait_ge(h_nrm, t - 1)
                spread(hall[:, t, :], lstat[t % 2][0:TR], h_stat, 4 * t)
                ve.wait_ge(h_root, t + 1)
                for n in range(5):
                    factor(n, lstat[t % 2][0:TR], h_fac, 5 * t)
            x = hall[:, TT - 1, :]
            ve.wait_ge(ln_in, 32)
            ve.wait_ge(h_nrm, TT)
            ve.tensor_tensor(x, x, lng[0:TR, :], ALU.mult).then_inc(h_last, 1)
            ve.wait_ge(h_last, 1)
            ve.tensor_tensor(x, x, lnb[0:TR, :], ALU.add).then_inc(h_last, 1)

            def esplit(n, s, first=False):
                ve.wait_ge(ehi_ok, n + 1)
                if not first:
                    ve.wait_ge(e_used, n - 2)
                ve.tensor_tensor(elo[s % 3][:, :], eraw[s][:, :], ehi[s % 3][:, :].bitcast(F32), ALU.subtract)\
                  .then_inc(elo_ok, 1)

            count = [0]

            def link(ins):
                count[0] += 1
                ins.then_inc(rd, 1)
                ve.wait_ge(rd, count[0])

            def over(x, n):
                return x[:, :].rearrange("p (t a) -> p t a", a=1).broadcast_to([TR, TT, n])

            i4, i16 = both_dims(con[0:TR, C_I4:C_I4 + 4], 4), both_dims(con[0:TR, C_I16:C_I16 + 16], 16)
            ve.wait_ge(lg_ps, TT)
            link(ve.tensor_tensor(lg[:, :, :], ps[0:TR, 6, 0:20 * TT].rearrange("p (t n) -> p t n", t=TT),
                                  both_dims(prm[0:TR, Q_BIAS:Q_BIAS + 20], 20), ALU.add))
            link(ve.tensor_reduce(gm[:, :], lg[:, :, 0:4], AX.X, ALU.max))
            ve.tensor_tensor(gd[:, :, :], lg[:, :, 0:4], over(gm, 4), ALU.subtract).then_inc(gd_ok, 1)
            link(ve.tensor_tensor(gk[:, :, :], lg[:, :, 0:4], over(gm, 4), ALU.is_lt))
            link(ve.scalar_tensor_tensor(gk[:, :, :], gk[:, :, :], 100.0, i4, ALU.mult, ALU.add))
            link(ve.tensor_reduce(gi[:, :], gk[:, :, :], AX.X, ALU.min))
            link(ve.tensor_tensor(gk[:, :, :], i4, over(gi, 4), ALU.not_equal))
            link(ve.scalar_tensor_tensor(em[:, :, :].rearrange("p t (g e) -> p t g e", g=4),
                                         gk[:, :, :].rearrange("p t (g a) -> p t g a", a=1).broadcast_to([TR, TT, 4, 4]),
                                         NEG, lg[:, :, 4:20].rearrange("p t (g e) -> p t g e", g=4), ALU.mult, ALU.add))

            def best(value, index, onehot):
                link(ve.tensor_reduce(value[:, :], em[:, :, :], AX.X, ALU.max))
                link(ve.tensor_tensor(cd[:, :, :], em[:, :, :], over(value, NE), ALU.is_lt))
                link(ve.scalar_tensor_tensor(cd[:, :, :], cd[:, :, :], 100.0, i16, ALU.mult, ALU.add))
                link(ve.tensor_reduce(index[:, :], cd[:, :, :], AX.X, ALU.min))
                link(ve.tensor_tensor(onehot, i16, over(index, NE), ALU.is_equal))

            best(m1, i1, picks[:, 0])
            link(ve.scalar_tensor_tensor(em[:, :, :], picks[:, 0], NEG, em[:, :, :], ALU.mult, ALU.add))
            best(m2, i2, picks[:, 1])
            ve.tensor_tensor(both[:, :, :], picks[:, 0], picks[:, 1], ALU.add).then_inc(both_ok, 1)
            ve.tensor_tensor(m2[:, :], m2[:, :], m1[:, :], ALU.subtract).then_inc(dist_ok, 1)
            esplit(0, 0, True)
            ve.wait_ge(r_exp, 2)
            link(ve.tensor_reduce(gs[:, :], gd[:, :, :], AX.X, ALU.add))
            link(ve.tensor_scalar(m1[:, :], m2[:, :], 1.0, None, ALU.add))
            link(ve.tensor_tensor(m1[:, :], m1[:, :], gs[:, :], ALU.mult))
            ve.wait_ge(rank_ps, 1)
            ve.wait_ge(rc_in, 16)
            rank = ps[0:TR, 7, 0:TT * NE].rearrange("p (t n) -> p t n", t=TT)
            total = ps[0:TR, 7, TT * NE:TT * NE + NE]
            ve.reciprocal(w1[:, :], m1[:, :])
            ve.tensor_tensor(rankb[:, :, :], rank, both_dims(con[0:TR, C_B1:C_B1 + NE], NE), ALU.add)
            link(ve.tensor_scalar(oc[:, :], total, float(CAP), None, ALU.is_gt))
            for m in range(2, TT):
                link(ve.scalar_tensor_tensor(oc[:, :], total, float(CAP * m), oc[:, :], ALU.is_gt, ALU.add))
            link(ve.tensor_tensor(ocl[:, :, :], oc[:, :].rearrange("p (a e) -> p a e", a=1).broadcast_to([TR, NE, NE]),
                                  rcon[0:TR, G_LT:G_LT + NE * NE].rearrange("p (a e) -> p a e", a=NE), ALU.mult))
            link(ve.tensor_reduce(excl[:, :], ocl[:, :, :], AX.X, ALU.add))
            link(ve.scalar_tensor_tensor(base2[:, :], excl[:, :], float(CAP), rcon[0:TR, G_BK:G_BK + NE],
                                         ALU.mult, ALU.add))
            link(ve.scalar_tensor_tensor(past[:, :, :], rank, float(CAP), both_dims(base2[0:TR, :], NE),
                                         ALU.is_ge, ALU.mult))
            link(ve.tensor_tensor(past[:, :, :], past[:, :, :], rankb[:, :, :], ALU.add))
            link(ve.tensor_tensor(picked[:, :, :, :], picks[:, :, :, :],
                                  past[:, :, :].rearrange("p (a t) n -> p a t n", a=1).broadcast_to([TR, 2, TT, NE]),
                                  ALU.mult))
            link(ve.tensor_reduce(slotf[:, :, :], picked[:, :, :, :], AX.X, ALU.add))

            def wider(x, n):
                return x[:, :, :].rearrange("p c (t a) -> p c t a", a=1).broadcast_to([TR, 2, TT, n])

            def along(x, n):
                return x.rearrange("p (c t n) -> p c t n", c=1, t=1).broadcast_to([TR, 2, TT, n])

            link(ve.tensor_tensor(atleast[:, :, :, :], wider(slotf, NCH + 1), along(rcon[0:TR, G_CH:G_CH + NCH + 1], NCH + 1),
                                  ALU.is_ge))
            link(ve.tensor_reduce(nfull[:, :, :], atleast[:, :, :, 1:NCH + 1], AX.X, ALU.add))
            link(ve.scalar_tensor_tensor(place[:, :, :], nfull[:, :, :], -float(CAP), slotf[:, :, :], ALU.mult, ALU.add))
            ve.tensor_tensor(rowhot[:, :, :, :], along(rcon[0:TR, G_ROW:G_ROW + CAP], CAP), wider(place, CAP),
                             ALU.is_equal).then_inc(list_ok, 1)
            link(ve.tensor_tensor(chunk[:, :, :, :], atleast[:, :, :, 0:NCH], atleast[:, :, :, 1:NCH + 1], ALU.subtract))
            ve.tensor_tensor(chunkr[:, :, :, :], chunk[:, :, :, :],
                             con[0:TR, C_TOK:C_TOK + TT].rearrange("p (c t n) -> p c t n", c=1, n=1)
                             .broadcast_to([TR, 2, TT, NCH]), ALU.mult).then_inc(list_ok, 1)
            ve.tensor_copy(s12[:, :, :], slotf[:, :, :]).then_inc(s12_ok, 1)
            ve.tensor_tensor(w2[:, :], m2[:, :], w1[:, :], ALU.mult)
            esplit(1, 1, True)
            ve.wait_ge(slot_ps, 1)
            ve.tensor_copy(slots[:, :], ps[:, 6, P:P + NCH]).then_inc(slot_ok, 1)
            esplit(2, 2, True)
            link(ve.tensor_tensor(incl[:, :], excl[:, :], oc[:, :], ALU.add))
            link(ve.tensor_tensor(ovf[:, :, :], con[0:TR, C_I8:C_I8 + 8].rearrange("p (j a) -> p j a", a=1).broadcast_to([TR, 8, NE]),
                                  incl[:, :].rearrange("p (a e) -> p a e", a=1).broadcast_to([TR, 8, NE]), ALU.is_ge))
            link(ve.tensor_reduce(ovi[:, :], ovf[:, :, :], AX.X, ALU.add))
            link(ve.tensor_scalar(ove[0:TR, 0:8], ovi[:, :], float(NE - 1), None, ALU.min))
            ve.tensor_copy(ove[0:TR, 8:9], incl[:, NE - 1:NE]).then_inc(over_ok, 1)

            def xet(c):
                ve.wait_ge(xet_hi, c + 1)
                ve.tensor_tensor(xetlo[:, :, :].rearrange("p (a k) c -> p a (k c)", a=2), ps[:, 4:6, :],
                                 xethi[:, :, :].rearrange("p (a k) c -> p a (k c)", a=2).bitcast(F32), ALU.subtract)\
                  .then_inc(xet_lo, 1)

            def silu(c):
                ve.wait_ge(sig_ok, c + 1)
                ve.wait_ge(hid_ok, c)
                ve.tensor_tensor(act[:, :], ps[:, 0, :], sig[:, :], ALU.mult).then_inc(act_ok, 1)

            def hidden(c, ready, first=False):
                ve.wait_ge(e_used, ready)
                ve.wait_ge(act_ok, c + 1)
                if not first:
                    ve.wait_ge(hidt_ps, c)
                ve.tensor_tensor(hid[:, :], ps[:, 1, :], act[:, :], ALU.mult).then_inc(hid_ok, 1)

            def hidt(c):
                ve.wait_ge(hidt_hi, c + 1)
                ve.tensor_tensor(htlo[:, :, :].rearrange("p j c -> p (j c)"), ps[:, 6, :],
                                 hthi[:, :, :].rearrange("p j c -> p (j c)").bitcast(F32), ALU.subtract)\
                  .then_inc(hidt_lo, 1)

            def expert(i, odd, more=True):
                e = 2 * i + odd

                def piece(e, k):
                    esplit(6 * e + k, 6 * odd + k)

                piece(e, 0)
                piece(e, 1)
                silu(e)
                hidt(e - 1)
                piece(e, 2)
                piece(e, 3)
                hidden(e, 6 * e + 2)
                if more:
                    xet(e + 1)
                piece(e, 4)
                piece(e, 5)

            xet(0)
            esplit(3, 3)
            silu(0)
            esplit(4, 4)
            esplit(5, 5)
            hidden(0, 4, True)
            xet(1)
            expert(0, 1)
            with ve.Fori(1, NE // 2 - 1) as i:
                expert(i, 0)
                expert(i, 1)
            expert(NE // 2 - 1, 0)
            expert(NE // 2 - 1, 1, False)
            hidt(NE - 1)
            ve.wait_ge(over_ok, 1)
            n_over = ve.value_load(ove[0:1, 8:9], min_val=0, max_val=NOVER)
            with ve.If(n_over > 0):
                with ve.Fori(0, NOVER) as j:
                    with ve.If(j < n_over):
                        n, c = 6 * j + 6 * NE, j + NE
                        xet(c)
                        for k in range(4):
                            esplit(n + k, 6 + k)
                        silu(c)
                        for k in range(4, 6):
                            esplit(n + k, 6 + k)
                        hidden(c, n + 4)
                        hidt(c)
            def root(t, n):
                if t >= 0:
                    if n == 0:
                        ve.wait_ge(f_root, t + 1)
                    factor(n, lstat[t % 2][0:TR], f_fac, 5 * t)

            ve.wait_ge(h_back, 16)
            for t in range(TT):
                ls = lstat[t % 2][0:TR]
                ve.wait_ge(ya_w, t + 1)
                ve.scalar_tensor_tensor(res[t][:, :], hall[:, t, :], ALPHA, ya[t][:, :], ALU.mult, ALU.add)\
                  .then_inc(f_part, 1)
                root(t - 1, 0)
                ve.wait_ge(f_part, t + 1)
                ve.wait_ge(ya_in[t], 32)
                ve.scalar_tensor_tensor(res[t][:, :], yb[t][:, :], w2[:, t:t + 1], res[t][:, :], ALU.mult, ALU.add)\
                  .then_inc(f_sum, 1)
                root(t - 1, 1)
                ve.wait_ge(f_sum, t + 1)
                if t >= 2:
                    ve.wait_ge(f_nrm, t - 1)
                ve.bn_stats(ls[:, 0:6], res[t][:, 0:512]).then_inc(f_stat, 1)
                root(t - 1, 2)
                ve.bn_stats(ls[:, 6:12], res[t][:, 512:D]).then_inc(f_stat, 1)
                root(t - 1, 3)
                ve.wait_ge(f_stat, 4 * t + 2)
                ve.bn_aggr(ls[:, 12:14], ls[:, 0:12]).then_inc(f_stat, 1)
                root(t - 1, 4)
                ve.wait_ge(f_stat, 4 * t + 3)
                ve.tensor_scalar(ls[:, 14:15], ls[:, 13:14], EPS, None, ALU.add).then_inc(f_stat, 1)
            for n in range(5):
                root(TT - 1, n)
            ve.wait_ge(ln2_in, 32)
            t = TT - 2
            ve.wait_ge(f_nrm, TT - 1)
            ve.tensor_tensor(res[t][:, :], res[t][:, :], lng[0:TR, :], ALU.mult).then_inc(f_last, 1)
            t = TT - 1
            ve.wait_ge(f_nrm, TT)
            ve.tensor_tensor(res[t][:, :], res[t][:, :], lng[0:TR, :], ALU.mult).then_inc(f_last, 1)
            ve.wait_ge(f_last, 2)
            ve.tensor_tensor(res[t][:, :], res[t][:, :], lnb[0:TR, :], ALU.add).then_inc(f_last, 1)

        @block.gpsimd
        def _(gp):
            gp.memset(xhi[:, KD * T:XPAD].bitcast(F32), 0.0).then_inc(pad_zero, 1)
            gp.memset(xlo[:, KD * T:XPAD].bitcast(F32), 0.0).then_inc(pad_zero, 1)
            gp.memset(kodd[:, :, :], 0.0).then_inc(pads, 1)
            gp.memset(qsp[:, :, :, :, :], 0.0)
            gp.memset(cqp[:, :, :, :], 0.0).then_inc(pads, 1)
            gp.memset(mkt[:, :, :], 0.0).then_inc(pads, 1)
            gp.memset(zrow[:, :], 0.0).then_inc(z_row, 1)
            gp.wait_ge(z_row, 1)
            for c in range(NE, NE + NOVER):
                gp.dma_start(y_dram[c * CAP:c * CAP + CAP, :], zrow[:, :]).then_inc(z_sent, 16)
            gp.wait_ge(con_in, 64)
            gp.wait_ge(xt_hi, KD + 1)
            gp.wait_ge(xt_lo, KD + 1)
            gp.wait_ge(z_out, ZU + 4)
            gp.wait_ge(st_out, 1)
            count = [0]

            def link(ins):
                count[0] += 1
                ins.then_inc(pool_step, 1)
                gp.wait_ge(pool_step, count[0])

            link(gp.tensor_copy(pext[:, :, :, PST], z[:, ZU:ZU + 4, SEQ:T]))
            for g, w in enumerate(POOL_W):
                src, d, k = z[:, ZU + g, :], 1, 0
                while d < w:
                    dst = pbuf[k % 2]
                    link(gp.tensor_copy(dst[:, 0:d], src[:, 0:d]))
                    link(gp.tensor_tensor(dst[:, d:SEQ], src[:, d:SEQ], src[:, 0:SEQ - d], ALU.add))
                    src, d, k = dst, 2 * d, k + 1
                cur, n = pext[:, g, :, PST + 1 - w:PST + 1], w
                while n > 1:
                    half = pext[:, g, :, PST + 1 - w:PST + 1 - w + n // 2]
                    link(gp.tensor_tensor(half, cur[:, :, 0:n // 2], cur[:, :, n // 2:n], ALU.add))
                    cur, n = half, n // 2
                link(gp.tensor_copy(src[:, SEQ:T], cur[:, :, 0]))
                link(gp.tensor_tensor(src[:, 0:16], src[:, 0:16], con[:, C_POOL + 16 * g:C_POOL + 16 * g + 16], ALU.mult))
                link(gp.tensor_scalar(src[:, 0:T], src[:, 0:T], 1.0 / w, None, ALU.mult))
                gp.tensor_tensor(pooled[:, g, :], src[:, 0:T], z[:, ZU + g, :], ALU.subtract).then_inc(pooled_in, 1)
                gp.wait_ge(pooled_in, g + 1)
            for r, t in enumerate(ROT):
                gp.wait_ge(z_out, ZT)
                gp.wait_ge(rot_ps, r + 1)
                gp.tensor_tensor(z[:, t, :], z[:, t, :], con[:, C_COS:C_COS + T], ALU.mult).then_inc(rot_cos, 1)
                if r == 7:
                    gp.wait_ge(row_ps, 2)
                    gp.wait_ge(kodd_ok, 1)
                    gp.wait_ge(qs_ok, 1)
                    gp.wait_ge(rot_cos, 8)
                    gp.memset(z[64:P, ZK:ZK + 2, :], 0.0).then_inc(pads, 1)
                    gp.wait_ge(pads, 4)
            for g, (kind, b, h) in enumerate(groups):
                s, w = g % 2, P if kind == "swa" and b == 0 else 2 * P
                gp.wait_ge(sc_rec, g + 1)
                gp.tensor_tensor(probs[s][:, :, 0:w], probs[s][:, :, 0:w],
                                 stat[:, s, 6, :].rearrange("p (j w) -> p j w", w=1).broadcast_to([P, GRP, w]), ALU.mult)\
                  .then_inc(sc_nrm, 1)
                if g == 0:
                    gp.wait_ge(piece_used, N_M + 2)
                    gp.memset(mkodd[:, :, :], 0.0).then_inc(pads, 1)
            gp.wait_ge(ln_in, 32)
            for t in range(TT):
                x = hall[:, t, :]
                if t < TT - 1:
                    gp.wait_ge(h_nrm, t + 1)
                    gp.tensor_tensor(x, x, lng[0:TR, :], ALU.mult).then_inc(h_gain, 1)
                    gp.wait_ge(h_gain, t + 1)
                    gp.tensor_tensor(x, x, lnb[0:TR, :], ALU.add).then_inc(h_done, 1)
                    gp.wait_ge(h_done, t + 1)
                else:
                    gp.wait_ge(h_last, 2)
                gp.dma_start(h_dram[t * TR:t * TR + TR, :], x).then_inc(h_sent, 16)
            gp.wait_ge(slot_ok, 1)
            gp.wait_ge(h_sent, 16 * TT)

            def gather(c, q, arrived=None, turned=None):
                if arrived is not None:
                    gp.wait_ge(xe_in[q], arrived)
                    gp.wait_ge(xet_ps, turned)
                gp.tensor_copy(slotc[q][:, :], slots[:, bass.ds(c, 1)]).then_inc(slc_ok, 1)
                gp.wait_ge(slc_ok, c + 1)
                gp.sem_inc(slc_seen, 1)
                gp.indirect_dma_start(out=xe[q][:, :], out_offset=None, in_=h_dram,
                                      in_offset=bass.IndirectOffsetOnAxis(ap=slotc[q][:, :], axis=0))\
                  .then_inc(xe_in[q], 16)

            for q in range(2):
                gather(q, q)
            with gp.Fori(1, NE // 2) as i:
                for q in range(2):
                    gather(2 * i + q, q, 16 * i, 2 * i + q - 1)
            gp.wait_ge(over_ok, 1)
            n_over = gp.value_load(ove[0:1, 8:9], min_val=0, max_val=NOVER)
            with gp.If(n_over > 0):
                with gp.Fori(0, NOVER) as j:
                    with gp.If(j < n_over):
                        gather(j + NE, 0, 16 * j + 16 * (NE // 2), j + NE)
            gp.wait_ge(moe_done, 1)
            gp.wait_ge(s12_ok, 1)
            for t in range(TT):
                for c, dst in enumerate((ya, yb)):
                    gp.indirect_dma_start(out=dst[t][:, :], out_offset=None, in_=y_dram,
                                          in_offset=bass.IndirectOffsetOnAxis(ap=s12[:, c, t:t + 1], axis=0))\
                      .then_inc(ya_in[t], 16)
            gp.wait_ge(ln2_in, 32)
            for t in range(TT - 1):
                gp.wait_ge(f_nrm, t + 1)
                if t < TT - 2:
                    gp.tensor_tensor(res[t][:, :], res[t][:, :], lng[0:TR, :], ALU.mult).then_inc(f_gain, 1)
                    gp.wait_ge(f_gain, t + 1)
                else:
                    gp.wait_ge(f_last, 1)
                gp.tensor_tensor(res[t][:, :], res[t][:, :], lnb[0:TR, :], ALU.add).then_inc(f_done, 1)


def constants():
    import numpy as np

    c = np.zeros((P, C_END), np.float32)
    c[:, C_ID:C_ID + P] = np.eye(P)
    half = HD // 8
    for head in range(2):
        for d in range(half):
            c[head * HD + d + half, C_ROT + head * HD + d] = -1.0
            c[head * HD + d, C_ROT + head * HD + d + half] = 1.0
    pos = np.concatenate([np.arange(SEQ), np.full(NS, 2048)]).astype(np.float32)
    inv = np.power(np.float32(500000.0), -np.arange(half, dtype=np.float32) * np.float32(2.0 / (2 * half)))
    ang = pos[None, :] * inv.astype(np.float32)[:, None]
    c[:, C_COS:C_COS + T] = 1.0
    for head in range(2):
        for rep in range(2):
            r = head * HD + rep * half
            c[r:r + half, C_COS:C_COS + T] = np.cos(ang)
            c[r:r + half, C_SIN:C_SIN + T] = np.sin(ang)
    i, k = np.arange(P)[:, None], np.arange(2 * P)[None, :]
    c[:, C_MASK:C_MASK + 2 * P] = np.where((k <= P + i) & (k >= i), 0.0, NEG)
    t = np.arange(16)
    for g, w in enumerate(POOL_W):
        c[:, C_POOL + 16 * g:C_POOL + 16 * g + 16] = w / np.minimum(t + 1, w)
    c[:TR, C_UP:C_UP + TR] = np.triu(np.ones((TR, TR)), 1)
    c[:, C_ONE:C_ONE + P] = 1.0
    c[:, C_I4:C_I4 + 4] = np.arange(4)
    c[:, C_I16:C_I16 + 16] = np.arange(16)
    c[:, C_B1:C_B1 + NE] = np.arange(NE) * CAP
    c[:TR, C_TOK:C_TOK + TT] = np.arange(TT)[None, :] * TR + np.arange(TR)[:, None]
    c[:, C_BM:C_BM + NS] = (np.arange(P)[:, None] % 32 // 4) == np.arange(NS)[None, :]
    c[:, C_I8:C_I8 + 8] = np.arange(8)
    g = np.zeros((P, G_END), np.float32)
    g[:, G_LT:G_LT + NE * NE] = np.tril(np.ones((NE, NE)), -1).reshape(-1)
    g[:, G_BK:G_BK + NE] = (NE - 1 - np.arange(NE)) * CAP
    g[:, G_CH:G_CH + NCH + 1] = np.arange(NCH + 1) * CAP
    g[:, G_ROW:G_ROW + CAP] = np.arange(CAP)
    return c, g


def kernel(**inputs):
    import numpy as np
    import concourse.bacc as bacc
    from concourse.bass_utils import run_bass_kernel_spmd

    x = {k: np.asarray(w) for k, w in inputs.items()}
    w_in = x["w_in"][0]
    heads = [8 * (t // 4) + t % 4 + 4 * s for t in range(8) for s in range(2)]
    q0, k0, v0, u0, c0, g0 = 0, 1024, 1280, 1536, 2048, 2304
    qcols = [q0 + h * HD + d for h in heads for d in range(HD)]
    zcols = list(range(u0, c0)) + list(range(k0, v0)) + list(range(c0, g0)) + qcols

    def blocks(w):
        return w.reshape(w.shape[0] // P, P, w.shape[1] // P, P).transpose(2, 1, 0, 3)

    wz = blocks(w_in[:, zcols]).reshape(ZP, 2, P, KD * P).transpose(0, 2, 1, 3).reshape(ZP, P, PW)
    wv = w_in[:, v0:u0].reshape(KD, P, 256).transpose(1, 0, 2).reshape(P, PW)
    wmem = np.concatenate([x["w_mem_k"][0], x["w_mem_v"][0]], 1).reshape(2, 4, P, 512).transpose(0, 2, 1, 3)
    wa = x["w_branch_a"][0][qcols]
    parts = [w_in[:, g0 + D * g:g0 + D * g + D] for g in range(3)] + [wa, x["w_branch_b"][0], x["w_branch_c"][0]]
    wm = np.concatenate([blocks(w) for w in parts], 2).reshape(KD, P, 2, MPW).transpose(0, 2, 1, 3)
    sinks = x["sinks"][0]
    params = np.concatenate([
        np.broadcast_to(sinks, (P, NH)),
        sinks.reshape(NKV, 1, GRP).repeat(NS, 1).reshape(P, 1),
        x["pool_scale"][0].reshape(4, P).T,
        np.broadcast_to(np.concatenate([x["b_group"][0], x["b_router"][0].reshape(-1)]), (P, 20)),
    ], 1)
    w_route = np.concatenate([x["w_group"][0], x["w_router"][0].reshape(D, NE)], 1)
    data = {
        "consts": constants()[0],
        "route_consts": constants()[1],
        "params": params,
        "x_prompt": x["x_prompt"].reshape(SEQ, D),
        "x_sample": x["x_sample"].reshape(NS, D),
        "cache_win_k": x["cache_win_k"].reshape(NS, WIN, 256),
        "cache_win_v": x["cache_win_v"].reshape(NS, WIN, 256),
        "state_pool": x["state_pool"].reshape(NS, PST, 512),
        "cache_mem_k": x["cache_mem_k"].reshape(NS, NMEM, 256),
        "cache_mem_v": x["cache_mem_v"].reshape(NS, NMEM, 256),
        "mem_prompt": x["mem_prompt"].reshape(NMEM, D),
        "wz": wz, "wv": wv, "wmem": wmem.reshape(2, P, PW), "wm": wm.reshape(2 * KD, P, MPW),
        "wo": x["w_out"][0].reshape(4, 2, P, D).transpose(0, 2, 1, 3).reshape(4, P, PW),
        "w_pool_mix": x["w_pool_mix"][0],
        "w_route": w_route.reshape(KD, P, 20).transpose(1, 0, 2),
        "ln1_g": x["ln1_g"], "ln1_b": x["ln1_b"], "ln2_g": x["ln2_g"], "ln2_b": x["ln2_b"],
        "w_gate": x["w_gate"][0], "w_up": x["w_up"][0], "w_down": x["w_down"][0],
    }
    outs = {
        "y_prompt": (SEQ, D), "y_sample": (NS, D),
        "new_k_prompt": (WIN, 256), "new_v_prompt": (WIN, 256), "new_pool_prompt": (PST, 512),
        "new_mem_k": (NMEM, 256), "new_mem_v": (NMEM, 256),
        "new_k_sample": (NS, WIN, 256), "new_v_sample": (NS, WIN, 256), "new_pool_sample": (NS, PST, 512),
    }
    shapes = [
        (1, SEQ, D), (NS, 1, D), (1, 1, WIN, NKV, HD), (1, 1, WIN, NKV, HD), (1, 1, PST, 512),
        (1, 1, NMEM, MH, HD), (1, 1, NMEM, MH, HD), (1, NS, WIN, NKV, HD), (1, NS, WIN, NKV, HD), (1, NS, PST, 512),
    ]
    nc = bacc.Bacc("TRN2", target_bir_lowering=False, num_devices=1)
    arrays, a, o = {}, {}, {}
    for name, w in data.items():
        arrays[name + "_in"] = np.ascontiguousarray(w)
        a[name] = nc.dram_tensor(name + "_in", w.shape, F32, kind="ExternalInput").ap()
    for name, shape in outs.items():
        o[name] = nc.dram_tensor(name, shape, F32, kind="ExternalOutput").ap()
    decoder_step(nc, a, o)
    r = run_bass_kernel_spmd(nc, [arrays], core_ids=[0]).results[0]
    return tuple(r[name].reshape(shape) for name, shape in zip(outs, shapes))
```
